# Optimizing a Trainium2 kernel written in Bass

```python
import jax
import jax.numpy as jnp
from jax import lax
import numpy as np

D_MODEL = 1024
BATCH = 1
SEQ = 256
DEPTH = 2
DEC_BATCH = 8
DEC_SEQ = 1
PAST_LEN = 2048
PAGE_SIZE = 128

RWKV_HEADS = 8
RWKV_HEAD_DIM = 64
RWKV_WIDTH = RWKV_HEADS * RWKV_HEAD_DIM
RWKV_DECAY_LORA = 64
RWKV_AAA_LORA = 64
RWKV_GATE_LORA = 128
RWKV_VRES_LORA = 32
RWKV_LNX_EPS = 64e-5
HGRN_HEADS = 4
HGRN_KEY_DIM = 128
HGRN_VAL_DIM = 128
HGRN_KEY_WIDTH = HGRN_HEADS * HGRN_KEY_DIM
HGRN_VAL_WIDTH = HGRN_HEADS * HGRN_VAL_DIM
HGRN_CHUNK = 64
SGU_GROUPS = 4
SGU_GROUP_DIM = 128
SGU_WIDTH = SGU_GROUPS * SGU_GROUP_DIM
SGU_CHUNK = 128
PEER_HEADS = 8
PEER_N_KEYS = 128
PEER_N_EXPERTS = PEER_N_KEYS * PEER_N_KEYS
PEER_HALF_DIM = 128
PEER_QUERY_DIM = 2 * PEER_HALF_DIM
PEER_TOPK = 16
PEER_TOKEN_BLOCK = 128
N_BRANCHES = 3
NORM_EPS = 1e-6
F_EPS = 1e-30
RWKV_COLS = 3 * RWKV_WIDTH + RWKV_DECAY_LORA + RWKV_AAA_LORA + RWKV_GATE_LORA
HGRN_COLS = 2 * HGRN_KEY_WIDTH + 2 * HGRN_VAL_WIDTH
SGU_COLS = 2 * SGU_WIDTH
GATE_COLS = N_BRANCHES * D_MODEL
IN_WIDTH = RWKV_COLS + HGRN_COLS + SGU_COLS + GATE_COLS
IN_SPLITS = (RWKV_COLS, RWKV_COLS + HGRN_COLS, RWKV_COLS + HGRN_COLS + SGU_COLS)
RWKV_SPLITS = (RWKV_WIDTH, 2 * RWKV_WIDTH, 3 * RWKV_WIDTH, 3 * RWKV_WIDTH + RWKV_DECAY_LORA, 3 * RWKV_WIDTH + RWKV_DECAY_LORA + RWKV_AAA_LORA)
HGRN_SPLITS = (HGRN_KEY_WIDTH, 2 * HGRN_KEY_WIDTH, 2 * HGRN_KEY_WIDTH + HGRN_VAL_WIDTH)

kernel_name = "hybrid_rwkv7_hgrn2_sgu_peer_step"

def rmsnorm(x, g, eps=NORM_EPS):
    xf = x.astype(jnp.float32)
    y = xf * lax.rsqrt(jnp.mean(xf * xf, axis=-1, keepdims=True) + eps)
    return (y * g.astype(jnp.float32)).astype(x.dtype)

def heads(t, n):
    return t.reshape(t.shape[0], t.shape[1], n, -1)

def token_shift(z, z_prev_row, mu):
    z_prev = jnp.concatenate([z_prev_row[:, None], z[:, :-1]], axis=1)
    return z + mu * (z_prev - z)

def rwkv7_recurrence(r, w, k, v, kk, a, s0):
    f32 = jnp.float32
    xs = tuple(jnp.moveaxis(t.astype(f32), 1, 0) for t in (r, w, k, v, kk, a))

    def step(s, inp):
        r_t, w_t, k_t, v_t, kk_t, a_t = inp
        sa = jnp.einsum("bhvk,bhk->bhv", s, -kk_t)
        s = (s * w_t[:, :, None, :] + sa[..., None] * (kk_t * a_t)[:, :, None, :]
             + v_t[..., None] * k_t[:, :, None, :])
        return s, jnp.einsum("bhvk,bhk->bhv", s, r_t)

    s, o = lax.scan(step, s0.astype(f32), xs)
    return jnp.moveaxis(o, 0, 1).astype(r.dtype), s.astype(s0.dtype)

def hgrn2_chunked(q, k, logf, v, s0):
    f32 = jnp.float32
    B, T, H, _ = q.shape
    DV = v.shape[-1]
    C = min(HGRN_CHUNK, T)
    n = -(-T // C)
    pad = n * C - T

    def prep(t):
        t = jnp.pad(t.astype(f32), ((0, 0), (0, pad), (0, 0), (0, 0)))
        return jnp.moveaxis(t.reshape(B, n, C, H, t.shape[-1]), 1, 0)

    causal = jnp.tril(jnp.ones((C, C), bool))[None, :, :, None, None]

    def step(s, inp):
        q_c, k_c, l_c, v_c = inp
        b = jnp.cumsum(l_c, axis=1)
        o_inter = jnp.einsum("bthk,bhkv->bthv", q_c * jnp.exp(b), s)
        diff = jnp.where(causal, b[:, :, None] - b[:, None, :], 0.0)
        decay = jnp.where(causal, jnp.exp(diff), 0.0)
        att = jnp.einsum("bthk,bshk,btshk->bths", q_c, k_c, decay)
        o = o_inter + jnp.einsum("bths,bshv->bthv", att, v_c)
        b_last = b[:, -1]
        s = (jnp.exp(b_last)[..., None] * s
             + jnp.einsum("bshk,bshv->bhkv", k_c * jnp.exp(b_last[:, None] - b), v_c))
        return s, o

    s, o = lax.scan(step, s0.astype(f32), (prep(q), prep(k), prep(logf), prep(v)))
    o = jnp.moveaxis(o, 0, 1).reshape(B, n * C, H, DV)[:, :T]
    return o.astype(v.dtype), s.astype(s0.dtype)

def spatial_gating(z, ln_g, ln_b, ws, bs):
    u, v = jnp.split(z, 2, axis=-1)
    vf = v.astype(jnp.float32)
    mean = jnp.mean(vf, axis=-1, keepdims=True)
    var = jnp.mean(jnp.square(vf - mean), axis=-1, keepdims=True)
    v = ((vf - mean) * lax.rsqrt(var + NORM_EPS) * ln_g + ln_b).astype(z.dtype)
    B, T, _ = v.shape
    n = -(-T // SGU_CHUNK)
    pad = n * SGU_CHUNK - T
    vc = jnp.pad(v, ((0, 0), (0, pad), (0, 0))).reshape(B, n, SGU_CHUNK, SGU_GROUPS, SGU_GROUP_DIM)
    wm = ws * jnp.tril(jnp.ones((SGU_CHUNK, SGU_CHUNK), ws.dtype))
    mixed = jnp.einsum("gts,bnsgc->bntgc", wm, vc) + bs.T[None, None, :, :, None]
    mixed = mixed.reshape(B, n * SGU_CHUNK, SGU_WIDTH)[:, :T]
    return u * mixed, v

def peer_ffn(h, wq, keys, down, up):
    shp = h.shape
    x = h.reshape(-1, D_MODEL)
    T = x.shape[0]
    tb = min(PEER_TOKEN_BLOCK, T)
    n = -(-T // tb)
    xb = jnp.pad(x, ((0, n * tb - T), (0, 0))).reshape(n, tb, D_MODEL)

    def block(xt):
        q = (xt @ wq).reshape(tb, PEER_HEADS, 2, PEER_HALF_DIM)
        s = jnp.einsum("thpd,hpnd->thpn", q, keys)
        s1, i1 = lax.top_k(s[:, :, 0], PEER_TOPK)
        s2, i2 = lax.top_k(s[:, :, 1], PEER_TOPK)
        comb = (s1[..., :, None] + s2[..., None, :]).reshape(tb, PEER_HEADS, PEER_TOPK * PEER_TOPK)
        sc, ci = lax.top_k(comb, PEER_TOPK)
        e1 = jnp.take_along_axis(i1, ci // PEER_TOPK, axis=-1)
        e2 = jnp.take_along_axis(i2, ci % PEER_TOPK, axis=-1)
        idx = e1 * PEER_N_KEYS + e2
        gate = jax.nn.softmax(sc.astype(jnp.float32), axis=-1)
        pre = jnp.einsum("td,thkd->thk", xt, down[idx])
        act = (jax.nn.gelu(pre.astype(jnp.float32), approximate=False) * gate).astype(xt.dtype)
        return jnp.einsum("thk,thkd->td", act, up[idx])

    out = lax.map(block, xb)
    return out.reshape(n * tb, D_MODEL)[:T].reshape(shp)

def hybrid_mixer(h, h_prev, s_rwkv, s_hgrn, v_first, p, lb, vres):
    f32 = jnp.float32
    B, T, _ = h.shape
    z_r, z_h, z_s, z_g = jnp.split(h @ p["w_in"], IN_SPLITS, axis=-1)

    z_r = token_shift(z_r, h_prev @ p["w_in"][:, :RWKV_COLS], p["shift_mu"])
    r, k, v, xw, xa, xg = jnp.split(z_r, RWKV_SPLITS, axis=-1)
    if vres is None:
        v_first = v
    else:
        w1, mu, w2, v0 = vres
        xv = token_shift(h @ w1, h_prev @ w1, mu)
        v = v + (v_first - v) * jax.nn.sigmoid(v0 + xv @ w2)
    wlog = -jax.nn.softplus(-(p["rwkv_w0"] + jnp.tanh(xw) @ p["rwkv_w2"])) - 0.5
    decay = jnp.exp(-jnp.exp(wlog.astype(f32)))
    a = jax.nn.sigmoid(p["rwkv_a0"] + xa @ p["rwkv_a2"])
    g = jax.nn.sigmoid(xg) @ p["rwkv_g2"]
    kk = heads(k * p["rwkv_kk"], RWKV_HEADS).astype(f32)
    kk = kk / jnp.maximum(jnp.sqrt(jnp.sum(kk * kk, axis=-1, keepdims=True)), 1e-12)
    k = k * (1.0 + (a - 1.0) * p["rwkv_ka"])
    rh, kh, vh, ah = (heads(t, RWKV_HEADS) for t in (r, k, v, a))
    o, s_rwkv = rwkv7_recurrence(rh, heads(decay, RWKV_HEADS), kh, vh, kk, ah, s_rwkv)
    of = o.astype(f32)
    mean = jnp.mean(of, axis=-1, keepdims=True)
    var = jnp.mean(jnp.square(of - mean), axis=-1, keepdims=True)
    o = ((of - mean) * lax.rsqrt(var + RWKV_LNX_EPS)).reshape(B, T, RWKV_WIDTH) * p["rwkv_lnx_g"] + p["rwkv_lnx_b"]
    bonus = jnp.sum(rh * kh * p["rwkv_rk"], axis=-1, keepdims=True) * vh
    o = (o + bonus.reshape(B, T, RWKV_WIDTH)) * g
    y_rwkv = o.astype(h.dtype) @ p["w_branch_rwkv"]

    q_raw, f_raw, i_raw, og = jnp.split(z_h, HGRN_SPLITS, axis=-1)
    ff = f_raw.astype(f32)
    sig = jax.nn.sigmoid(ff)
    f_gate = lb + (1.0 - lb) * sig
    logf = jnp.log(jnp.maximum(f_gate, F_EPS))
    kin = 1.0 - f_gate
    oh, s_hgrn = hgrn2_chunked(heads(jax.nn.silu(q_raw), HGRN_HEADS), heads(kin, HGRN_HEADS),
                               heads(logf, HGRN_HEADS), heads(i_raw, HGRN_HEADS), s_hgrn)
    oh = rmsnorm(oh, p["hgrn_norm_g"].reshape(HGRN_HEADS, HGRN_VAL_DIM))
    y_hgrn = (oh.reshape(B, T, HGRN_VAL_WIDTH) * jax.nn.silu(og)) @ p["w_branch_hgrn"]

    y_sgu, v_rows = spatial_gating(jax.nn.gelu(z_s, approximate=False), p["sgu_ln_g"], p["sgu_ln_b"],
                                   p["sgu_ws"], p["sgu_b"])
    y_sgu = y_sgu @ p["w_branch_sgu"]

    gates = jax.nn.sigmoid(z_g).reshape(B, T, N_BRANCHES, D_MODEL)
    merged = gates[:, :, 0] * y_rwkv + gates[:, :, 1] * y_hgrn + gates[:, :, 2] * y_sgu
    return merged @ p["w_out"], s_rwkv, s_hgrn, v_first, v_rows

def run_trunk(x, shift0, rwkv0, hgrn0, layers, vres_layers, lb_all, norm_final_g):
    shifts, rwkvs, hgrns, vrows = [], [], [], []
    v_first = None
    for l in range(DEPTH):
        p = {name: arr[l] for name, arr in layers.items()}
        vres = None if l == 0 else tuple(arr[l - 1] for arr in vres_layers)
        h = rmsnorm(x, p["norm_mix_g"])
        y, s_r, s_h, v_first, v_rows = hybrid_mixer(h, shift0[l], rwkv0[l], hgrn0[l], v_first, p, lb_all[l], vres)
        x = x + y
        x = x + peer_ffn(rmsnorm(x, p["norm_ffn_g"]), p["peer_wq"], p["peer_keys"], p["peer_down"], p["peer_up"])
        shifts.append(h[:, -1])
        rwkvs.append(s_r)
        hgrns.append(s_h)
        vrows.append(v_rows)
    return rmsnorm(x, norm_final_g), jnp.stack(shifts), jnp.stack(rwkvs), jnp.stack(hgrns), jnp.stack(vrows)

def setup_inputs(seed: int = 0) -> dict:
    key = jax.random.key(seed)
    ks = iter(jax.random.split(key, 64))
    f32 = jnp.float32

    def nrm(shape, scale):
        return jax.random.normal(next(ks), shape, f32) * scale

    def unif(shape, lo, hi):
        return jax.random.uniform(next(ks), shape, f32, lo, hi)

    L, D = DEPTH, D_MODEL
    return {
        "x_prompt": nrm((BATCH, SEQ, D), 1.0),
        "x_sample": nrm((DEC_BATCH, DEC_SEQ, D), 1.0),
        "state_shift": nrm((L, DEC_BATCH, D), 1.0),
        "state_rwkv": nrm((L, DEC_BATCH, RWKV_HEADS, RWKV_HEAD_DIM, RWKV_HEAD_DIM), 0.1),
        "state_hgrn": nrm((L, DEC_BATCH, HGRN_HEADS, HGRN_KEY_DIM, HGRN_VAL_DIM), 0.1),
        "norm_mix_g": 1.0 + nrm((L, D), 0.02),
        "w_in": nrm((L, D, IN_WIDTH), D ** -0.5),
        "shift_mu": unif((L, RWKV_COLS), 0.0, 1.0),
        "rwkv_w0": unif((L, RWKV_WIDTH), -4.0, 1.0),
        "rwkv_w2": nrm((L, RWKV_DECAY_LORA, RWKV_WIDTH), 0.5 * RWKV_DECAY_LORA ** -0.5),
        "rwkv_a0": nrm((L, RWKV_WIDTH), 0.1),
        "rwkv_a2": nrm((L, RWKV_AAA_LORA, RWKV_WIDTH), 0.5 * RWKV_AAA_LORA ** -0.5),
        "rwkv_g2": nrm((L, RWKV_GATE_LORA, RWKV_WIDTH), RWKV_GATE_LORA ** -0.5),
        "rwkv_kk": 0.85 + nrm((L, RWKV_WIDTH), 0.05),
        "rwkv_ka": 1.0 + nrm((L, RWKV_WIDTH), 0.05),
        "rwkv_rk": nrm((L, RWKV_HEADS, RWKV_HEAD_DIM), 0.1),
        "rwkv_lnx_g": 1.0 + nrm((L, RWKV_WIDTH), 0.02),
        "rwkv_lnx_b": nrm((L, RWKV_WIDTH), 0.02),
        "vres_w1": nrm((L - 1, D, RWKV_VRES_LORA), D ** -0.5),
        "vres_mu": unif((L - 1, RWKV_VRES_LORA), 0.0, 1.0),
        "vres_w2": nrm((L - 1, RWKV_VRES_LORA, RWKV_WIDTH), 0.5 * RWKV_VRES_LORA ** -0.5),
        "vres_v0": 1.0 + nrm((L - 1, RWKV_WIDTH), 0.1),
        "hgrn_lb": nrm((L, HGRN_KEY_WIDTH), 0.5),
        "hgrn_norm_g": 1.0 + nrm((L, HGRN_VAL_WIDTH), 0.02),
        "sgu_ln_g": 1.0 + nrm((L, SGU_WIDTH), 0.02),
        "sgu_ln_b": nrm((L, SGU_WIDTH), 0.02),
        "sgu_ws": nrm((L, SGU_GROUPS, SGU_CHUNK, SGU_CHUNK), 0.5 * SGU_CHUNK ** -0.5),
        "sgu_b": 1.0 + nrm((L, SGU_GROUPS, SGU_CHUNK), 0.02),
        "w_branch_rwkv": nrm((L, RWKV_WIDTH, D), RWKV_WIDTH ** -0.5),
        "w_branch_hgrn": nrm((L, HGRN_VAL_WIDTH, D), HGRN_VAL_WIDTH ** -0.5),
        "w_branch_sgu": nrm((L, SGU_WIDTH, D), SGU_WIDTH ** -0.5),
        "w_out": nrm((L, D, D), D ** -0.5),
        "norm_ffn_g": 1.0 + nrm((L, D), 0.02),
        "peer_wq": nrm((L, D, PEER_HEADS * PEER_QUERY_DIM), D ** -0.5),
        "peer_keys": nrm((L, PEER_HEADS, 2, PEER_N_KEYS, PEER_HALF_DIM), PEER_HALF_DIM ** -0.5),
        "peer_down": nrm((L, PEER_N_EXPERTS, D), D ** -0.5),
        "peer_up": nrm((L, PEER_N_EXPERTS, D), (PEER_HEADS * PEER_TOPK) ** -0.5),
        "norm_final_g": 1.0 + nrm((D,), 0.02),
    }

def reference(x_prompt, x_sample, state_shift, state_rwkv, state_hgrn,
              norm_mix_g, w_in, shift_mu, rwkv_w0, rwkv_w2, rwkv_a0, rwkv_a2, rwkv_g2,
              rwkv_kk, rwkv_ka, rwkv_rk, rwkv_lnx_g, rwkv_lnx_b,
              vres_w1, vres_mu, vres_w2, vres_v0,
              hgrn_lb, hgrn_norm_g, sgu_ln_g, sgu_ln_b, sgu_ws, sgu_b,
              w_branch_rwkv, w_branch_hgrn, w_branch_sgu, w_out, norm_ffn_g,
              peer_wq, peer_keys, peer_down, peer_up, norm_final_g):
    layers = {
        "norm_mix_g": norm_mix_g, "w_in": w_in, "shift_mu": shift_mu,
        "rwkv_w0": rwkv_w0, "rwkv_w2": rwkv_w2, "rwkv_a0": rwkv_a0, "rwkv_a2": rwkv_a2,
        "rwkv_g2": rwkv_g2, "rwkv_kk": rwkv_kk, "rwkv_ka": rwkv_ka, "rwkv_rk": rwkv_rk,
        "rwkv_lnx_g": rwkv_lnx_g, "rwkv_lnx_b": rwkv_lnx_b,
        "hgrn_norm_g": hgrn_norm_g, "sgu_ln_g": sgu_ln_g, "sgu_ln_b": sgu_ln_b,
        "sgu_ws": sgu_ws, "sgu_b": sgu_b,
        "w_branch_rwkv": w_branch_rwkv, "w_branch_hgrn": w_branch_hgrn, "w_branch_sgu": w_branch_sgu,
        "w_out": w_out, "norm_ffn_g": norm_ffn_g,
        "peer_wq": peer_wq, "peer_keys": peer_keys, "peer_down": peer_down, "peer_up": peer_up,
    }
    vres_layers = (vres_w1, vres_mu, vres_w2, vres_v0)
    sm = jax.nn.softmax(hgrn_lb.astype(jnp.float32), axis=0)
    lb_all = jnp.clip(jnp.cumsum(sm, axis=0) - sm[0], 0.0, 1.0)

    shift0_p = jnp.zeros((DEPTH, BATCH, D_MODEL), x_prompt.dtype)
    rwkv0_p = jnp.zeros((DEPTH, BATCH) + state_rwkv.shape[2:], state_rwkv.dtype)
    hgrn0_p = jnp.zeros((DEPTH, BATCH) + state_hgrn.shape[2:], state_hgrn.dtype)
    y_prompt, shift_prompt, rwkv_prompt, hgrn_prompt, _ = run_trunk(
        x_prompt, shift0_p, rwkv0_p, hgrn0_p, layers, vres_layers, lb_all, norm_final_g)
    y_sample, shift_sample, rwkv_sample, hgrn_sample, sgu_v_sample = run_trunk(
        x_sample, state_shift, state_rwkv, state_hgrn, layers, vres_layers, lb_all, norm_final_g)
    return (y_prompt, y_sample, shift_prompt, shift_sample, rwkv_prompt, rwkv_sample,
            hgrn_prompt, hgrn_sample, sgu_v_sample)


_drawn_inputs = setup_inputs


def setup_inputs(seed=0):
    import zlib

    import numpy as np

    out = dict(_drawn_inputs(seed))
    spreads = {}
    factors = {'rwkv_lnx_g': 62.555,
     'rwkv_lnx_b': 59.053,
     'hgrn_norm_g': 59.543,
     'sgu_ln_g': 21.887,
     'sgu_ln_b': 21.833,
     'sgu_b': 62.044,
     'norm_ffn_g': 41.178,
     'norm_final_g': 19.439,
     'rwkv_rk': 5.109}
    for name, (base, spread) in spreads.items():
        noise = np.random.default_rng([zlib.crc32(name.encode()), seed]).standard_normal(out[name].shape)
        drawn = base * np.exp(spread * noise) if base else spread * noise
        out[name] = jnp.asarray(drawn.astype(out[name].dtype))
    for name, factor in factors.items():
        out[name] = (out[name] * factor).astype(out[name].dtype)
    return out
```

```python
from contextlib import ExitStack

import numpy as np

import concourse.bass as bass
from concourse import mybir

F32 = mybir.dt.float32
U32 = mybir.dt.uint32
ALU = mybir.AluOpType
ACT = mybir.ActivationFunctionType
AX = mybir.AxisListType

P = 128
D_MODEL = 1024
KD = D_MODEL // P
SEQ, DEC, DEPTH = 256, 8, 2
T = SEQ + DEC
TS = T + DEC
W = 512
NW = W // P
RH, RN = 8, 64
RC = 64
NRC = SEQ // RC
HC = 128
NHC = SEQ // HC
LEV_R, LEV_H = 6, 7
PH, TOPK, NK = 8, 16, 128
ZR_W = TS + 1
RT, HT_, ST = 14, 16, 8
EPS, LNX_EPS = 1e-6, 64e-5
RINGP = 5
HALF = NK // 2
GRP = 4
NGRP = HALF // GRP
TB = 4

PARS = [("mix_g", 8), ("ffn_g", 8), ("mu", RT), ("w0", 4), ("a0", 4), ("kk", 4), ("ka", 4), ("rk", 4),
        ("lg", 4), ("lb", 4), ("vmu", 1), ("v0", 4), ("hg", 4), ("sg", 4), ("sb", 4), ("on", 1), ("off", 1)]
PAR_AT, PAR_N = {}, 0
for _n, _c in PARS:
    PAR_AT[_n] = (PAR_N, _c)
    PAR_N += _c
COM_AT = {"lb0": (0, 4), "lb1": (4, 4), "fin_g": (8, 8), "eps": (16, 1), "leps": (17, 1)}
COM_N = 18

CP_AT = {"ident": (0, 128), "ones": (128, 128), "bones": (256, 128), "iota": (384, 128), "iota16": (512, 16)}
CP_N = 528
CM_AT = {"rw": (0, 128), "n0": (128, 64), "lev": (192, 64 * LEV_R), "low": (576, 64), "hg": (640, 128 * 8),
         "triu": (1664, 128), "rscan": (1792, T), "hscan": (1792 + T, T)}
CM_N = 1792 + 2 * T


def masks():
    i = np.arange(P)
    cp = np.zeros((P, CP_N), np.float32)
    cp[:, 0:128] = np.eye(P)
    cp[:, 128:256] = 1
    cp[:, 256:384] = (i[:, None] // RN == i[None] // RN)
    cp[:, 384:512] = i[None]
    cp[:, 512:528] = i[None, :16]
    cm = np.zeros((P, CM_N), np.float32)
    s, t = i[:, None] % RC, i[None, :RC]
    cm[:, 0:64], cm[:, 64:128] = s < t, s <= t
    r, c = i[:RC, None], i[None, :RC]
    for lev in range(LEV_R):
        b = 2 << lev
        m = (r // b == c // b) & (r % b >= b // 2) & (c % b < b // 2)
        cm[:RC, 192 + 64 * lev:256 + 64 * lev] = m
        if lev == 0:
            cm[:RC, 128:192] = m.T
    cm[:RC, 576:640] = c < r
    s, t = i[:, None], i[None]
    for lev in range(LEV_H):
        b = 2 << lev
        cm[:, 640 + 128 * lev:768 + 128 * lev] = (s // b == t // b) & (s % b < b // 2) & (t % b >= b // 2)
    cm[:, 640 + 128 * LEV_H:768 + 128 * LEV_H] = s == t
    cm[:, 1664:1792] = s <= t
    t = np.arange(T)
    cm[:, 1792:1792 + T] = ((t % RC != 0) & (t < SEQ))[None]
    cm[:, 1792 + T:] = ((t % HC != 0) & (t < SEQ))[None]
    return cp, cm


def build(nc, d):
    ctx = ExitStack()
    with ctx:
        def sb(name, *shape):
            return ctx.enter_context(nc.sbuf_tensor(name, list(shape), F32))

        xT = sb("xT", P, KD, T)
        hT = sb("hT", P, KD, TS)
        ring = sb("ring", P, 2 * RINGP, KD, P)
        CP = sb("CP", P, CP_N)
        PAR = sb("PAR", P, DEPTH, PAR_N)
        COM = sb("COM", P, COM_N)
        LBS = sb("LBS", P, 6, NW)
        V1 = sb("V1", P, NW, T)
        NRM = sb("NRM", P, T)
        ARENA = 35800
        arena = sb("arena", P, ARENA)
        bank = [ctx.enter_context(nc.psum_tensor(f"bank{i}", [P, 512], F32)) for i in range(8)]

        def at(off, *dims):
            n = 1
            for x in dims:
                n *= x
            assert off + n <= ARENA, (off, n)
            v = arena[:, off:off + n]
            if len(dims) == 2:
                v = v.rearrange("p (a b) -> p a b", a=dims[0])
            if len(dims) == 3:
                v = v.rearrange("p (a b c) -> p a b c", a=dims[0], b=dims[1])
            return v

        CM = at(0, CM_N)
        o = CM_N
        W2A2 = at(o, W)
        G2 = at(o + 512, W)
        VW1 = at(o + 1024, KD, 32)
        VW2 = at(o + 1280, W)
        WST = at(o + 1792, NW, P)
        SBR = at(o + 2304, NW, P)
        o += 2816
        ZR = at(o, RT, ZR_W)
        XV = at(o + RT * ZR_W, ZR_W)
        RZ = o
        o += 4096
        HG = at(o, HT_, T)
        o += HT_ * T
        SG = at(o, ST, T)
        o += ST * T
        YR, YH, YS = (at(o + n * NW * T, NW, T) for n in range(3))
        o += 3 * NW * T
        WORK = o
        AR = at(o, NW, 2, T)
        BKV = at(o + 2112, NW * NRC, 3, RC)
        EC = at(o + 5280, NW, T)
        GG = at(o + 6336, NW, T)
        BO = at(o + 7392, NW, T)
        M = at(o + 8448, 4 * RH, P)
        LEFT = o + 12544
        D = at(LEFT, RT, T)
        XVS, LW, SGX = (at(LEFT + RT * T + n * T, T) for n in range(3))
        SW, AA, VG = (at(o + 8448 + n * NW * T, NW, T) for n in range(3))
        CU, T1, T2 = (at(RZ + n * NW * T, NW, T) for n in range(3))
        KK, T3 = YH, YS
        XT_ = at(RZ, 4 * RH, RC)
        YSC = at(RZ + 2048, W)
        BD = at(RZ + 2560, NW, P)
        TT_ = at(RZ + 3072, W)
        SQ = at(RZ + 3584, 6, NW, DEC)
        X_, P1, ML, L_ = (at(LEFT + n * 1024, 2 * RH, RC) for n in range(4))
        BKT = at(LEFT, NRC, W)
        UV = at(LEFT + 2048, NRC, W)
        SR = at(o + 8448, RN, RN)
        TR = at(LEFT, RN, RN)
        RQ = at(o, 6, RN)
        SA = at(o + 384, RN)
        OS = at(o + 448, RN)
        OT = at(o + 512, W)
        TQ = at(o + 2112, 6, W)
        names = ["EB", "QH", "KH", "BC", "FF", "U1", "U2", "HX0", "HX1"]
        HV = {n: at(o + i * NW * T, NW, T) for i, n in enumerate(names)}
        q = o + len(names) * NW * T
        AT_, VT, KT = (at(q + n * 1024, NHC, NW, P) for n in range(3))
        q += 3072
        SH, T5, VS = (at(q + n * 512, NW, P) for n in range(3))
        SHS = at(RZ, DEC, NW, P)
        VC, VQ = at(o, NW, T), at(o + 1056, NW, T)
        VT2 = at(o + 2112, NHC, NW, P)
        SC8 = at(o + 3136, 8)
        MG = at(o + 4096, KD, T)
        GS = at(o + 4096 + KD * T, 2, T)
        PR = at(o + 4096 + KD * T + 2 * T, T)
        NSQ = at(WORK, KD, T)

        UPR = at(0, 2 * GRP, D_MODEL)
        DNR = at(8192, GRP, KD, P)
        GM = at(12288, T, HALF)
        ACC = at(29184, KD, T)
        ACTB = at(31296, 2 * GRP, T)
        GB = at(33408, 2, T)
        E1T, E2T, GTT = (at(33936 + n * T, T) for n in range(3))
        OH1 = at(34728, 2, TB, P)
        QT = at(12288, 2 * PH, T)
        SC = at(12288 + 4224, 3, 2 * PH, P)
        q = 12288 + 4224 + 6144
        SV = at(q, PH, 2, TOPK)
        SI = at(q + 256, PH, 2, TOPK)
        SIF = at(q + 512, PH, 2, TOPK)
        COMB = at(q + 768, PH, TOPK, TOPK)
        q += 768 + 2048
        CV, CI, CA, CB, E1, E2, GA = (at(q + n * 128, PH, TOPK) for n in range(7))
        SM = at(q + 896, 2, PH)
        OHB = at(q + 912, P, TOPK)
        OH2 = sb("OH2", P, 2, TB, HALF)
        KEYS = at(0, 2 * PH, P)
        FSQ = at(12288, KD, T)

        names = """x_in par_in smalls_in lb_in lb_exp mix_sq mix_ss mix_std h_ready shift_out z_mm z_evac xv_mm
            xv_evac zs_ready lora_in lora_mm lora_evac decay_in decay_out kk_sq kk_ss kk_std prep_done bon_done
            bon_mm mat_mm mat_evac l_mm l_evac p_mm p_evac x_in2 x_mm x_done tok_mm tok_evac y_mm y_evac u_mm
            u_evac o_evac s_mm s_evac sq_mm sq_evac rq_in sr_in sr_done sr_out so_out so_in ot_mm gn_m gn_sq gn_v
            gn_std yr_done hg_in hg_sig f_ready f_ln b_ready eb_done lev_in lev_exp lev_x att_mm att_evac kh_in
            kh_exp kh_done ht_mm ht_evac ho_evac hs_mm hs_evac shs_in vs_mm vs_evac vb_mm vb_evac hso_mm hso_evac
            hn_sq hn_mm hn_std h_out sg_mm sg_mu sg_vm sg_std sg_vn sgt_mm sgt_evac mx_mm mx_evac sgo_out
            gate_mm gate_evac br_mm br_evac wo_mm wo_evac ffn_sq ffn_ss ffn_std h2_ready keys_moved q_mm q_evac
            sc_mm sc_evac sm_in sm_exp e_ready et_mm et_evac oh_ready g_mm g_evac pre_mm gelu_done act_ready
            out_mm out_evac y_out bd_out hp_out arena_free dve_step mg_add mg_done""".split()
        S = {n: ctx.enter_context(nc.semaphore(n)) for n in dict.fromkeys(names)}
        ring_in = [ctx.enter_context(nc.semaphore(f"ring_in{i}")) for i in range(RINGP)]
        ring_free = [ctx.enter_context(nc.semaphore(f"ring_free{i}")) for i in range(RINGP)]
        dn_in = [ctx.enter_context(nc.semaphore(f"dn_in{i}")) for i in range(GRP)]
        up_in = [ctx.enter_context(nc.semaphore(f"up_in{i}")) for i in range(2)]
        NSMALL = 8
        USES = [11, 11, 11, 10, 9]

        def par(l, n, a=0, b=None):
            c, k = PAR_AT[n]
            return PAR[:, l, c + a:c + (k if b is None else b)]

        def com(n, a=0, b=None):
            c, k = COM_AT[n]
            return COM[:, c + a:c + (k if b is None else b)]

        def cp(n):
            c, k = CP_AT[n]
            return CP[:, c:c + k]

        def cm(n, a=0, k=None):
            c, w = CM_AT[n]
            return CM[:, c + a:c + a + (w if k is None else k)]

        ident, ones, bones = cp("ident"), cp("ones"), cp("bones")

        def over(ap, n):
            return ap.rearrange("p (a b) -> p a b", b=1).broadcast_to([ap.shape[0], ap.shape[1], n])

        def rows(ap, n):
            return ap.rearrange("p (a b) -> p a b", a=1).broadcast_to([ap.shape[0], n, ap.shape[1]])

        block = ctx.enter_context(nc.Block())

        @block.sync
        def _(sp):
            sp.dma_start(xT[:], d["x"]).then_inc(S["x_in"], 16)
            for dst, src in ((CP[:], d["cp"]), (PAR[:], d["par"]), (COM[:], d["com"])):
                sp.dma_start(dst, src).then_inc(S["par_in"], 16)
            use = [0] * RINGP

            def pair(slot, src, l, n=2, i=0):
                sp.wait_ge(ring_free[slot], i + (l * USES[slot] + use[slot] + 1))
                sp.dma_start(ring[:, 2 * slot:2 * slot + n].rearrange("p s k m -> p s (k m)"), src)\
                    .then_inc(ring_in[slot], 16)

            for l in range(DEPTH):
                if l:
                    sp.wait_ge(S["arena_free"], l)
                for dst, src in ((CM, d["cm"]), (W2A2, d["w2a2"][l]), (G2, d["g2"][l]), (VW1, d["vw1"][l]),
                                 (VW2[0:32], d["vw2"][l]), (WST, d["wst"][l]), (SBR[0:1], d["sb"][l]),
                                 (hT[:, :, T:TS], d["sh"][l])):
                    sp.dma_start(dst, src).then_inc(S["smalls_in"], 16)
                use = [0] * RINGP
                wm = d["wm"][l]

                def tiles(first, n):
                    return wm[first:first + n].rearrange("s p m -> p s m")

                def rtiles(base, i, step, off, n):
                    return wm[bass.ds(i * step + (base + off), n)].rearrange("s p m -> p s m")

                with sp.Fori(0, 3) as i:
                    for s in range(RINGP):
                        pair(s, rtiles(0, i, 10, 2 * s, 2), l, i=i)
                use = [3] * RINGP
                for s in range(4):
                    pair(s, tiles(30 + 2 * s, 2), l)
                    use[s] += 1
                with sp.Fori(0, 4) as i:
                    for s in range(RINGP):
                        pair(s, rtiles(38, i, 9, 2 * s, 2 if s < 4 else 1), l, n=2 if s < 4 else 1, i=i)
                use = [u + 4 for u in use]
                for n in range(13):
                    s = n % RINGP
                    pair(s, tiles(74 + 2 * n, 2), l)
                    use[s] += 1
                assert use == USES, use
                sp.wait_ge(S["e_ready"], 3 * (l + 1))
                with sp.Fori(0, NGRP) as i:
                    for par_ in range(2):
                        for j in range(GRP):
                            sp.wait_ge(S["pre_mm"], i * (2 * GRP) + (l * NK + par_ * GRP + j + 1))
                            e = i * (2 * GRP) + (par_ * GRP + j)
                            sp.dma_start(DNR[:, j].rearrange("p k e -> p (k e)"),
                                         d["down"][l][bass.ds(e, 1)].rearrange("a p m -> p (a m)"))\
                                .then_inc(dn_in[j], 16)
                        sp.wait_ge(S["out_mm"], i * (2 * KD) + (l * 2 * NGRP + par_ + 1) * KD)
                        sp.dma_start(UPR[:, par_ * GRP:(par_ + 1) * GRP],
                                     d["up"][l][:, bass.ds(i * (2 * GRP) + par_ * GRP, GRP)])\
                            .then_inc(up_in[par_], 16)
            sp.wait_ge(S["y_out"], 16)

        @block.tensor
        def _(pe):
            def mm(out, lhsT, rhs, start=True, stop=True):
                return pe.matmul(out, lhsT, rhs, start=start, stop=stop)

            def need(name, n):
                pe.wait_ge(S[name], n)

            for s in range(RINGP):
                pe.sem_inc(ring_free[s], 1)
            pe.sem_inc(S["pre_mm"], GRP)
            pe.sem_inc(S["out_mm"], 2 * KD)
            need("par_in", 48)
            use = [0] * RINGP

            def arrive(slot, l, i=0):
                pe.wait_ge(ring_in[slot], (i + (l * USES[slot] + use[slot] + 1)) * 16)

            def proj(out, slot_tile, src, n, k=KD, half=0):
                for kk in range(k):
                    ins = mm(out, ring[:, slot_tile, half * k + kk, :], src[:, kk, 0:n], kk == 0, kk == k - 1)
                return ins

            def spread(sq, outs, weights=ones):
                for i, b in enumerate(outs):
                    ins = mm(b[:, 0:T], weights, sq[:, i, :])
                return ins

            for l in range(DEPTH):
                use = [0] * RINGP
                need("mix_sq", l + 1)
                for k in range(KD):
                    ins = mm(bank[0][:, 0:T], ones, NSQ[:, k, :], k == 0, k == KD - 1)
                ins.then_inc(S["mix_ss"], 1)
                need("h_ready", l + 1)
                need("smalls_in", 16 * NSMALL * (l + 1))
                for k in range(KD):
                    ins = mm(bank[2][0:32, 0:TS], VW1[:, k, :], hT[:, k, :], k == 0, k == KD - 1)
                ins.then_inc(S["xv_mm"], 1)
                with pe.Fori(0, 3) as i:
                    for c in range(10):
                        if c % 2 == 0:
                            arrive(c // 2, l, i)
                        pe.wait_ge(S["z_evac"], i * 10 + (l * 38 + c + 1))
                        proj(bank[c % 2][:, 0:TS], c, hT, TS).then_inc(S["z_mm"], 1)
                        if c % 2:
                            pe.drain().then_inc(ring_free[c // 2], 1)
                use = [3] * RINGP
                for c in range(8):
                    if c % 2 == 0:
                        arrive(c // 2, l)
                    need("z_evac", l * 38 + 30 + c + 1)
                    proj(bank[c % 2][:, 0:TS], c, hT, TS).then_inc(S["z_mm"], 1)
                    if c % 2:
                        pe.drain().then_inc(ring_free[c // 2], 1)
                        use[c // 2] += 1
                need("lora_in", 3 * (l + 1))
                need("zs_ready", 2 * (l + 1))
                lora = [(W2A2[0:64], LW[0:64]), (W2A2[64:128], LW[64:128]), (VW2[0:32], XVS[0:32]), (G2, SGX)]
                for n in range(16):
                    if n >= 4:
                        need("lora_evac", l * 16 + n - 3)
                    w, x = lora[n // 4]
                    mm(bank[2 + n % 4][:, 0:T], w[:, (n % 4) * P:(n % 4 + 1) * P], x).then_inc(S["lora_mm"], 1)
                need("lora_evac", l * 16 + 16)
                need("kk_sq", l + 1)
                spread(T3, bank[2:6], bones).then_inc(S["kk_ss"], 1)
                need("prep_done", l + 1)
                spread(T1, bank[2:6], bones).then_inc(S["bon_mm"], 1)
                need("bon_done", l + 1)
                for g in range(2 * NRC):
                    n, pr = g // 2, g % 2
                    if g >= 4:
                        need("mat_evac", l * 8 + g - 3)
                    hp = slice(64 * pr, 64 * pr + 64)
                    for j in range(NW):
                        ins = mm(bank[g % 4][:, j * P:(j + 1) * P].rearrange("p (a t) -> p a t", a=2),
                                 BKV[hp, j * NRC + n, 0:2, :].rearrange("p a t -> p (a t)"),
                                 AR[hp, j, :, n * RC:(n + 1) * RC])
                    ins.then_inc(S["mat_mm"], 1)
                for half in range(2):
                    for pr in range(2):
                        hp = slice(64 * pr, 64 * pr + 64)
                        if half:
                            need("l_evac", l * 2 + half)
                        for nn in range(2):
                            n = 2 * half + nn
                            for j in range(NW):
                                c = (nn * NW + j) * RC
                                ins = mm(bank[4 + pr][0:RC, c:c + RC], AR[hp, j, 0, n * RC:(n + 1) * RC],
                                         BKV[hp, j * NRC + n, 0, :])
                    ins.then_inc(S["l_mm"], 1)
                    for lev in range(1, LEV_R):
                        e = (l * 2 + half) * (LEV_R - 1) + lev
                        need("x_in2", e)
                        for m in range(2 * RH):
                            ins = mm(bank[m // 8][0:RC, (m % 8) * RC:(m % 8 + 1) * RC], ML[0:RC, m, :],
                                     XT_[0:RC, 16 * half + m, :])
                        ins.then_inc(S["p_mm"], 1)
                        need("p_evac", e)
                        for m in range(2 * RH):
                            c = slice((m % 8) * RC, (m % 8 + 1) * RC)
                            mm(bank[2 + m // 8][0:RC, c], X_[0:RC, m, :], P1[0:RC, m, :])
                        for m in range(2 * RH):
                            c = slice((m % 8) * RC, (m % 8 + 1) * RC)
                            ins = mm(bank[6 + m // 8][0:RC, c], P1[0:RC, m, :], X_[0:RC, m, :])
                        ins.then_inc(S["x_mm"], 1)
                need("x_done", l + 1)
                for n in range(NRC):
                    for v in range(2):
                        g = 2 * n + v
                        if g >= 4:
                            need("tok_evac", l * 8 + g - 3)
                        for j in range(NW):
                            ins = pe.transpose(bank[g % 4][:, j * P:(j + 1) * P],
                                               BKV[:, j * NRC + n, v:v + 2, :].rearrange("p a t -> p (a t)"), ident)
                        ins.then_inc(S["tok_mm"], 1)
                need("tok_evac", l * 8 + 8)
                for n in range(NRC):
                    e = l * NRC + n + 1
                    c = slice(n * RC, (n + 1) * RC)
                    need("s_evac", e + l)
                    for j in range(NW):
                        mm(bank[4][0:RC, j * P:(j + 1) * P], AR[:, j, 0, c], BD[:, j, :])
                    for h in range(RH):
                        idx = n * RH + (h % 2) * NW + h // 2
                        hc = slice(h * RN, (h + 1) * RN)
                        ins = mm(bank[5][0:RC, hc], M[64:128, idx, 0:64], UV[64:128, n, hc])
                    ins.then_inc(S["y_mm"], 1)
                    need("y_evac", e)
                    for h in range(RH):
                        idx = n * RH + (h % 2) * NW + h // 2
                        hc = slice(h * RN, (h + 1) * RN)
                        ins = mm(bank[6][0:RC, hc], XT_[0:RC, idx, :], YSC[0:RC, hc])
                    ins.then_inc(S["u_mm"], 1)
                    need("u_evac", e)
                    if n:
                        need("o_evac", e - 1)
                    for j in range(NW):
                        mm(bank[7][:, j * P:(j + 1) * P], BKT[:, n, j * P:(j + 1) * P], UV[:, n, j * P:(j + 1) * P])
                    for j in range(NW):
                        oc = slice(j * RC, (j + 1) * RC)
                        mm(bank[0][:, oc], BD[:, j, :], AR[:, j, 1, c], True, False)
                        for hh in range(2):
                            idx = n * RH + hh * NW + j
                            h = 2 * j + hh
                            ins = mm(bank[0][64 * hh:64 * hh + 64, oc], UV[:, n, h * RN:(h + 1) * RN],
                                     M[:, idx, 64:128], False, True)
                    ins.then_inc(S["s_mm"], 1)
                need("o_evac", (l + 1) * NRC)
                for g in range(6):
                    if g >= 2:
                        need("sq_evac", l * 6 + g - 1)
                    for j in range(NW):
                        ins = pe.transpose(bank[g % 2][0:DEC, j * P:(j + 1) * P], SQ[:, g, j, :], ident)
                    ins.then_inc(S["sq_mm"], 1)
                need("so_in", 16 * (l + 1))
                need("sq_evac", l * 6 + 6)
                for j in range(NW):
                    ins = pe.transpose(bank[0][:, j * DEC:(j + 1) * DEC], OT[0:DEC, j * P:(j + 1) * P], ident[0:DEC, 0:DEC])
                ins.then_inc(S["ot_mm"], 1)
                need("so_out", l + 1)
                spread(YR, bank[2:6], bones).then_inc(S["gn_sq"], 1)
                need("gn_m", l + 1)
                spread(at(WORK + 1056, NW, T), bank[2:6], bones).then_inc(S["gn_v"], 1)

                for lev in range(LEV_H + 1):
                    need("lev_x", l * (LEV_H + 1) + lev + 1)
                    for c in range(NHC):
                        if lev:
                            need("att_evac", l * 2 * (LEV_H + 1) + 2 * lev + c - 1)
                        cc = slice(c * HC, (c + 1) * HC)
                        for h in range(NW):
                            if lev == 0:
                                a, b = HG[:, 4 + h, cc], HG[:, h, cc]
                            else:
                                a = b = HV[f"HX{lev % 2}"][:, h, cc]
                            ins = mm(bank[c][:, h * P:(h + 1) * P], a, b)
                        ins.then_inc(S["att_mm"], 1)
                need("att_evac", (l + 1) * 2 * (LEV_H + 1))
                need("kh_done", l + 1)
                for g in range(2 * NHC):
                    c = g // 2
                    cc = slice(c * HC, (c + 1) * HC)
                    for h in range(NW):
                        src = HG[:, 8 + h, cc] if g % 2 == 0 else HV["KH"][:, h, cc]
                        ins = pe.transpose(bank[2 + g][:, h * P:(h + 1) * P], src, ident)
                    ins.then_inc(S["ht_mm"], 1)
                for h in range(NW):
                    ins = pe.transpose(bank[6][0:DEC, h * P:(h + 1) * P], HG[:, 8 + h, SEQ:T], ident)
                ins.then_inc(S["vs_mm"], 1)
                need("ht_evac", (l + 1) * 4)
                for c in range(NHC):
                    cc = slice(c * HC, (c + 1) * HC)
                    need("hs_evac", l * 3 + c + 1)
                    for h in range(NW):
                        hc = slice(h * P, (h + 1) * P)
                        mm(bank[2][:, hc], SH[:, h, :], HV["QH"][:, h, cc], True, False)
                        mm(bank[2][:, hc], VT[:, c, h, :], AT_[:, c, h, :], False, True)
                    for h in range(NW):
                        ins = mm(bank[3][:, h * P:(h + 1) * P], KT[:, c, h, :], VT[:, c, h, :])
                    ins.then_inc(S["hs_mm"], 1)
                    need("ho_evac", l * 2 + c + 1)
                need("vs_evac", l + 1)
                for b in range(DEC):
                    if b >= 2:
                        need("vb_evac", l * DEC + b - 1)
                    mm(bank[4 + b % 2][:, 0:W], ident[0:DEC, b:b + 1].broadcast_to([DEC, P]),
                       VS[0:DEC].rearrange("p a b -> p (a b)")).then_inc(S["vb_mm"], 1)
                need("vb_evac", (l + 1) * DEC)
                for b in range(DEC):
                    for h in range(NW):
                        ins = mm(bank[6][:, h * DEC + b:h * DEC + b + 1], SHS[:, b, h, :], HG[:, h, SEQ + b:SEQ + b + 1])
                ins.then_inc(S["hso_mm"], 1)
                need("hn_sq", l + 1)
                spread(HV["U1"], bank[2:6]).then_inc(S["hn_mm"], 1)

                need("z_evac", 2 + (l + 1) * 38)
                for h in range(NW):
                    ins = mm(bank[0][:, 0:T], ones, SG[:, NW + h, :], h == 0, h == NW - 1)
                ins.then_inc(S["sg_mm"], 1)
                need("sg_mu", l + 1)
                for h in range(NW):
                    ins = mm(bank[1][:, 0:T], ones, VQ[:, h, :], h == 0, h == NW - 1)
                ins.then_inc(S["sg_vm"], 1)
                need("sg_vn", l + 1)
                for c in range(NHC):
                    for h in range(NW):
                        ins = pe.transpose(bank[2 + c][:, h * P:(h + 1) * P], VC[:, h, c * HC:(c + 1) * HC], ident)
                    ins.then_inc(S["sgt_mm"], 1)
                need("sgt_evac", 2 * (l + 1))
                for c in range(NHC):
                    for h in range(NW):
                        hc = slice(h * P, (h + 1) * P)
                        mm(bank[4 + c][:, hc], VT2[:, c, h, :], WST[:, h, :], True, False)
                        mm(bank[4 + c][:, hc], ones[0:1, :], SBR[0:1, h, :], False, True)
                mm(bank[6][:, 0:NW], ones[0:1, :], WST[0:1, :, 0])
                mm(bank[6][:, NW:2 * NW], ones[0:1, :], SBR[0:1, :, 0]).then_inc(S["mx_mm"], 1)

                need("mx_evac", l + 1)
                need("yr_done", 2 * (l + 1))
                with pe.Fori(0, 4) as i:
                    for q in range(6):
                        for s in ((0, 3), (), (1,), (), (2, 4), ())[q]:
                            arrive(s, l, i)
                        pe.wait_ge(S["gate_evac"], i * 6 + (l * 24 + q + 1))
                        proj(bank[q % 2][:, 0:T], q, hT, T).then_inc(S["gate_mm"], 1)
                        pe.wait_ge(S["br_evac"], i * 6 + (l * 24 + q + 1))
                        proj(bank[2 + q % 2][:, 0:T], 6 + q // 2, (YR, YH, YS)[q % 3], T, NW, q % 2)\
                            .then_inc(S["br_mm"], 1)
                        for s in ((), (0,), (), (1, 3), (), (2, 4))[q]:
                            pe.drain().then_inc(ring_free[s], 1)
                use = [8, 8, 8, 8, 7]
                need("br_evac", (l + 1) * 24 + 2)
                need("gate_evac", (l + 1) * 24 + 2)
                need("mg_done", l + 1)
                for m in range(KD):
                    s = m // 2
                    if m % 2 == 0:
                        arrive(s, l)
                    proj(bank[m][:, 0:T], m, MG, T).then_inc(S["wo_mm"], 1)
                    if m % 2:
                        pe.drain().then_inc(ring_free[s], 1)
                        use[s] += 1
                need("ffn_sq", l + 1)
                for k in range(KD):
                    ins = mm(bank[0][:, 0:T], ones, NSQ[:, k, :], k == 0, k == KD - 1)
                ins.then_inc(S["ffn_ss"], 1)
                need("h2_ready", l + 1)
                need("keys_moved", l + 1)
                pe.sem_inc(ring_free[4], 1)
                use[4] += 1
                for n in range(2 * PH):
                    s = n // 2 % RINGP
                    if n % 2 == 0:
                        arrive(s, l)
                    if n >= 2:
                        need("q_evac", l * 16 + n - 1)
                    proj(bank[n % 2][:, 0:T], 2 * s + n % 2, hT, T).then_inc(S["q_mm"], 1)
                    if n % 2:
                        pe.drain().then_inc(ring_free[s], 1)
                        use[s] += 1
                assert use == USES, use
                need("q_evac", l * 16 + 16)
                for g in range(12):
                    tc, hp0 = g // 4, 4 * (g % 4)
                    m = P if tc < 2 else DEC
                    if g >= 2:
                        need("sc_evac", l * 12 + g - 1)
                    for k in range(4):
                        ins = mm(bank[4 + g % 2][0:m, k * P:(k + 1) * P], QT[:, hp0 + k, tc * P:tc * P + m],
                                 KEYS[:, hp0 + k, :])
                    ins.then_inc(S["sc_mm"], 1)
                for tc in range(3):
                    need("e_ready", l * 3 + tc + 1)
                    m = P if tc < 2 else DEC
                    if tc:
                        need("et_evac", l * 3 + tc)
                    for k, src in enumerate((E1, E2, GA)):
                        ins = pe.transpose(bank[6][:, k * P:k * P + m], src[0:m].rearrange("p a b -> p (a b)"),
                                           ident[0:m, 0:m])
                    ins.then_inc(S["et_mm"], 1)

                with pe.Fori(0, 2) as hf:
                    with pe.Fori(0, T // TB // 2) as i:
                        for b in range(2):
                            pe.wait_ge(S["oh_ready"], hf * (T // TB) + i * 2 + (l * 2 * (T // TB) + b + 1))
                            pe.wait_ge(S["g_evac"], hf * (T // TB) + i * 2 + (l * 2 * (T // TB) + b + 1))
                            for t in range(TB):
                                ins = mm(bank[6 + b][:, t * HALF:(t + 1) * HALF], OH1[:, b, t, :], OH2[:, b, t, :])
                            ins.then_inc(S["g_mm"], 1)

                    def down(g, i, par_):
                        for j in range(GRP):
                            e = hf * HALF + i * (2 * GRP) + (g * GRP + j)
                            pe.wait_ge(dn_in[j], (hf * NGRP + i * 2 + (l * 2 * NGRP + g + 1)) * 16)
                            pe.wait_ge(S["gelu_done"], e + (l * NK + 1))
                            for k in range(KD):
                                ins = mm(bank[j % 2][:, 0:T], DNR[:, j, k, :], hT[:, k, 0:T], k == 0, k == KD - 1)
                            ins.then_inc(S["pre_mm"], 1)

                    def up(g, i, par_):
                        pe.wait_ge(up_in[par_], (hf * (NGRP // 2) + i + (l * NGRP + g // 2 + 1)) * 16)
                        pe.wait_ge(S["act_ready"], hf * HALF + i * (2 * GRP) + (l * NK + (g + 1) * GRP + 2))
                        for k in range(KD):
                            pe.wait_ge(S["out_evac"], hf * (NGRP * KD) + i * (2 * KD) + (l * 2 * NGRP * KD + g * KD + k + 1))
                            for j in range(GRP):
                                ins = mm(bank[2 + k % 4][:, 0:T], UPR[:, par_ * GRP + j, k * P:(k + 1) * P],
                                         ACTB[:, par_ * GRP + j, :], j == 0, j == GRP - 1)
                            ins.then_inc(S["out_mm"], 1)

                    down(0, 0, 0)
                    with pe.Fori(0, NGRP // 2 - 1) as i:
                        down(1, i, 1)
                        up(0, i, 0)
                        down(2, i, 0)
                        up(1, i, 1)
                    down(NGRP - 1, 0, 1)
                    up(NGRP - 2, 0, 0)
                    up(NGRP - 1, 0, 1)
            need("mix_sq", DEPTH + 1)
            for k in range(KD):
                ins = mm(bank[0][:, 0:T], ones, NSQ[:, k, :], k == 0, k == KD - 1)
            ins.then_inc(S["mix_ss"], 1)

        @block.scalar
        def _(act):
            def need(name, n):
                act.wait_ge(S[name], n)

            def f(out, in_, fn, **kw):
                return act.activation(out, in_, fn, **kw)

            act.sem_inc(S["z_evac"], 2)
            act.sem_inc(S["gelu_done"], 2)
            act.sem_inc(S["gate_evac"], 2)
            act.sem_inc(S["g_evac"], 2)
            need("par_in", 48)
            need("lb_in", 1)
            f(LBS[:, 2:4], LBS[:, 0:2], ACT.Exp).then_inc(S["lb_exp"], 1)
            for l in range(DEPTH):
                need("mix_ss", l + 1)
                f(NRM[:], bank[0][:, 0:T], ACT.Sqrt, scale=1.0 / D_MODEL, bias=com("eps")).then_inc(S["mix_std"], 1)
                need("h_ready", l + 1)
                need("smalls_in", 16 * NSMALL * (l + 1))
                act.dma_start(d["o_shift"][l], hT[:, :, SEQ - 1:T]).then_inc(S["shift_out"], 16)
                need("xv_mm", l + 1)
                f(XV[0:32, 1:ZR_W], bank[2][0:32, 0:TS], ACT.Copy).then_inc(S["xv_evac"], 1)
                def evac(turns, base, dst, n, fn=ACT.Copy):
                    with act.Fori(0, turns) as i:
                        for b in range(2):
                            act.wait_ge(S["z_mm"], i * 2 + (l * 38 + base + b + 1))
                            f(dst(i * 2 + b), bank[b][:, 0:n], fn).then_inc(S["z_evac"], 1)
                evac(7, 0, lambda c: ZR[:, bass.ds(c, 1), 1:ZR_W].rearrange("p a t -> p (a t)"), TS)
                evac(8, 14, lambda c: HG[:, bass.ds(c, 1), :].rearrange("p a t -> p (a t)"), T)
                evac(4, 30, lambda c: SG[:, bass.ds(c, 1), :].rearrange("p a t -> p (a t)"), T, ACT.Gelu)
                need("zs_ready", 2 * l + 2)
                f(LW[0:64], D[0:64, 12, :], ACT.Tanh).then_inc(S["lora_in"], 1)
                f(LW[64:128], D[64:128, 12, :], ACT.Copy).then_inc(S["lora_in"], 1)
                f(SGX, D[:, 13, :], ACT.Sigmoid).then_inc(S["lora_in"], 1)
                for n in range(16):
                    need("lora_mm", l * 16 + n + 1)
                    j = n % 4
                    src = bank[2 + j][:, 0:T]
                    if n < 12:
                        dst = (SW, AA, VG)[n // 4][:, j, :]
                        b = par(l, ("w0", "a0", "v0")[n // 4], j, j + 1)
                        f(dst, src, ACT.Sigmoid, bias=b).then_inc(S["lora_evac"], 1)
                    else:
                        f(GG[:, j, :], src, ACT.Copy).then_inc(S["lora_evac"], 1)
                need("decay_in", l + 1)
                f(EC, CU, ACT.Exp).then_inc(S["decay_out"], 1)
                f(T1, T2, ACT.Exp).then_inc(S["decay_out"], 1)
                need("decay_out", 3 * l + 2)
                f(T2, CU, ACT.Exp, scale=-1.0).then_inc(S["decay_out"], 1)
                need("kk_ss", l + 1)
                need("decay_out", 3 * l + 3)
                for j in range(NW):
                    ins = f(T3[:, j, :], bank[2 + j][:, 0:T], ACT.Sqrt)
                ins.then_inc(S["kk_std"], 1)
                for half in range(2):
                    for lev in range(1, LEV_R):
                        e = (l * 2 + half) * (LEV_R - 1) + lev
                        need("p_mm", e)
                        for b in range(2):
                            ins = f(P1[0:RC, 8 * b:8 * b + 8].rearrange("p a b -> p (a b)"), bank[b][0:RC, :], ACT.Copy)
                        ins.then_inc(S["p_evac"], 1)
                for n in range(NRC):
                    for v in range(2):
                        need("tok_mm", l * 8 + 2 * n + v + 1)
                        if v == 0:
                            f(BKT[:, n], bank[2 * n % 4][:, :], ACT.Copy).then_inc(S["tok_evac"], 1)
                        else:
                            f(UV[64:128, n], bank[(2 * n + 1) % 4][64:128, :], ACT.Copy).then_inc(S["tok_evac"], 1)
                for n in range(NRC):
                    e = l * NRC + n + 1
                    need("u_mm", e)
                    f(UV[0:64, n], bank[6][0:64, :], ACT.Copy).then_inc(S["u_evac"], 1)
                    need("s_mm", e)
                    f(YR[:, :, n * RC:(n + 1) * RC], bank[0][:, 0:NW * RC].rearrange("p (a t) -> p a t", a=NW),
                      ACT.Copy).then_inc(S["o_evac"], 1)
                need("s_evac", (l + 1) * (NRC + 1))
                act.dma_start(d["o_rp"][l], BD).then_inc(S["bd_out"], 16)
                act.dma_start(SR[0:64], d["rs"][l]).then_inc(S["sr_in"], 16)
                for g in range(6):
                    need("sq_mm", l * 6 + g + 1)
                    f(TQ[0:DEC, g], bank[g % 2][0:DEC, :], ACT.Copy).then_inc(S["sq_evac"], 1)
                need("sq_evac", l * 6 + 6)
                for g in range(6):
                    act.dma_start(RQ[0:64, g], TQ[0:DEC, g]).then_inc(S["rq_in"], 16)
                need("sr_done", l + 1)
                act.dma_start(OT[0:DEC], OS[0:64]).then_inc(S["so_in"], 16)
                act.dma_start(d["o_rs"][l], SR[0:64]).then_inc(S["sr_out"], 16)
                need("ot_mm", l + 1)
                f(YR[:, :, SEQ:T], bank[0][:, 0:NW * DEC].rearrange("p (a t) -> p a t", a=NW), ACT.Copy)\
                    .then_inc(S["so_out"], 1)
                need("gn_v", l + 1)
                for j in range(NW):
                    ins = f(T3[:, j, :], bank[2 + j][:, 0:T], ACT.Sqrt, scale=1.0 / RN, bias=com("leps"))
                ins.then_inc(S["gn_std"], 1)
                need("hg_in", l + 1)
                act.dma_start(SHS, d["hs"][l]).then_inc(S["shs_in"], 16)
                f(HV["U1"], HG[:, 0:4, :], ACT.Sigmoid).then_inc(S["hg_sig"], 1)
                f(HV["FF"], HG[:, 4:8, :], ACT.Sigmoid).then_inc(S["hg_sig"], 1)
                f(HV["U2"], HG[:, 12:16, :], ACT.Sigmoid).then_inc(S["hg_sig"], 1)
                need("f_ready", l + 1)
                f(HV["BC"], HV["U1"], ACT.Ln).then_inc(S["f_ln"], 1)
                f(HV["KH"], HV["U2"], ACT.Ln).then_inc(S["f_ln"], 1)
                need("b_ready", l + 1)
                f(HV["EB"], HV["BC"], ACT.Exp).then_inc(S["eb_done"], 1)
                for lev in range(1, LEV_H + 1):
                    need("lev_in", l * LEV_H + lev)
                    hx = HV[f"HX{lev % 2}"]
                    f(hx[:, :, 0:SEQ], hx[:, :, 0:SEQ], ACT.Exp).then_inc(S["lev_exp"], 1)
                need("kh_in", l + 1)
                f(HV["KH"][:, :, 0:SEQ], HV["KH"][:, :, 0:SEQ], ACT.Exp).then_inc(S["kh_exp"], 1)
                for g in range(4):
                    need("ht_mm", l * 4 + g + 1)
                    f((VT, KT)[g % 2][:, g // 2].rearrange("p a b -> p (a b)"), bank[2 + g][:, :], ACT.Copy)\
                        .then_inc(S["ht_evac"], 1)
                need("vs_mm", l + 1)
                f(VS[0:DEC].rearrange("p a b -> p (a b)"), bank[6][0:DEC, :], ACT.Copy).then_inc(S["vs_evac"], 1)
                for c in range(NHC):
                    need("hs_mm", l * 2 + c + 1)
                    f(YH[:, :, c * HC:(c + 1) * HC], bank[2][:, :].rearrange("p (a t) -> p a t", a=NW),
                      ACT.Copy).then_inc(S["ho_evac"], 1)
                need("hs_evac", l * 3 + 3)
                act.dma_start(d["o_hp"][l], SH).then_inc(S["hp_out"], 16)
                need("hso_mm", l + 1)
                f(YH[:, :, SEQ:T], bank[6][:, 0:NW * DEC].rearrange("p (a t) -> p a t", a=NW), ACT.Copy)\
                    .then_inc(S["hso_evac"], 1)
                act.dma_start(d["o_hs"][l], SHS).then_inc(S["h_out"], 16)
                need("hn_mm", l + 1)
                for j in range(NW):
                    ins = f(HV["U2"][:, j, :], bank[2 + j][:, 0:T], ACT.Sqrt, scale=1.0 / P, bias=com("eps"))
                ins.then_inc(S["hn_std"], 1)
                need("sg_vm", l + 1)
                f(NRM[:], bank[1][:, 0:T], ACT.Sqrt, scale=1.0 / W, bias=com("eps")).then_inc(S["sg_std"], 1)
                need("sg_vn", l + 1)
                act.dma_start(d["o_sg"][l], VC[:, :, SEQ:T]).then_inc(S["sgo_out"], 16)
                for c in range(NHC):
                    need("sgt_mm", l * 2 + c + 1)
                    f(VT2[:, c].rearrange("p a b -> p (a b)"), bank[2 + c][:, :], ACT.Copy).then_inc(S["sgt_evac"], 1)
                with act.Fori(0, 12) as i:
                    for b in range(2):
                        act.wait_ge(S["gate_mm"], i * 2 + (l * 24 + b + 1))
                        act.wait_ge(S["br_evac"], i * 2 + (l * 24 + b + 1))
                        f(GS[:, b, :], bank[b][:, 0:T], ACT.Sigmoid).then_inc(S["gate_evac"], 1)
                need("ffn_ss", l + 1)
                f(NRM[:], bank[0][:, 0:T], ACT.Sqrt, scale=1.0 / D_MODEL, bias=com("eps")).then_inc(S["ffn_std"], 1)
                for n in range(16):
                    need("q_mm", l * 16 + n + 1)
                    f(QT[:, n, :], bank[n % 2][:, 0:T], ACT.Copy).then_inc(S["q_evac"], 1)
                for n in range(12):
                    tc, m = n // 4, P if n < 8 else DEC
                    need("sc_mm", l * 12 + n + 1)
                    f(SC[0:m, tc, (n % 4) * 4:(n % 4) * 4 + 4].rearrange("p a b -> p (a b)"),
                      bank[4 + n % 2][0:m, :], ACT.Copy).then_inc(S["sc_evac"], 1)
                for tc in range(3):
                    m = P if tc < 2 else DEC
                    need("sm_in", l * 3 + tc + 1)
                    f(GA[0:m], GA[0:m], ACT.Exp).then_inc(S["sm_exp"], 1)
                with act.Fori(0, 2) as hf:
                    with act.Fori(0, T // TB // 2) as i:
                        for b in range(2):
                            act.wait_ge(S["g_mm"], hf * (T // TB) + i * 2 + (l * 2 * (T // TB) + b + 1))
                            f(GM[:, bass.ds(i * (2 * TB) + b * TB, TB), :].rearrange("p a b -> p (a b)"),
                              bank[6 + b][:, 0:TB * HALF], ACT.Copy).then_inc(S["g_evac"], 1)
                    with act.Fori(0, HALF // 4) as i:
                        for b in range(4):
                            e = hf * HALF + i * 4
                            act.wait_ge(S["pre_mm"], e + (l * NK + b + 1 + GRP))
                            act.wait_ge(S["act_ready"], e + (l * NK + b + 1))
                            f(GB[:, b % 2, :], bank[b % 2][:, 0:T], ACT.Gelu).then_inc(S["gelu_done"], 1)
            need("mix_ss", DEPTH + 1)
            f(NRM[:], bank[0][:, 0:T], ACT.Sqrt, scale=1.0 / D_MODEL, bias=com("eps")).then_inc(S["mix_std"], 1)
            need("h_ready", DEPTH + 1)
            act.dma_start(d["o_y"], hT[:, :, 0:T]).then_inc(S["y_out"], 16)
            for n in ("shift_out", "bd_out", "sr_out", "hp_out", "h_out", "sgo_out"):
                need(n, 16 * DEPTH)
            need("y_out", 16)

        @block.vector
        def _(dve):
            steps = [0]

            def need(name, n):
                dve.wait_ge(S[name], n)

            def step(ins):
                steps[0] += 1
                ins.then_inc(S["dve_step"], 1)
                dve.wait_ge(S["dve_step"], steps[0])

            def done(ins, name, n):
                ins.then_inc(S[name], 1)
                dve.wait_ge(S[name], n)

            def tt(out, a, b, op):
                return dve.tensor_tensor(out, a, b, op)

            def ts(out, a, s1, op0, s2=None, op1=ALU.bypass):
                if s2 is None:
                    return dve.tensor_scalar(out, a, s1, None, op0)
                return dve.tensor_scalar(out, a, s1, s2, op0, op1)

            def stt(out, a, s, b, op0, op1):
                return dve.scalar_tensor_tensor(out=out, in0=a, scalar=s, in1=b, op0=op0, op1=op1)

            def tiled(v, n, w=T):
                return over(v, w)

            def norm(l, g, std_name, std_n, ready, ready_n, sq_name, sq_n):
                done(tt(NSQ, xT[:], xT[:], ALU.mult), sq_name, sq_n)
                need(std_name, std_n)
                step(dve.reciprocal(NRM[:], NRM[:]))
                for k in range(KD):
                    ins = stt(hT[:, k, 0:T], xT[:, k, :], g(k), NRM[:], ALU.mult, ALU.mult)
                done(ins, ready, ready_n)

            dve.sem_inc(S["act_ready"], 2)
            dve.sem_inc(S["br_evac"], 2)
            dve.sem_inc(S["mg_add"], 1)
            dve.sem_inc(S["out_evac"], 4)
            need("par_in", 48)
            step(tt(LBS[:, 4], com("lb0"), com("lb1"), ALU.max))
            tt(LBS[:, 0], com("lb0"), LBS[:, 4], ALU.subtract)
            done(tt(LBS[:, 1], com("lb1"), LBS[:, 4], ALU.subtract), "lb_in", 1)
            need("lb_exp", 1)
            step(tt(LBS[:, 4], LBS[:, 2], LBS[:, 3], ALU.add))
            step(dve.reciprocal(LBS[:, 4], LBS[:, 4]))
            step(tt(LBS[:, 2:4], LBS[:, 2:4], rows(LBS[:, 4], 2), ALU.mult))
            step(tt(LBS[:, 5], LBS[:, 2], LBS[:, 3], ALU.add))
            tt(LBS[:, 4], LBS[:, 2], LBS[:, 2], ALU.subtract)
            step(tt(LBS[:, 5], LBS[:, 5], LBS[:, 2], ALU.subtract))
            step(ts(LBS[:, 4:6], LBS[:, 4:6], 0.0, ALU.max, 1.0, ALU.min))
            step(dve.memset(V1[:], 0.0))
            need("x_in", 16)

            for l in range(DEPTH):
                norm(l, lambda k: par(l, "mix_g", k, k + 1), "mix_std", l + 1, "h_ready", l + 1, "mix_sq", l + 1)
                need("smalls_in", 16 * NSMALL * (l + 1))
                dve.memset(ZR[:, :, 0], 0.0)
                dve.memset(XV[0:32, 0:1], 0.0)
                step(tt(WST, WST, rows(cm("triu"), NW), ALU.mult))
                need("xv_evac", l + 1)
                tt(XVS[0:32, 0:SEQ], XV[0:32, 0:SEQ], XV[0:32, 1:SEQ + 1], ALU.subtract)
                step(tt(XVS[0:32, SEQ:T], XV[0:32, T + 1:ZR_W], XV[0:32, SEQ + 1:T + 1], ALU.subtract))
                done(stt(XVS[0:32], XVS[0:32], par(l, "vmu")[0:32], XV[0:32, 1:T + 1], ALU.mult, ALU.add),
                     "zs_ready", 2 * l + 1)
                need("z_evac", 2 + l * 38 + RT)
                tt(D[:, :, 0:SEQ], ZR[:, :, 0:SEQ], ZR[:, :, 1:SEQ + 1], ALU.subtract)
                step(tt(D[:, :, SEQ:T], ZR[:, :, T + 1:ZR_W], ZR[:, :, SEQ + 1:T + 1], ALU.subtract))
                step(tt(D, D, over(par(l, "mu"), T), ALU.mult))
                done(tt(D, D, ZR[:, :, 1:T + 1], ALU.add), "zs_ready", 2 * l + 2)
                R, K, V = D[:, 0:4, :], D[:, 4:8, :], D[:, 8:12, :]
                need("lora_evac", l * 16 + 4)
                step(ts(SW, SW, -float(np.exp(-0.5)), ALU.mult))
                for j in range(NW):
                    ins = dve.tensor_tensor_scan(CU[:, j, :], cm("rscan"), SW[:, j, :], 0.0, ALU.mult, ALU.add)
                step(ins)
                done(tt(T2, CU, SW, ALU.subtract), "decay_in", l + 1)
                need("lora_evac", l * 16 + 12)
                step(ts(VG, VG, par(l, "on"), ALU.mult))
                step(ts(V1[:], V1[:], par(l, "on"), ALU.mult))
                for j in range(NW):
                    ins = stt(V1[:, j], V[:, j], par(l, "off"), V1[:, j], ALU.mult, ALU.add)
                step(ins)
                step(tt(KK, V1[:], V, ALU.subtract))
                step(tt(KK, KK, VG, ALU.mult))
                step(tt(V, V, KK, ALU.add))

                def chunked(x):
                    return x[:, :, 0:SEQ].rearrange("p j (n t) -> p j n t", t=RC)

                def slot(g):
                    return BKV[:, :, g, :].rearrange("p (j n) t -> p j n t", j=NW)

                dve.tensor_copy(slot(2), chunked(V))
                step(tt(KK, K, over(par(l, "kk"), T), ALU.mult))
                done(tt(T3, KK, KK, ALU.mult), "kk_sq", l + 1)
                need("kk_std", l + 1)
                step(ts(T3, T3, 1e-12, ALU.max))
                step(dve.reciprocal(T3, T3))
                step(tt(KK, KK, T3, ALU.mult))
                need("decay_out", 3 * l + 3)
                tt(AR[:, :, 1, :], R, EC, ALU.mult)
                step(ts(T3, KK, -1.0, ALU.mult))
                step(tt(KK, KK, AA, ALU.mult))
                step(tt(AR[:, :, 0, :], T3, T1, ALU.mult))
                tt(slot(0), chunked(KK), chunked(T2), ALU.mult)
                step(ts(AA, AA, -1.0, ALU.add))
                step(tt(AA, AA, over(par(l, "ka"), T), ALU.mult))
                for j in range(NW):
                    ins = stt(K[:, j], AA[:, j], 1.0, K[:, j], ALU.add, ALU.mult)
                step(ins)
                tt(slot(1), chunked(K), chunked(T2), ALU.mult)
                step(tt(T1, R, K, ALU.mult))
                tt(T1, T1, over(par(l, "rk"), T), ALU.mult).then_inc(S["prep_done"], 1)
                for g, src in enumerate((T3, KK, K, R, EC, V)):
                    ins = dve.tensor_copy(SQ[:, g], src[:, :, SEQ:T])
                step(ins)
                need("bon_mm", l + 1)
                for j in range(NW):
                    ins = tt(BO[:, j, :], bank[2 + j][:, 0:T], V[:, j, :], ALU.mult)
                done(ins, "bon_done", l + 1)
                for g in range(2 * NRC):
                    need("mat_mm", l * 8 + g + 1)
                    ins = tt(M[:, 4 * g:4 * g + 4, :], bank[g % 4][:, :].rearrange("p (a b) -> p a b", a=NW),
                             rows(cm("rw"), NW), ALU.mult)
                    ins.then_inc(S["mat_evac"], 1)
                need("mat_evac", l * 8 + 8)
                for half in range(2):
                    need("l_mm", l * 2 + half + 1)
                    Lv = L_[0:RC].rearrange("p (n q j) s -> p n q (j s)", n=2, q=2)
                    for pr in range(2):
                        ins = tt(Lv[:, :, pr].rearrange("p n (j s) -> p n j s", j=NW),
                                 bank[4 + pr][0:RC, :].rearrange("p (n j s) -> p n j s", n=2, j=NW),
                                 cm("low")[0:RC].rearrange("p (a b s) -> p a b s", a=1, b=1)
                                 .broadcast_to([RC, 2, NW, RC]), ALU.mult)
                    done(ins, "l_evac", l * 2 + half + 1)
                    XH = XT_[0:RC, 16 * half:16 * half + 16, :]
                    I16 = rows(ident[0:RC, 0:RC], 16)
                    step(tt(X_[0:RC], L_[0:RC], rows(cm("lev", 0, RC)[0:RC], 16), ALU.mult))
                    tt(X_[0:RC], X_[0:RC], I16, ALU.add)
                    step(tt(XH, M[0:RC, 16 * half:16 * half + 16, 0:RC], rows(cm("n0")[0:RC], 16), ALU.mult))
                    step(tt(XH, XH, I16, ALU.add))
                    for lev in range(1, LEV_R):
                        e = (l * 2 + half) * (LEV_R - 1) + lev
                        done(tt(ML[0:RC], L_[0:RC], rows(cm("lev", RC * lev, RC)[0:RC], 16), ALU.mult), "x_in2", e)
                        need("x_mm", e)
                        for b in range(2):
                            c = slice(8 * b, 8 * b + 8)
                            xh = XT_[0:RC, 16 * half + 8 * b:16 * half + 8 * b + 8, :]
                            tt(xh, xh, bank[2 + b][0:RC, :].rearrange("p (a b) -> p a b", a=8), ALU.add)
                            ins = tt(X_[0:RC, c], X_[0:RC, c], bank[6 + b][0:RC, :].rearrange("p (a b) -> p a b", a=8),
                                     ALU.add)
                        step(ins)
                ins = dve.memset(BD, 0.0)
                done(ins, "s_evac", l * (NRC + 1) + 1)
                dve.memset(TT_, 0.0).then_inc(S["x_done"], 1)
                for n in range(NRC):
                    e = l * NRC + n + 1
                    need("y_mm", e)
                    step(dve.tensor_copy(YSC[0:RC], bank[4][0:RC, :]))
                    done(tt(YSC[0:RC], YSC[0:RC], bank[5][0:RC, :], ALU.add), "y_evac", e)
                    need("s_mm", e)
                    step(tt(TT_.rearrange("p (a b) -> p a b", a=NW), bank[7][:, :].rearrange("p (a b) -> p a b", a=NW),
                            rows(bones, NW), ALU.mult))
                    step(tt(BD, BD, TT_.rearrange("p (a b) -> p a b", a=NW), ALU.add))
                    done(tt(BD, BD, over(EC[:, :, (n + 1) * RC - 1], P), ALU.mult), "s_evac", e + l + 1)
                need("sr_in", 16 * (l + 1))
                need("rq_in", 96 * (l + 1))
                nkk, kka, k2, r, w, v = (RQ[0:64, g] for g in range(6))
                S64, T64 = SR[0:64], TR[0:64]
                step(tt(T64, S64, rows(nkk, RN), ALU.mult))
                step(dve.tensor_reduce(SA[0:64], T64, AX.X, ALU.add))
                step(tt(S64, S64, rows(w, RN), ALU.mult))
                step(tt(T64, over(SA[0:64], RN), rows(kka, RN), ALU.mult))
                step(tt(S64, S64, T64, ALU.add))
                step(tt(T64, over(v, RN), rows(k2, RN), ALU.mult))
                step(tt(S64, S64, T64, ALU.add))
                step(tt(T64, S64, rows(r, RN), ALU.mult))
                done(dve.tensor_reduce(OS[0:64], T64, AX.X, ALU.add), "sr_done", l + 1)
                need("gn_sq", l + 1)
                for j in range(NW):
                    ins = stt(YR[:, j], bank[2 + j][:, 0:T], -1.0 / RN, YR[:, j], ALU.mult, ALU.add)
                step(ins)
                done(tt(at(WORK + 1056, NW, T), YR, YR, ALU.mult), "gn_m", l + 1)
                need("gn_std", l + 1)
                step(dve.reciprocal(T3, T3))
                step(tt(YR, YR, T3, ALU.mult))
                step(tt(YR, YR, over(par(l, "lg"), T), ALU.mult))
                step(tt(YR, YR, over(par(l, "lb"), T), ALU.add))
                step(tt(YR, YR, BO, ALU.add))
                done(tt(YR, YR, GG, ALU.mult), "yr_done", 2 * l + 1)
                need("z_evac", 2 + (l + 1) * 38)
                need("sr_out", 16 * (l + 1))
                need("bd_out", 16 * (l + 1))
                done(dve.memset(HV["HX0"], 0.0), "hg_in", l + 1)
                need("hg_sig", 3 * (l + 1))
                FF, U1, U2, BC, EB, KH, QH = (HV[n] for n in ("FF", "U1", "U2", "BC", "EB", "KH", "QH"))
                tt(HG[:, 0:4, :], HG[:, 0:4, :], U1, ALU.mult)
                tt(HG[:, 12:16, :], HG[:, 12:16, :], U2, ALU.mult)
                lbl = LBS[:, 4 + l]
                step(ts(SC8[:, 0:4], lbl, -1.0, ALU.mult, 1.0, ALU.add))
                step(tt(FF, FF, over(SC8[:, 0:4], T), ALU.mult))
                step(tt(FF, FF, over(lbl, T), ALU.add))
                ts(HG[:, 4:8, :], FF, -1.0, ALU.mult, 1.0, ALU.add)
                step(ts(FF, FF, 1e-30, ALU.max))
                ts(U1, FF, 2.0 ** -60, ALU.max)
                done(ts(U2, FF, 2.0 ** 60, ALU.mult, 1.0, ALU.min), "f_ready", l + 1)
                need("f_ln", 2 * (l + 1))
                step(tt(U1, BC, KH, ALU.add))
                for j in range(NW):
                    ins = dve.tensor_tensor_scan(BC[:, j, :], cm("hscan"), U1[:, j, :], 0.0, ALU.mult, ALU.add)
                done(ins, "b_ready", l + 1)
                need("eb_done", l + 1)
                tt(QH, HG[:, 0:4, :], EB, ALU.mult).then_inc(S["lev_x"], 1)
                for c in range(NHC):
                    cc = slice(c * HC, (c + 1) * HC)
                    ins = tt(KH[:, :, cc], over(BC[:, :, (c + 1) * HC - 1], HC), BC[:, :, cc], ALU.subtract)
                ins.then_inc(S["kh_in"], 1)

                def cut(ap, b):
                    return ap.rearrange("p a (n b) -> p a n b", b=b)

                def att(lev):
                    for c in range(NHC):
                        e = l * 2 * (LEV_H + 1) + 2 * lev + c + 1
                        need("att_mm", e)
                        src = bank[c][:, :].rearrange("p (a b) -> p a b", a=NW)
                        if lev == 0:
                            done(tt(AT_[:, c], src, rows(cm("hg", P * LEV_H, P), NW), ALU.mult), "att_evac", e)
                        else:
                            step(tt(T5, src, rows(cm("hg", P * (lev - 1), P), NW), ALU.mult))
                            done(tt(AT_[:, c], AT_[:, c], T5, ALU.add), "att_evac", e)

                for lev in range(1, LEV_H + 1):
                    hx = HV[f"HX{lev % 2}"]
                    b = 1 << (lev - 1)
                    for j in range(NW):
                        bc = BC[:, j, 0:SEQ].rearrange("p (n b) -> p n b", b=2 * b)
                        hh = hx[:, j, 0:SEQ].rearrange("p (n b) -> p n b", b=2 * b)
                        ref = bc[:, :, b - 1:b].broadcast_to([P, SEQ // (2 * b), b])
                        tt(hh[:, :, 0:b], ref, bc[:, :, 0:b], ALU.subtract)
                        ins = tt(hh[:, :, b:2 * b], bc[:, :, b:2 * b], ref, ALU.subtract)
                    ins.then_inc(S["lev_in"], 1)
                    att(lev - 1)
                    need("lev_exp", l * LEV_H + lev)
                    for j in range(NW):
                        hh = hx[:, j, 0:SEQ].rearrange("p (n b) -> p n b", b=2 * b)
                        kk_ = HG[:, 4 + j, 0:SEQ].rearrange("p (n b) -> p n b", b=2 * b)
                        qq = HG[:, j, 0:SEQ].rearrange("p (n b) -> p n b", b=2 * b)
                        tt(hh[:, :, 0:b], hh[:, :, 0:b], kk_[:, :, 0:b], ALU.mult)
                        ins = tt(hh[:, :, b:2 * b], hh[:, :, b:2 * b], qq[:, :, b:2 * b], ALU.mult)
                    ins.then_inc(S["lev_x"], 1)
                att(LEV_H)
                need("kh_exp", l + 1)
                done(tt(KH[:, :, 0:SEQ], KH[:, :, 0:SEQ], HG[:, 4:8, 0:SEQ], ALU.mult), "kh_done", l + 1)
                done(dve.memset(SH, 0.0), "hs_evac", 3 * l + 1)
                for c in range(NHC):
                    need("hs_mm", 2 * l + c + 1)
                    step(tt(SH, SH, over(EB[:, :, (c + 1) * HC - 1], P), ALU.mult))
                    done(tt(SH, SH, bank[3][:, :].rearrange("p (a b) -> p a b", a=NW), ALU.add), "hs_evac", 3 * l + c + 2)
                need("shs_in", 16 * (l + 1))
                for b in range(DEC):
                    need("vb_mm", l * DEC + b + 1)
                    tt(SHS[:, b], SHS[:, b], over(EB[:, :, SEQ + b], P), ALU.mult)
                    step(tt(T5, bank[4 + b % 2][:, :].rearrange("p (a b) -> p a b", a=NW),
                            over(HG[:, 4:8, SEQ + b], P), ALU.mult))
                    done(tt(SHS[:, b], SHS[:, b], T5, ALU.add), "vb_evac", l * DEC + b + 1)
                need("ho_evac", 2 * (l + 1))
                need("hso_evac", l + 1)
                done(tt(U1, YH, YH, ALU.mult), "hn_sq", l + 1)
                need("hn_std", l + 1)
                step(dve.reciprocal(U2, U2))
                step(tt(YH, YH, U2, ALU.mult))
                step(tt(YH, YH, over(par(l, "hg"), T), ALU.mult))
                done(tt(YH, YH, HG[:, 12:16, :], ALU.mult), "yr_done", 2 * l + 2)
                need("sg_mm", l + 1)
                for j in range(NW):
                    ins = stt(VC[:, j], bank[0][:, 0:T], -1.0 / W, SG[:, NW + j], ALU.mult, ALU.add)
                step(ins)
                done(tt(VQ, VC, VC, ALU.mult), "sg_mu", l + 1)
                need("sg_std", l + 1)
                step(dve.reciprocal(NRM[:], NRM[:]))
                step(tt(VC, VC, rows(NRM[:], NW), ALU.mult))
                step(tt(VC, VC, over(par(l, "sg"), T), ALU.mult))
                done(tt(VC, VC, over(par(l, "sb"), T), ALU.add), "sg_vn", l + 1)
                need("mx_mm", l + 1)
                for c in range(NHC):
                    cc = slice(c * HC, (c + 1) * HC)
                    tt(YS[:, :, cc], bank[4 + c][:, :].rearrange("p (a b) -> p a b", a=NW), SG[:, 0:4, cc], ALU.mult)
                step(dve.tensor_copy(SC8, bank[6][:, 0:8]))
                step(tt(YS[:, :, SEQ:T], VC[:, :, SEQ:T], over(SC8[:, 0:4], DEC), ALU.mult))
                step(tt(YS[:, :, SEQ:T], YS[:, :, SEQ:T], over(SC8[:, 4:8], DEC), ALU.add))
                done(tt(YS[:, :, SEQ:T], YS[:, :, SEQ:T], SG[:, 0:4, SEQ:T], ALU.mult), "mx_evac", l + 1)
                with dve.Fori(0, 4) as i:
                    for q in range(6):
                        dve.wait_ge(S["gate_evac"], i * 6 + (l * 24 + q + 3))
                        dve.wait_ge(S["br_mm"], i * 6 + (l * 24 + q + 1))
                        mg = MG[:, bass.ds(i * 2 + q // 3, 1), :].rearrange("p a t -> p (a t)")
                        src = bank[2 + q % 2][:, 0:T]
                        if q % 3 == 0:
                            tt(mg, src, GS[:, q % 2, :], ALU.mult).then_inc(S["br_evac"], 1)
                        else:
                            dve.wait_ge(S["mg_add"], i * 4 + (l * 16 + q - 1 - q // 3 + 1))
                            tt(PR, src, GS[:, q % 2, :], ALU.mult).then_inc(S["br_evac"], 1)
                            dve.wait_ge(S["br_evac"], i * 6 + (l * 24 + q + 3))
                            tt(mg, mg, PR, ALU.add).then_inc(S["mg_add"], 1)
                need("br_evac", 2 + 24 * (l + 1))
                need("mg_add", 1 + 16 * (l + 1))
                done(dve.memset(PR, 0.0), "mg_done", l + 1)
                for m in range(KD):
                    need("wo_mm", l * 8 + m + 1)
                    ins = tt(xT[:, m, :], xT[:, m, :], bank[m][:, 0:T], ALU.add)
                    ins.then_inc(S["wo_evac"], 1)
                need("wo_evac", 8 * (l + 1))
                for n in ("shift_out", "sgo_out", "hp_out", "h_out"):
                    need(n, 16 * (l + 1))
                dve.wait_ge(ring_in[4], (l * USES[4] + 8) * 16)
                dve.tensor_copy(KEYS, ring[:, 8:10].rearrange("p s k m -> p (s k) m")).then_inc(S["keys_moved"], 1)
                norm(l, lambda k: par(l, "ffn_g", k, k + 1), "ffn_std", l + 1, "h2_ready", l + 1, "ffn_sq", l + 1)
                for tc in range(3):
                    m = P if tc < 2 else DEC
                    need("sc_evac", l * 12 + 4 * tc + 4)
                    if tc:
                        need("et_mm", l * 3 + tc)
                    for h in range(PH):
                        for p in range(2):
                            top16(dve, step, SC[0:m, tc, 2 * h + p], SV[0:m, h, p], SI[0:m, h, p].bitcast(U32))
                    step(dve.tensor_copy(SIF[0:m], SI[0:m].bitcast(U32)))
                    for h in range(PH):
                        step(tt(COMB[0:m, h], over(SV[0:m, h, 0], TOPK), rows(SV[0:m, h, 1], TOPK), ALU.add))
                        top16(dve, step, COMB[0:m, h].rearrange("p a b -> p (a b)"), CV[0:m, h], CI[0:m, h].bitcast(U32))
                    cu = CI[0:m].bitcast(U32)
                    ts(CA[0:m].bitcast(U32), cu, 4, ALU.logical_shift_right)
                    step(ts(CB[0:m].bitcast(U32), cu, 15, ALU.bitwise_and))
                    dve.tensor_copy(E1[0:m], CA[0:m].bitcast(U32))
                    step(dve.tensor_copy(E2[0:m], CB[0:m].bitcast(U32)))
                    for p, e in enumerate((E1, E2)):
                        ef = e[0:m].rearrange("p a b -> p (a b)")
                        step(tt(OHB[0:m], over(ef, TOPK), rows(cp("iota16")[0:m], P), ALU.is_equal))
                        for h in range(PH):
                            ins = tt(OHB[0:m, h * TOPK:(h + 1) * TOPK], OHB[0:m, h * TOPK:(h + 1) * TOPK],
                                     rows(SIF[0:m, h, p], TOPK), ALU.mult)
                        step(ins)
                        step(dve.tensor_reduce(ef, OHB[0:m], AX.X, ALU.add))
                    done(tt(GA[0:m], CV[0:m], CV[0:m, :, 0:1].broadcast_to([m, PH, TOPK]), ALU.subtract),
                         "sm_in", l * 3 + tc + 1)
                    need("sm_exp", l * 3 + tc + 1)
                    step(dve.tensor_reduce(SM[0:m, 0], GA[0:m], AX.X, ALU.add))
                    step(dve.reciprocal(SM[0:m, 1], SM[0:m, 0]))
                    tt(GA[0:m], GA[0:m], over(SM[0:m, 1], TOPK), ALU.mult).then_inc(S["e_ready"], 1)
                    need("et_mm", l * 3 + tc + 1)
                    for k, dst in enumerate((E1T, E2T, GTT)):
                        ins = dve.tensor_copy(dst[:, tc * P:tc * P + m], bank[6][:, k * P:k * P + m])
                    done(ins, "et_evac", l * 3 + tc + 1)
                step(dve.memset(ACC, 0.0))
                with dve.Fori(0, 2) as hf:
                    with dve.Fori(0, T // TB // 2) as i:
                        for b in range(2):
                            dve.wait_ge(S["g_evac"], hf * (T // TB) + i * 2 + (l * 2 * (T // TB) + b + 1))
                            for t in range(TB):
                                tk = bass.ds(i * (2 * TB) + b * TB + t, 1)
                                ts(OH1[:, b, t, :], cp("iota"), E1T[:, tk], ALU.is_equal)
                                ins = ts(OH2[:, b, t, :], cp("iota")[:, bass.ds(hf * HALF, HALF)], E2T[:, tk], ALU.is_equal,
                                         GTT[:, tk], ALU.mult)
                            ins.then_inc(S["oh_ready"], 1)
                    dve.wait_ge(S["g_evac"], hf * (T // TB) + (l * 2 * (T // TB) + T // TB + 2))

                    def gate(g, i, par_):
                        for j in range(GRP):
                            e = hf * HALF + i * (2 * GRP) + (l * NK + g * GRP + j)
                            dve.wait_ge(S["gelu_done"], e + 3)
                            tt(ACTB[:, par_ * GRP + j, :], GB[:, j % 2, :],
                               GM[:, :, bass.ds(i * (2 * GRP) + g * GRP + j, 1)].rearrange("p t a -> p (t a)"),
                               ALU.mult).then_inc(S["act_ready"], 1)

                    def gather(g, i):
                        for k in range(KD):
                            n = hf * (NGRP * KD) + i * (2 * KD) + (l * 2 * NGRP * KD + g * KD + k + 1)
                            dve.wait_ge(S["out_mm"], n + 2 * KD)
                            tt(ACC[:, k, :], ACC[:, k, :], bank[2 + k % 4][:, 0:T], ALU.add)\
                                .then_inc(S["out_evac"], 1)

                    gate(0, 0, 0)
                    with dve.Fori(0, NGRP // 2 - 1) as i:
                        gate(1, i, 1)
                        gather(0, i)
                        gate(2, i, 0)
                        gather(1, i)
                    gate(NGRP - 1, 0, 1)
                    gather(NGRP - 2, 0)
                    gather(NGRP - 1, 0)
                need("out_evac", 4 + (l + 1) * 2 * NGRP * KD)
                done(tt(xT[:], xT[:], ACC, ALU.add), "arena_free", l + 1)
            norm(0, lambda k: com("fin_g", k, k + 1), "mix_std", DEPTH + 1, "h_ready", DEPTH + 1, "mix_sq", DEPTH + 1)


def top16(dve, step, scores, values, index):
    step(dve.max(values[:, 0:8], scores))
    dve.max_index(index[:, 0:8], values[:, 0:8], scores)
    step(dve.match_replace(scores, values[:, 0:8], scores, -3.0e38))
    step(dve.max(values[:, 8:16], scores))
    step(dve.max_index(index[:, 8:16], values[:, 8:16], scores))


INS = ["x", "cp", "cm", "par", "com", "w2a2", "g2", "vw1", "vw2", "wst", "sb", "sh", "wm", "down", "up", "rs", "hs"]
OUTS = {"o_y": (P, KD, T), "o_shift": (DEPTH, P, KD, DEC + 1), "o_rp": (DEPTH, P, NW, P),
        "o_rs": (DEPTH, DEC * RH, RN, RN), "o_hp": (DEPTH, P, NW, P), "o_hs": (DEPTH, P, DEC, NW, P),
        "o_sg": (DEPTH, P, NW, DEC)}


def lay_out(a):
    def col(v):
        return v.reshape(-1, P).T

    def wtile(w, k):
        return w.reshape(k, P, -1, P).transpose(2, 1, 0, 3)

    f = np.float32
    z32 = np.zeros((96,), f)
    out = {"x": np.concatenate([a["x_prompt"][0], a["x_sample"][:, 0]], 0).T.reshape(KD, P, T).transpose(1, 0, 2)}
    out["cp"], out["cm"] = masks()
    par = []
    for l in range(DEPTH):
        vmu = a["vres_mu"][l - 1] if l else np.zeros(32, f)
        v0 = a["vres_v0"][l - 1] if l else np.zeros(W, f)
        cols = {"mix_g": a["norm_mix_g"][l], "ffn_g": a["norm_ffn_g"][l], "mu": a["shift_mu"][l],
                "w0": a["rwkv_w0"][l], "a0": a["rwkv_a0"][l], "kk": a["rwkv_kk"][l], "ka": a["rwkv_ka"][l],
                "rk": a["rwkv_rk"][l].reshape(-1), "lg": a["rwkv_lnx_g"][l], "lb": a["rwkv_lnx_b"][l],
                "vmu": np.concatenate([vmu, z32]), "v0": v0, "hg": a["hgrn_norm_g"][l], "sg": a["sgu_ln_g"][l],
                "sb": a["sgu_ln_b"][l], "on": np.full(P, float(l > 0), f), "off": np.full(P, float(l == 0), f)}
        par.append(np.concatenate([col(cols[n]) for n, _ in PARS], 1))
    out["par"] = np.stack(par, 1)
    out["com"] = np.concatenate([col(a["hgrn_lb"][0]), col(a["hgrn_lb"][1]), col(a["norm_final_g"]),
                                 np.full((P, 1), EPS, f), np.full((P, 1), LNX_EPS, f)], 1)
    out["w2a2"] = np.concatenate([a["rwkv_w2"], a["rwkv_a2"]], 1)
    out["g2"] = a["rwkv_g2"]
    z = np.zeros((1, D_MODEL, 32), f)
    out["vw1"] = np.concatenate([z, a["vres_w1"]], 0).reshape(DEPTH, KD, P, 32).transpose(0, 2, 1, 3)
    out["vw2"] = np.concatenate([np.zeros((1, 32, W), f), a["vres_w2"]], 0)
    out["wst"] = a["sgu_ws"].transpose(0, 3, 1, 2)
    out["sb"] = a["sgu_b"].reshape(DEPTH, 1, NW, P)
    out["sh"] = a["state_shift"].transpose(0, 2, 1).reshape(DEPTH, KD, P, DEC).transpose(0, 2, 1, 3)
    wm = []
    for l in range(DEPTH):
        win = wtile(a["w_in"][l], KD).reshape(-1, P, D_MODEL)
        gates = win[38:].reshape(3, KD, P, D_MODEL)
        br = np.stack([wtile(a[n][l], NW) for n in ("w_branch_rwkv", "w_branch_hgrn", "w_branch_sgu")])
        rows_ = [win[:38]]
        for mp in range(4):
            rows_.append(gates[:, 2 * mp:2 * mp + 2].transpose(1, 0, 2, 3).reshape(6, P, D_MODEL))
            b = br[:, 2 * mp:2 * mp + 2].transpose(1, 0, 2, 3, 4).reshape(3, 2, P, W)
            rows_.append(b.transpose(0, 2, 1, 3).reshape(3, P, D_MODEL))
        rows_.append(wtile(a["w_out"][l], KD).reshape(-1, P, D_MODEL))
        keys = a["peer_keys"][l].reshape(2 * PH, NK, P).transpose(2, 0, 1).reshape(P, 2, D_MODEL)
        rows_.append(keys.transpose(1, 0, 2))
        rows_.append(wtile(a["peer_wq"][l], KD).reshape(-1, P, D_MODEL))
        wm.append(np.concatenate(rows_, 0))
    out["wm"] = np.stack(wm)
    out["down"] = a["peer_down"].reshape(DEPTH, P, NK, KD, P).transpose(0, 2, 4, 3, 1).reshape(DEPTH, NK, P, D_MODEL)
    out["up"] = a["peer_up"].reshape(DEPTH, P, NK, D_MODEL)
    out["rs"] = a["state_rwkv"].reshape(DEPTH, DEC * RH, RN, RN)
    out["hs"] = a["state_hgrn"].transpose(0, 3, 1, 2, 4)
    return {n: np.ascontiguousarray(v) for n, v in out.items()}


def kernel(**inputs):
    import concourse.bacc as bacc
    from concourse.bass_utils import run_bass_kernel_spmd

    arrays = lay_out({n: np.asarray(v) for n, v in inputs.items()})
    nc = bacc.Bacc("TRN2", target_bir_lowering=False, num_devices=1)
    d = {n: nc.dram_tensor(n, arrays[n].shape, F32, kind="ExternalInput").ap() for n in INS}
    for n, shape in OUTS.items():
        d[n] = nc.dram_tensor(n, shape, F32, kind="ExternalOutput").ap()
    build(nc, d)
    r = run_bass_kernel_spmd(nc, [{n: arrays[n] for n in INS}], core_ids=[0]).results[0]
    y = r["o_y"].transpose(2, 1, 0).reshape(T, D_MODEL)
    sh = r["o_shift"].transpose(0, 3, 2, 1).reshape(DEPTH, DEC + 1, D_MODEL)
    rp = r["o_rp"].reshape(DEPTH, 2, RN, NW, 2, RN)
    rp = np.stack([rp[:, 0, :, :, 0], rp[:, 1, :, :, 1]], 3)
    rp = rp.transpose(0, 2, 3, 4, 1).reshape(DEPTH, 1, RH, RN, RN)
    return (y[None, :SEQ], y[SEQ:, None], sh[:, 0:1], sh[:, 1:], rp,
            r["o_rs"].reshape(DEPTH, DEC, RH, RN, RN),
            r["o_hp"].transpose(0, 2, 1, 3).reshape(DEPTH, 1, NW, P, P),
            r["o_hs"].transpose(0, 2, 3, 1, 4),
            r["o_sg"].transpose(0, 3, 2, 1).reshape(DEPTH, DEC, 1, W))
```

```python
from contextlib import ExitStack

import numpy as np

import concourse.bass as bass
from concourse import mybir

F32 = mybir.dt.float32
U32 = mybir.dt.uint32
ALU = mybir.AluOpType
ACT = mybir.ActivationFunctionType
AX = mybir.AxisListType

P = 128
D_MODEL = 1024
KD = D_MODEL // P
SEQ, DEC, DEPTH = 256, 8, 2
T = SEQ + DEC
TS = T + DEC
W = 512
NW = W // P
RH, RN = 8, 64
RC = 64
NRC = SEQ // RC
HC = 128
NHC = SEQ // HC
LEV_R, LEV_H = 6, 7
PH, TOPK, NK = 8, 16, 128
ZR_W = TS + 1
RT, HT_, ST = 14, 16, 8
EPS, LNX_EPS = 1e-6, 64e-5
RINGP = 5
HALF = NK // 2
GRP = 2
NGRP = HALF // GRP
TB = 8
NB = T // TB

PARS = [("mix_g", 8), ("ffn_g", 8), ("mu", RT), ("w0", 4), ("a0", 4), ("kk", 4), ("ka", 4), ("rk", 4),
        ("lg", 4), ("lb", 4), ("vmu", 1), ("v0", 4), ("hg", 4), ("sg", 4), ("sb", 4), ("on", 1), ("off", 1)]
PAR_AT, PAR_N = {}, 0
for _n, _c in PARS:
    PAR_AT[_n] = (PAR_N, _c)
    PAR_N += _c
COM_AT = {"lb0": (0, 4), "lb1": (4, 4), "fin_g": (8, 8), "eps": (16, 1), "leps": (17, 1)}
COM_N = 18

CP_AT = {"ident": (0, 128), "ones": (128, 128), "bones": (256, 128), "iota": (384, 128), "iota16": (512, 16)}
CP_N = 528
CM_AT = {"rw": (0, 128), "n0": (128, 64), "lev": (192, 64 * LEV_R), "low": (576, 64), "hg": (640, 128 * 8),
         "triu": (1664, 128), "rscan": (1792, T), "hscan": (1792 + T, T)}
CM_N = 1792 + 2 * T


def masks():
    i = np.arange(P)
    cp = np.zeros((P, CP_N), np.float32)
    cp[:, 0:128] = np.eye(P)
    cp[:, 128:256] = 1
    cp[:, 256:384] = (i[:, None] // RN == i[None] // RN)
    cp[:, 384:512] = i[None]
    cp[:, 512:528] = i[None, :16]
    cm = np.zeros((P, CM_N), np.float32)
    s, t = i[:, None] % RC, i[None, :RC]
    cm[:, 0:64], cm[:, 64:128] = s < t, s <= t
    r, c = i[:RC, None], i[None, :RC]
    for lev in range(LEV_R):
        b = 2 << lev
        m = (r // b == c // b) & (r % b >= b // 2) & (c % b < b // 2)
        cm[:RC, 192 + 64 * lev:256 + 64 * lev] = m
        if lev == 0:
            cm[:RC, 128:192] = m.T
    cm[:RC, 576:640] = c < r
    s, t = i[:, None], i[None]
    for lev in range(LEV_H):
        b = 2 << lev
        cm[:, 640 + 128 * lev:768 + 128 * lev] = (s // b == t // b) & (s % b < b // 2) & (t % b >= b // 2)
    cm[:, 640 + 128 * LEV_H:768 + 128 * LEV_H] = s == t
    cm[:, 1664:1792] = s <= t
    t = np.arange(T)
    cm[:, 1792:1792 + T] = ((t % RC != 0) & (t < SEQ))[None]
    cm[:, 1792 + T:] = ((t % HC != 0) & (t < SEQ))[None]
    return cp, cm


def build(nc, d):
    ctx = ExitStack()
    with ctx:
        def sb(name, *shape, dt=F32):
            return ctx.enter_context(nc.sbuf_tensor(name, list(shape), dt))

        xT = sb("xT", P, KD, T)
        hT = sb("hT", P, KD, TS)
        ring = sb("ring", P, 2 * RINGP, KD, P)
        CP = sb("CP", P, CP_N)
        PAR = sb("PAR", P, DEPTH, PAR_N)
        COM = sb("COM", P, COM_N)
        LBS = sb("LBS", P, 6, NW)
        V1 = sb("V1", P, NW, T)
        NRM = sb("NRM", P, T)
        ARENA = 35800
        mixer_memory = ExitStack()
        arena = mixer_memory.enter_context(nc.sbuf_tensor("arena", [P, ARENA], F32))
        bank = [ctx.enter_context(nc.psum_tensor(f"bank{i}", [P, 512], F32)) for i in range(8)]

        def at(off, *dims):
            n = 1
            for x in dims:
                n *= x
            assert off + n <= ARENA, (off, n)
            v = arena[:, off:off + n]
            if len(dims) == 2:
                v = v.rearrange("p (a b) -> p a b", a=dims[0])
            if len(dims) == 3:
                v = v.rearrange("p (a b c) -> p a b c", a=dims[0], b=dims[1])
            return v

        CM = at(0, CM_N)
        o = CM_N
        W2A2 = at(o, W)
        G2 = at(o + 512, W)
        VW1 = at(o + 1024, KD, 32)
        VW2 = at(o + 1280, W)
        WST = at(o + 1792, NW, P)
        SBR = at(o + 2304, NW, P)
        o += 2816
        ZR = at(o, RT, ZR_W)
        XV = at(o + RT * ZR_W, ZR_W)
        RZ = o
        o += 4096
        HG = at(o, HT_, T)
        o += HT_ * T
        SG = at(o, ST, T)
        o += ST * T
        YR, YH, YS = (at(o + n * NW * T, NW, T) for n in range(3))
        o += 3 * NW * T
        WORK = o
        AR = at(o, NW, 2, T)
        BKV = at(o + 2112, NW * NRC, 3, RC)
        EC = at(o + 5280, NW, T)
        GG = at(o + 6336, NW, T)
        BO = at(o + 7392, NW, T)
        M = at(o + 8448, 4 * RH, P)
        LEFT = o + 12544
        D = at(LEFT, RT, T)
        XVS, LW, SGX = (at(LEFT + RT * T + n * T, T) for n in range(3))
        SW, AA, VG = (at(o + 8448 + n * NW * T, NW, T) for n in range(3))
        CU, T1, T2 = (at(RZ + n * NW * T, NW, T) for n in range(3))
        KK, T3 = YH, YS
        XT_ = at(RZ, 4 * RH, RC)
        YSC = at(RZ + 2048, W)
        BD = at(RZ + 2560, NW, P)
        TT_ = at(RZ + 3072, W)
        SQ = at(RZ + 3584, 6, NW, DEC)
        X_, P1, ML, L_ = (at(LEFT + n * 1024, 2 * RH, RC) for n in range(4))
        BKT = at(LEFT, NRC, W)
        UV = at(LEFT + 2048, NRC, W)
        SR = at(o + 8448, RN, RN)
        TR = at(LEFT, RN, RN)
        RQ = at(o, 6, RN)
        SA = at(o + 384, RN)
        OS = at(o + 448, RN)
        OT = at(o + 512, W)
        TQ = at(o + 2112, 6, W)
        names = ["EB", "QH", "KH", "BC", "FF", "U1", "U2", "HX0", "HX1"]
        HV = {n: at(o + i * NW * T, NW, T) for i, n in enumerate(names)}
        q = o + len(names) * NW * T
        AT_, VT, KT = (at(q + n * 1024, NHC, NW, P) for n in range(3))
        q += 3072
        SH, T5, VS = (at(q + n * 512, NW, P) for n in range(3))
        SHS = at(RZ, DEC, NW, P)
        VC, VQ = at(o, NW, T), at(o + 1056, NW, T)
        VT2 = at(o + 2112, NHC, NW, P)
        SC8 = at(o + 3136, 8)
        MG = at(o + 4096, KD, T)
        GS = at(o + 4096 + KD * T, 2, T)
        PR = at(o + 4096 + KD * T + 2 * T, T)
        NSQ = at(WORK, KD, T)

        mixer_memory.close()
        FR = mybir.dt.float32r
        ACTS = sb("ACTS", P, HALF, T)
        ET = sb("ET", P, 2, T)
        GHL = sb("GHL", P, 2, T, dt=FR)
        HHL = sb("HHL", P, 2, KD, T, dt=FR)
        DHL = sb("DHL", P, 2, 2, D_MODEL, dt=FR)
        topk_memory = ExitStack()
        TKN = 10304
        tk = topk_memory.enter_context(nc.sbuf_tensor("topk", [P, TKN], F32))
        topk_memory.close()
        UHL = sb("UHL", P, 2, 2, GRP, D_MODEL, dt=FR)
        AHL = sb("AHL", P, 2, 2, GRP, T, dt=FR)
        at_ = [0]

        def tka(*dims):
            n = int(np.prod(dims))
            v = tk[:, at_[0]:at_[0] + n]
            at_[0] += n
            assert at_[0] <= TKN
            if len(dims) == 2:
                v = v.rearrange("p (a b) -> p a b", a=dims[0])
            if len(dims) == 3:
                v = v.rearrange("p (a b c) -> p a b c", a=dims[0], b=dims[1])
            return v

        QT = tka(2 * PH, T)
        SC = [tka(2 * PH, P)] + [ring[:, 2 * n:2 * n + 2].rearrange("p s k m -> p (s k) m") for n in range(2)]
        SV, SI = tka(PH, 2, TOPK), tka(PH, 2, TOPK)
        COMB = tka(PH, TOPK, TOPK)
        CV, CI = tka(PH, TOPK), tka(PH, TOPK)
        EG = [[tka(PH, TOPK) for n in range(3)] for tc in range(3)]
        SM = tka(2, PH)
        qt = QT.rearrange("p a t -> p (a t)")
        PKR = qt[:, 0:2 * NK].rearrange("p (a b) -> p a b", a=2)
        SE1, SE2, SGA = (qt[:, 2 * NK + n * TOPK:2 * NK + (n + 1) * TOPK] for n in range(3))
        KEYS = ring[:, 4:6].rearrange("p s k m -> p (s k) m")
        OH1 = UHL[:, 0, 0].rearrange("p a m -> p (a m)").rearrange("p (b t e) -> p b t e", b=2, t=TB)
        OH2 = UHL[:, 0, 1].rearrange("p a m -> p (a m)")[:, 0:4 * TB * HALF]\
            .rearrange("p (b q e) -> p b q e", b=2, q=2)
        OHE = UHL[:, 1, 0].rearrange("p a m -> p (a m)")[:, 0:2 * TB * HALF]\
            .rearrange("p (b t e) -> p b t e", b=2, t=TB)
        RAWD, RAWU = 6, 0

        names = """par_in smalls_in lb_in lb_exp mix_sq mix_ss mix_std h_ready shift_out z_mm z_evac xv_mm
            xv_evac zs_ready lora_in lora_mm lora_evac decay_in decay_out kk_sq kk_ss kk_std prep_done bon_done
            bon_mm mat_mm mat_evac l_mm l_evac p_mm p_evac x_in2 x_mm x_done tok_mm tok_evac y_mm y_evac u_mm
            u_evac o_evac s_mm s_evac sq_mm sq_evac rq_in sr_in sr_done sr_out so_out so_in ot_mm gn_m gn_sq gn_v
            gn_std yr_done hg_in hg_sig f_ready f_ln b_ready eb_done lev_in lev_exp lev_x att_mm att_evac kh_in
            kh_exp kh_done ht_mm ht_evac ho_evac hs_mm hs_evac shs_in vs_mm vs_evac vb_mm vb_evac hso_mm hso_evac
            hn_sq hn_mm hn_std h_out sg_mm sg_mu sg_vm sg_std sg_vn sgt_mm sgt_evac mx_mm mx_evac sgo_out
            gate_mm gate_evac br_mm br_evac wo_mm wo_evac ffn_sq ffn_ss ffn_std h2_ready q_mm q_evac
            sc_mm sc_evac sm_in sm_exp e_ready et_mm et_evac oh1_ready oe_ready oh_ready g_mm g_evac
            dhi_done dlo_done uhi_done ulo_done ahi_done alo_done hlo_done packed_in gs_done pre_mm gelu_done
            out_mm out_evac y_out bd_out hp_out arena_free dve_step mg_add mg_done""".split()
        S = {n: ctx.enter_context(nc.semaphore(n)) for n in dict.fromkeys(names)}
        ring_in = [ctx.enter_context(nc.semaphore(f"ring_in{i}")) for i in range(RINGP)]
        ring_free = [ctx.enter_context(nc.semaphore(f"ring_free{i}")) for i in range(RINGP)]
        dn_in = [ctx.enter_context(nc.semaphore(f"dn_in{i}")) for i in range(4)]
        up_in = [ctx.enter_context(nc.semaphore(f"up_in{i}")) for i in range(2)]
        NSMALL = 8
        USES = [11, 11, 11, 10, 9]

        def par(l, n, a=0, b=None):
            c, k = PAR_AT[n]
            return PAR[:, l, c + a:c + (k if b is None else b)]

        def com(n, a=0, b=None):
            c, k = COM_AT[n]
            return COM[:, c + a:c + (k if b is None else b)]

        def cp(n):
            c, k = CP_AT[n]
            return CP[:, c:c + k]

        def cm(n, a=0, k=None):
            c, w = CM_AT[n]
            return CM[:, c + a:c + a + (w if k is None else k)]

        ident, ones, bones = cp("ident"), cp("ones"), cp("bones")

        def over(ap, n):
            return ap.rearrange("p (a b) -> p a b", b=1).broadcast_to([ap.shape[0], ap.shape[1], n])

        def rows(ap, n):
            return ap.rearrange("p (a b) -> p a b", a=1).broadcast_to([ap.shape[0], n, ap.shape[1]])

        block = ctx.enter_context(nc.Block())

        @block.sync
        def _(sp):
            sp.dma_start(xT[:], d["x"]).then_inc(S["par_in"], 16)
            for dst, src in ((CP[:], d["cp"]), (PAR[:], d["par"]), (COM[:], d["com"])):
                sp.dma_start(dst, src).then_inc(S["par_in"], 16)
            use = [0] * RINGP

            def pair(slot, src, l, n=2, i=0):
                sp.wait_ge(ring_free[slot], i + (l * USES[slot] + use[slot] + 1))
                sp.dma_start(ring[:, 2 * slot:2 * slot + n].rearrange("p s k m -> p s (k m)"), src)\
                    .then_inc(ring_in[slot], 16)

            for l in range(DEPTH):
                if l:
                    sp.wait_ge(S["arena_free"], l)
                for dst, src in ((CM, d["cm"]), (W2A2, d["w2a2"][l]), (G2, d["g2"][l]), (VW1, d["vw1"][l]),
                                 (VW2[0:32], d["vw2"][l]), (WST, d["wst"][l]), (SBR[0:1], d["sb"][l]),
                                 (hT[:, :, T:TS], d["sh"][l])):
                    sp.dma_start(dst, src).then_inc(S["smalls_in"], 16)
                use = [0] * RINGP
                wm = d["wm"][l]

                def tiles(first, n):
                    return wm[first:first + n].rearrange("s p m -> p s m")

                def rtiles(base, i, step, off, n):
                    return wm[bass.ds(i * step + (base + off), n)].rearrange("s p m -> p s m")

                with sp.Fori(0, 3) as i:
                    for s in range(RINGP):
                        pair(s, rtiles(0, i, 10, 2 * s, 2), l, i=i)
                use = [3] * RINGP
                for s in range(4):
                    pair(s, tiles(30 + 2 * s, 2), l)
                    use[s] += 1
                with sp.Fori(0, 4) as i:
                    for s in range(RINGP):
                        pair(s, rtiles(38, i, 9, 2 * s, 2 if s < 4 else 1), l, n=2 if s < 4 else 1, i=i)
                use = [u + 4 for u in use]
                for n in range(13):
                    s = n % RINGP
                    pair(s, tiles(74 + 2 * n, 2), l)
                    use[s] += 1
                assert use == USES, use
                def down(n, slot, turn):
                    sp.wait_ge(S["dlo_done"], turn + (l * NK + n + 1))
                    sp.dma_start(ring[:, RAWD + slot].rearrange("p k e -> p (k e)"),
                                 d["down"][l][bass.ds(turn + n, 1)].rearrange("a p m -> p (a m)"))\
                        .then_inc(dn_in[slot], 16)

                def up(g, slot, turn):
                    sp.wait_ge(S["ulo_done"], turn + (l * 2 * NGRP + g + 1))
                    sp.wait_ge(S["alo_done"], turn + (l * 2 * NGRP + g + 1))
                    sp.dma_start(ring[:, RAWU + 2 * slot:RAWU + 2 * slot + 2].rearrange("p s k m -> p s (k m)"),
                                 d["up"][l][:, bass.ds(turn * GRP + g * GRP, GRP)]).then_inc(up_in[slot], 16)

                sp.wait_ge(S["sc_mm"], 12 * (l + 1))
                with sp.Fori(0, HALF // 4) as i:
                    for b in range(4):
                        down(b, b, i * 4)
                sp.wait_ge(S["packed_in"], (l + 1) * 64)
                with sp.Fori(0, NGRP // 2) as i:
                    for b in range(2):
                        up(b, b, i * 2)
                        down(HALF + 2 * b, 2 * b, i * 4)
                        down(HALF + 2 * b + 1, 2 * b + 1, i * 4)
                with sp.Fori(0, NGRP // 2) as i:
                    for b in range(2):
                        up(NGRP + b, b, i * 2)
            sp.wait_ge(S["y_out"], 16)

        @block.tensor
        def _(pe):
            def mm(out, lhsT, rhs, start=True, stop=True):
                return pe.matmul(out, lhsT, rhs, start=start, stop=stop)

            def need(name, n):
                pe.wait_ge(S[name], n)

            for s in range(RINGP):
                pe.sem_inc(ring_free[s], 1)
            pe.sem_inc(S["pre_mm"], 2)
            pe.sem_inc(S["out_mm"], 2 * KD)
            pe.sem_inc(S["g_mm"], 2)
            need("par_in", 64)
            use = [0] * RINGP

            def arrive(slot, l, i=0):
                pe.wait_ge(ring_in[slot], (i + (l * USES[slot] + use[slot] + 1)) * 16)

            def proj(out, slot_tile, src, n, k=KD, half=0):
                for kk in range(k):
                    ins = mm(out, ring[:, slot_tile, half * k + kk, :], src[:, kk, 0:n], kk == 0, kk == k - 1)
                return ins

            def spread(sq, outs, weights=ones):
                for i, b in enumerate(outs):
                    ins = mm(b[:, 0:T], weights, sq[:, i, :])
                return ins

            for l in range(DEPTH):
                use = [0] * RINGP
                need("mix_sq", l + 1)
                for k in range(KD):
                    ins = mm(bank[0][:, 0:T], ones, NSQ[:, k, :], k == 0, k == KD - 1)
                ins.then_inc(S["mix_ss"], 1)
                need("h_ready", l + 1)
                need("smalls_in", 16 * NSMALL * (l + 1))
                for k in range(KD):
                    ins = mm(bank[2][0:32, 0:TS], VW1[:, k, :], hT[:, k, :], k == 0, k == KD - 1)
                ins.then_inc(S["xv_mm"], 1)
                with pe.Fori(0, 3) as i:
                    for c in range(10):
                        if c % 2 == 0:
                            arrive(c // 2, l, i)
                        pe.wait_ge(S["z_evac"], i * 10 + (l * 38 + c + 1))
                        proj(bank[c % 2][:, 0:TS], c, hT, TS).then_inc(S["z_mm"], 1)
                        if c % 2:
                            pe.drain().then_inc(ring_free[c // 2], 1)
                use = [3] * RINGP
                for c in range(8):
                    if c % 2 == 0:
                        arrive(c // 2, l)
                    need("z_evac", l * 38 + 30 + c + 1)
                    proj(bank[c % 2][:, 0:TS], c, hT, TS).then_inc(S["z_mm"], 1)
                    if c % 2:
                        pe.drain().then_inc(ring_free[c // 2], 1)
                        use[c // 2] += 1
                need("lora_in", 3 * (l + 1))
                need("zs_ready", 2 * (l + 1))
                lora = [(W2A2[0:64], LW[0:64]), (W2A2[64:128], LW[64:128]), (VW2[0:32], XVS[0:32]), (G2, SGX)]
                for n in range(16):
                    if n >= 4:
                        need("lora_evac", l * 16 + n - 3)
                    w, x = lora[n // 4]
                    mm(bank[2 + n % 4][:, 0:T], w[:, (n % 4) * P:(n % 4 + 1) * P], x).then_inc(S["lora_mm"], 1)
                need("lora_evac", l * 16 + 16)
                need("kk_sq", l + 1)
                spread(T3, bank[2:6], bones).then_inc(S["kk_ss"], 1)
                need("prep_done", l + 1)
                spread(T1, bank[2:6], bones).then_inc(S["bon_mm"], 1)
                need("bon_done", l + 1)
                for g in range(2 * NRC):
                    n, pr = g // 2, g % 2
                    if g >= 4:
                        need("mat_evac", l * 8 + g - 3)
                    hp = slice(64 * pr, 64 * pr + 64)
                    for j in range(NW):
                        ins = mm(bank[g % 4][:, j * P:(j + 1) * P].rearrange("p (a t) -> p a t", a=2),
                                 BKV[hp, j * NRC + n, 0:2, :].rearrange("p a t -> p (a t)"),
                                 AR[hp, j, :, n * RC:(n + 1) * RC])
                    ins.then_inc(S["mat_mm"], 1)
                for half in range(2):
                    for pr in range(2):
                        hp = slice(64 * pr, 64 * pr + 64)
                        if half:
                            need("l_evac", l * 2 + half)
                        for nn in range(2):
                            n = 2 * half + nn
                            for j in range(NW):
                                c = (nn * NW + j) * RC
                                ins = mm(bank[4 + pr][0:RC, c:c + RC], AR[hp, j, 0, n * RC:(n + 1) * RC],
                                         BKV[hp, j * NRC + n, 0, :])
                    ins.then_inc(S["l_mm"], 1)
                    for lev in range(1, LEV_R):
                        e = (l * 2 + half) * (LEV_R - 1) + lev
                        need("x_in2", e)
                        for m in range(2 * RH):
                            ins = mm(bank[m // 8][0:RC, (m % 8) * RC:(m % 8 + 1) * RC], ML[0:RC, m, :],
                                     XT_[0:RC, 16 * half + m, :])
                        ins.then_inc(S["p_mm"], 1)
                        need("p_evac", e)
                        for m in range(2 * RH):
                            c = slice((m % 8) * RC, (m % 8 + 1) * RC)
                            mm(bank[2 + m // 8][0:RC, c], X_[0:RC, m, :], P1[0:RC, m, :])
                        for m in range(2 * RH):
                            c = slice((m % 8) * RC, (m % 8 + 1) * RC)
                            ins = mm(bank[6 + m // 8][0:RC, c], P1[0:RC, m, :], X_[0:RC, m, :])
                        ins.then_inc(S["x_mm"], 1)
                need("x_done", l + 1)
                for n in range(NRC):
                    for v in range(2):
                        g = 2 * n + v
                        if g >= 4:
                            need("tok_evac", l * 8 + g - 3)
                        for j in range(NW):
                            ins = pe.transpose(bank[g % 4][:, j * P:(j + 1) * P],
                                               BKV[:, j * NRC + n, v:v + 2, :].rearrange("p a t -> p (a t)"), ident)
                        ins.then_inc(S["tok_mm"], 1)
                need("tok_evac", l * 8 + 8)
                for n in range(NRC):
                    e = l * NRC + n + 1
                    c = slice(n * RC, (n + 1) * RC)
                    need("s_evac", e + l)
                    for j in range(NW):
                        mm(bank[4][0:RC, j * P:(j + 1) * P], AR[:, j, 0, c], BD[:, j, :])
                    for h in range(RH):
                        idx = n * RH + (h % 2) * NW + h // 2
                        hc = slice(h * RN, (h + 1) * RN)
                        ins = mm(bank[5][0:RC, hc], M[64:128, idx, 0:64], UV[64:128, n, hc])
                    ins.then_inc(S["y_mm"], 1)
                    need("y_evac", e)
                    for h in range(RH):
                        idx = n * RH + (h % 2) * NW + h // 2
                        hc = slice(h * RN, (h + 1) * RN)
                        ins = mm(bank[6][0:RC, hc], XT_[0:RC, idx, :], YSC[0:RC, hc])
                    ins.then_inc(S["u_mm"], 1)
                    need("u_evac", e)
                    if n:
                        need("o_evac", e - 1)
                    for j in range(NW):
                        mm(bank[7][:, j * P:(j + 1) * P], BKT[:, n, j * P:(j + 1) * P], UV[:, n, j * P:(j + 1) * P])
                    for j in range(NW):
                        oc = slice(j * RC, (j + 1) * RC)
                        mm(bank[0][:, oc], BD[:, j, :], AR[:, j, 1, c], True, False)
                        for hh in range(2):
                            idx = n * RH + hh * NW + j
                            h = 2 * j + hh
                            ins = mm(bank[0][64 * hh:64 * hh + 64, oc], UV[:, n, h * RN:(h + 1) * RN],
                                     M[:, idx, 64:128], False, True)
                    ins.then_inc(S["s_mm"], 1)
                need("o_evac", (l + 1) * NRC)
                for g in range(6):
                    if g >= 2:
                        need("sq_evac", l * 6 + g - 1)
                    for j in range(NW):
                        ins = pe.transpose(bank[g % 2][0:DEC, j * P:(j + 1) * P], SQ[:, g, j, :], ident)
                    ins.then_inc(S["sq_mm"], 1)
                need("so_in", 16 * (l + 1))
                need("sq_evac", l * 6 + 6)
                for j in range(NW):
                    ins = pe.transpose(bank[0][:, j * DEC:(j + 1) * DEC], OT[0:DEC, j * P:(j + 1) * P], ident[0:DEC, 0:DEC])
                ins.then_inc(S["ot_mm"], 1)
                need("so_out", l + 1)
                spread(YR, bank[2:6], bones).then_inc(S["gn_sq"], 1)
                need("gn_m", l + 1)
                spread(at(WORK + 1056, NW, T), bank[2:6], bones).then_inc(S["gn_v"], 1)

                for lev in range(LEV_H + 1):
                    need("lev_x", l * (LEV_H + 1) + lev + 1)
                    for c in range(NHC):
                        if lev:
                            need("att_evac", l * 2 * (LEV_H + 1) + 2 * lev + c - 1)
                        cc = slice(c * HC, (c + 1) * HC)
                        for h in range(NW):
                            if lev == 0:
                                a, b = HG[:, 4 + h, cc], HG[:, h, cc]
                            else:
                                a = b = HV[f"HX{lev % 2}"][:, h, cc]
                            ins = mm(bank[c][:, h * P:(h + 1) * P], a, b)
                        ins.then_inc(S["att_mm"], 1)
                need("att_evac", (l + 1) * 2 * (LEV_H + 1))
                need("kh_done", l + 1)
                for g in range(2 * NHC):
                    c = g // 2
                    cc = slice(c * HC, (c + 1) * HC)
                    for h in range(NW):
                        src = HG[:, 8 + h, cc] if g % 2 == 0 else HV["KH"][:, h, cc]
                        ins = pe.transpose(bank[2 + g][:, h * P:(h + 1) * P], src, ident)
                    ins.then_inc(S["ht_mm"], 1)
                for h in range(NW):
                    ins = pe.transpose(bank[6][0:DEC, h * P:(h + 1) * P], HG[:, 8 + h, SEQ:T], ident)
                ins.then_inc(S["vs_mm"], 1)
                need("ht_evac", (l + 1) * 4)
                for c in range(NHC):
                    cc = slice(c * HC, (c + 1) * HC)
                    need("hs_evac", l * 3 + c + 1)
                    for h in range(NW):
                        hc = slice(h * P, (h + 1) * P)
                        mm(bank[2][:, hc], SH[:, h, :], HV["QH"][:, h, cc], True, False)
                        mm(bank[2][:, hc], VT[:, c, h, :], AT_[:, c, h, :], False, True)
                    for h in range(NW):
                        ins = mm(bank[3][:, h * P:(h + 1) * P], KT[:, c, h, :], VT[:, c, h, :])
                    ins.then_inc(S["hs_mm"], 1)
                    need("ho_evac", l * 2 + c + 1)
                need("vs_evac", l + 1)
                for b in range(DEC):
                    if b >= 2:
                        need("vb_evac", l * DEC + b - 1)
                    mm(bank[4 + b % 2][:, 0:W], ident[0:DEC, b:b + 1].broadcast_to([DEC, P]),
                       VS[0:DEC].rearrange("p a b -> p (a b)")).then_inc(S["vb_mm"], 1)
                need("vb_evac", (l + 1) * DEC)
                for b in range(DEC):
                    for h in range(NW):
                        ins = mm(bank[6][:, h * DEC + b:h * DEC + b + 1], SHS[:, b, h, :], HG[:, h, SEQ + b:SEQ + b + 1])
                ins.then_inc(S["hso_mm"], 1)
                need("hn_sq", l + 1)
                spread(HV["U1"], bank[2:6]).then_inc(S["hn_mm"], 1)

                need("z_evac", 2 + (l + 1) * 38)
                for h in range(NW):
                    ins = mm(bank[0][:, 0:T], ones, SG[:, NW + h, :], h == 0, h == NW - 1)
                ins.then_inc(S["sg_mm"], 1)
                need("sg_mu", l + 1)
                for h in range(NW):
                    ins = mm(bank[1][:, 0:T], ones, VQ[:, h, :], h == 0, h == NW - 1)
                ins.then_inc(S["sg_vm"], 1)
                need("sg_vn", l + 1)
                for c in range(NHC):
                    for h in range(NW):
                        ins = pe.transpose(bank[2 + c][:, h * P:(h + 1) * P], VC[:, h, c * HC:(c + 1) * HC], ident)
                    ins.then_inc(S["sgt_mm"], 1)
                need("sgt_evac", 2 * (l + 1))
                for c in range(NHC):
                    for h in range(NW):
                        hc = slice(h * P, (h + 1) * P)
                        mm(bank[4 + c][:, hc], VT2[:, c, h, :], WST[:, h, :], True, False)
                        mm(bank[4 + c][:, hc], ones[0:1, :], SBR[0:1, h, :], False, True)
                mm(bank[6][:, 0:NW], ones[0:1, :], WST[0:1, :, 0])
                mm(bank[6][:, NW:2 * NW], ones[0:1, :], SBR[0:1, :, 0]).then_inc(S["mx_mm"], 1)

                need("mx_evac", l + 1)
                need("yr_done", 2 * (l + 1))
                with pe.Fori(0, 4) as i:
                    for q in range(6):
                        for s in ((0, 3), (), (1,), (), (2, 4), ())[q]:
                            arrive(s, l, i)
                        pe.wait_ge(S["gate_evac"], i * 6 + (l * 24 + q + 1))
                        proj(bank[q % 2][:, 0:T], q, hT, T).then_inc(S["gate_mm"], 1)
                        pe.wait_ge(S["br_evac"], i * 6 + (l * 24 + q + 1))
                        proj(bank[2 + q % 2][:, 0:T], 6 + q // 2, (YR, YH, YS)[q % 3], T, NW, q % 2)\
                            .then_inc(S["br_mm"], 1)
                        for s in ((), (0,), (), (1, 3), (), (2, 4))[q]:
                            pe.drain().then_inc(ring_free[s], 1)
                use = [8, 8, 8, 8, 7]
                need("br_evac", (l + 1) * 24 + 2)
                need("gate_evac", (l + 1) * 24 + 2)
                need("mg_done", l + 1)
                for m in range(KD):
                    s = m // 2
                    if m % 2 == 0:
                        arrive(s, l)
                    proj(bank[m][:, 0:T], m, MG, T).then_inc(S["wo_mm"], 1)
                    if m % 2:
                        pe.drain().then_inc(ring_free[s], 1)
                        use[s] += 1
                need("ffn_sq", l + 1)
                for k in range(KD):
                    ins = mm(bank[0][:, 0:T], ones, NSQ[:, k, :], k == 0, k == KD - 1)
                ins.then_inc(S["ffn_ss"], 1)
                need("h2_ready", l + 1)
                for n in range(2 * PH):
                    s = (4 + n // 2) % RINGP
                    if n % 2 == 0:
                        arrive(s, l)
                    if n >= 2:
                        need("q_evac", l * 16 + n - 1)
                    proj(bank[n % 2][:, 0:T], 2 * s + n % 2, hT, T).then_inc(S["q_mm"], 1)
                    if n % 2:
                        pe.drain().then_inc(ring_free[s], 1)
                        use[s] += 1
                need("q_evac", l * 16 + 16)
                arrive(2, l)
                use[2] += 1
                assert use == USES, use
                for g in range(12):
                    tc, hp0 = g // 4, 4 * (g % 4)
                    m = P if tc < 2 else DEC
                    if g >= 2:
                        need("sc_evac", l * 12 + g - 1)
                    for k in range(4):
                        ins = mm(bank[4 + g % 2][0:m, k * P:(k + 1) * P], QT[:, hp0 + k, tc * P:tc * P + m],
                                 KEYS[:, hp0 + k, :])
                    ins.then_inc(S["sc_mm"], 1)

                def down(n, b, turn):
                    pe.wait_ge(S["gelu_done"], turn + (l * NK + n + 1))
                    pe.wait_ge(S["dhi_done"], turn + (l * NK + n + 1))
                    for k in range(KD):
                        for q in range(2):
                            mm(bank[b][:, 0:T], DHL[:, b, 0, k * P:(k + 1) * P], HHL[:, q, k, :], k + q == 0, False)
                    pe.wait_ge(S["dlo_done"], turn + (l * NK + n + 5))
                    for k in range(KD):
                        ins = mm(bank[b][:, 0:T], DHL[:, b, 1, k * P:(k + 1) * P], HHL[:, 0, k, :], False, k == KD - 1)
                    ins.then_inc(S["pre_mm"], 1)

                def up(g, b, turn):
                    pe.wait_ge(S["alo_done"], turn + (l * 2 * NGRP + g + 3))
                    pe.wait_ge(S["ulo_done"], turn + (l * 2 * NGRP + g + 3))
                    for k in range(KD):
                        kc = slice(k * P, (k + 1) * P)
                        pe.wait_ge(S["out_evac"], turn * KD + ((l * 2 * NGRP + g) * KD + k + 1))
                        for j in range(GRP):
                            for q, r in ((0, 0), (0, 1), (1, 0)):
                                ins = mm(bank[2 + k % 4][:, 0:T], UHL[:, b, q, j, kc], AHL[:, b, r, j, :],
                                         j + q + r == 0, j == GRP - 1 and q == 1)
                        ins.then_inc(S["out_mm"], 1)

                def gates(n, b, turn):
                    pe.wait_ge(S["g_evac"], turn + (n + 1))
                    pe.wait_ge(S["oh1_ready"], turn + (n + 1))
                    pe.wait_ge(S["oh_ready"], turn + (n + 1))
                    for t in range(TB):
                        for q in range(2):
                            ins = mm(bank[6 + b][:, t * HALF:(t + 1) * HALF], OH1[:, b, t, :],
                                     OH2[:, b, q, t * HALF:(t + 1) * HALF], q == 0, q == 1)
                    ins.then_inc(S["g_mm"], 1)

                need("hlo_done", l + 1)
                with pe.Fori(0, HALF // 2) as i:
                    for b in range(2):
                        down(b, b, i * 2)
                need("e_ready", l + 1)
                need("packed_in", 64 * (l + 1))
                for tc in range(3):
                    m = P if tc < 2 else DEC
                    for k in range(3):
                        ins = pe.transpose(bank[2 + tc][:, k * P:k * P + m], EG[tc][k][0:m].rearrange("p a b -> p (a b)"),
                                           ident[0:m, 0:m])
                ins.then_inc(S["et_mm"], 1)
                pe.sem_inc(ring_free[2], 1)
                for hf in range(2):
                    base = (l * 2 + hf) * NB
                    with pe.Fori(0, NB // 2) as i:
                        for b in range(2):
                            gates(base + b, b, i * 2)
                    gates(base + NB - 1, 0, 0)
                    if hf == 0:
                        with pe.Fori(0, NGRP // 2) as i:
                            for b in range(2):
                                up(b, b, i * 2)
                                down(HALF + 2 * b, 0, i * 4)
                                down(HALF + 2 * b + 1, 1, i * 4)
                    else:
                        with pe.Fori(0, NGRP // 2) as i:
                            for b in range(2):
                                up(NGRP + b, b, i * 2)
            need("mix_sq", DEPTH + 1)
            for k in range(KD):
                ins = mm(bank[0][:, 0:T], ones, NSQ[:, k, :], k == 0, k == KD - 1)
            ins.then_inc(S["mix_ss"], 1)

        @block.scalar
        def _(act):
            def need(name, n):
                act.wait_ge(S[name], n)

            def f(out, in_, fn, **kw):
                return act.activation(out, in_, fn, **kw)

            act.sem_inc(S["z_evac"], 2)
            act.sem_inc(S["gelu_done"], 2)
            act.sem_inc(S["gate_evac"], 2)
            need("par_in", 64)
            need("lb_in", 1)
            f(LBS[:, 2:4], LBS[:, 0:2], ACT.Exp).then_inc(S["lb_exp"], 1)
            for l in range(DEPTH):
                need("mix_ss", l + 1)
                f(NRM[:], bank[0][:, 0:T], ACT.Sqrt, scale=1.0 / D_MODEL, bias=com("eps")).then_inc(S["mix_std"], 1)
                need("h_ready", l + 1)
                need("smalls_in", 16 * NSMALL * (l + 1))
                act.dma_start(d["o_shift"][l], hT[:, :, SEQ - 1:T]).then_inc(S["shift_out"], 16)
                need("xv_mm", l + 1)
                f(XV[0:32, 1:ZR_W], bank[2][0:32, 0:TS], ACT.Copy).then_inc(S["xv_evac"], 1)
                def evac(turns, base, dst, n, fn=ACT.Copy):
                    with act.Fori(0, turns) as i:
                        for b in range(2):
                            act.wait_ge(S["z_mm"], i * 2 + (l * 38 + base + b + 1))
                            f(dst(i * 2 + b), bank[b][:, 0:n], fn).then_inc(S["z_evac"], 1)
                evac(7, 0, lambda c: ZR[:, bass.ds(c, 1), 1:ZR_W].rearrange("p a t -> p (a t)"), TS)
                evac(8, 14, lambda c: HG[:, bass.ds(c, 1), :].rearrange("p a t -> p (a t)"), T)
                evac(4, 30, lambda c: SG[:, bass.ds(c, 1), :].rearrange("p a t -> p (a t)"), T, ACT.Gelu)
                need("zs_ready", 2 * l + 2)
                f(LW[0:64], D[0:64, 12, :], ACT.Tanh).then_inc(S["lora_in"], 1)
                f(LW[64:128], D[64:128, 12, :], ACT.Copy).then_inc(S["lora_in"], 1)
                f(SGX, D[:, 13, :], ACT.Sigmoid).then_inc(S["lora_in"], 1)
                for n in range(16):
                    need("lora_mm", l * 16 + n + 1)
                    j = n % 4
                    src = bank[2 + j][:, 0:T]
                    if n < 12:
                        dst = (SW, AA, VG)[n // 4][:, j, :]
                        b = par(l, ("w0", "a0", "v0")[n // 4], j, j + 1)
                        f(dst, src, ACT.Sigmoid, bias=b).then_inc(S["lora_evac"], 1)
                    else:
                        f(GG[:, j, :], src, ACT.Copy).then_inc(S["lora_evac"], 1)
                need("decay_in", l + 1)
                f(EC, CU, ACT.Exp).then_inc(S["decay_out"], 1)
                f(T1, T2, ACT.Exp).then_inc(S["decay_out"], 1)
                need("decay_out", 3 * l + 2)
                f(T2, CU, ACT.Exp, scale=-1.0).then_inc(S["decay_out"], 1)
                need("kk_ss", l + 1)
                need("decay_out", 3 * l + 3)
                for j in range(NW):
                    ins = f(T3[:, j, :], bank[2 + j][:, 0:T], ACT.Sqrt)
                ins.then_inc(S["kk_std"], 1)
                for half in range(2):
                    for lev in range(1, LEV_R):
                        e = (l * 2 + half) * (LEV_R - 1) + lev
                        need("p_mm", e)
                        for b in range(2):
                            ins = f(P1[0:RC, 8 * b:8 * b + 8].rearrange("p a b -> p (a b)"), bank[b][0:RC, :], ACT.Copy)
                        ins.then_inc(S["p_evac"], 1)
                for n in range(NRC):
                    for v in range(2):
                        need("tok_mm", l * 8 + 2 * n + v + 1)
                        if v == 0:
                            f(BKT[:, n], bank[2 * n % 4][:, :], ACT.Copy).then_inc(S["tok_evac"], 1)
                        else:
                            f(UV[64:128, n], bank[(2 * n + 1) % 4][64:128, :], ACT.Copy).then_inc(S["tok_evac"], 1)
                for n in range(NRC):
                    e = l * NRC + n + 1
                    need("u_mm", e)
                    f(UV[0:64, n], bank[6][0:64, :], ACT.Copy).then_inc(S["u_evac"], 1)
                    need("s_mm", e)
                    f(YR[:, :, n * RC:(n + 1) * RC], bank[0][:, 0:NW * RC].rearrange("p (a t) -> p a t", a=NW),
                      ACT.Copy).then_inc(S["o_evac"], 1)
                need("s_evac", (l + 1) * (NRC + 1))
                act.dma_start(d["o_rp"][l], BD).then_inc(S["bd_out"], 16)
                act.dma_start(SR[0:64], d["rs"][l]).then_inc(S["sr_in"], 16)
                for g in range(6):
                    need("sq_mm", l * 6 + g + 1)
                    f(TQ[0:DEC, g], bank[g % 2][0:DEC, :], ACT.Copy).then_inc(S["sq_evac"], 1)
                need("sq_evac", l * 6 + 6)
                for g in range(6):
                    act.dma_start(RQ[0:64, g], TQ[0:DEC, g]).then_inc(S["rq_in"], 16)
                need("sr_done", l + 1)
                act.dma_start(OT[0:DEC], OS[0:64]).then_inc(S["so_in"], 16)
                act.dma_start(d["o_rs"][l], SR[0:64]).then_inc(S["sr_out"], 16)
                need("ot_mm", l + 1)
                f(YR[:, :, SEQ:T], bank[0][:, 0:NW * DEC].rearrange("p (a t) -> p a t", a=NW), ACT.Copy)\
                    .then_inc(S["so_out"], 1)
                need("gn_v", l + 1)
                for j in range(NW):
                    ins = f(T3[:, j, :], bank[2 + j][:, 0:T], ACT.Sqrt, scale=1.0 / RN, bias=com("leps"))
                ins.then_inc(S["gn_std"], 1)
                need("hg_in", l + 1)
                act.dma_start(SHS, d["hs"][l]).then_inc(S["shs_in"], 16)
                f(HV["U1"], HG[:, 0:4, :], ACT.Sigmoid).then_inc(S["hg_sig"], 1)
                f(HV["FF"], HG[:, 4:8, :], ACT.Sigmoid).then_inc(S["hg_sig"], 1)
                f(HV["U2"], HG[:, 12:16, :], ACT.Sigmoid).then_inc(S["hg_sig"], 1)
                need("f_ready", l + 1)
                f(HV["BC"], HV["U1"], ACT.Ln).then_inc(S["f_ln"], 1)
                f(HV["KH"], HV["U2"], ACT.Ln).then_inc(S["f_ln"], 1)
                need("b_ready", l + 1)
                f(HV["EB"], HV["BC"], ACT.Exp).then_inc(S["eb_done"], 1)
                for lev in range(1, LEV_H + 1):
                    need("lev_in", l * LEV_H + lev)
                    hx = HV[f"HX{lev % 2}"]
                    f(hx[:, :, 0:SEQ], hx[:, :, 0:SEQ], ACT.Exp).then_inc(S["lev_exp"], 1)
                need("kh_in", l + 1)
                f(HV["KH"][:, :, 0:SEQ], HV["KH"][:, :, 0:SEQ], ACT.Exp).then_inc(S["kh_exp"], 1)
                for g in range(4):
                    need("ht_mm", l * 4 + g + 1)
                    f((VT, KT)[g % 2][:, g // 2].rearrange("p a b -> p (a b)"), bank[2 + g][:, :], ACT.Copy)\
                        .then_inc(S["ht_evac"], 1)
                need("vs_mm", l + 1)
                f(VS[0:DEC].rearrange("p a b -> p (a b)"), bank[6][0:DEC, :], ACT.Copy).then_inc(S["vs_evac"], 1)
                for c in range(NHC):
                    need("hs_mm", l * 2 + c + 1)
                    f(YH[:, :, c * HC:(c + 1) * HC], bank[2][:, :].rearrange("p (a t) -> p a t", a=NW),
                      ACT.Copy).then_inc(S["ho_evac"], 1)
                need("hs_evac", l * 3 + 3)
                act.dma_start(d["o_hp"][l], SH).then_inc(S["hp_out"], 16)
                need("hso_mm", l + 1)
                f(YH[:, :, SEQ:T], bank[6][:, 0:NW * DEC].rearrange("p (a t) -> p a t", a=NW), ACT.Copy)\
                    .then_inc(S["hso_evac"], 1)
                act.dma_start(d["o_hs"][l], SHS).then_inc(S["h_out"], 16)
                need("hn_mm", l + 1)
                for j in range(NW):
                    ins = f(HV["U2"][:, j, :], bank[2 + j][:, 0:T], ACT.Sqrt, scale=1.0 / P, bias=com("eps"))
                ins.then_inc(S["hn_std"], 1)
                need("sg_vm", l + 1)
                f(NRM[:], bank[1][:, 0:T], ACT.Sqrt, scale=1.0 / W, bias=com("eps")).then_inc(S["sg_std"], 1)
                need("sg_vn", l + 1)
                act.dma_start(d["o_sg"][l], VC[:, :, SEQ:T]).then_inc(S["sgo_out"], 16)
                for c in range(NHC):
                    need("sgt_mm", l * 2 + c + 1)
                    f(VT2[:, c].rearrange("p a b -> p (a b)"), bank[2 + c][:, :], ACT.Copy).then_inc(S["sgt_evac"], 1)
                with act.Fori(0, 12) as i:
                    for b in range(2):
                        act.wait_ge(S["gate_mm"], i * 2 + (l * 24 + b + 1))
                        act.wait_ge(S["br_evac"], i * 2 + (l * 24 + b + 1))
                        f(GS[:, b, :], bank[b][:, 0:T], ACT.Sigmoid).then_inc(S["gate_evac"], 1)
                need("ffn_ss", l + 1)
                f(NRM[:], bank[0][:, 0:T], ACT.Sqrt, scale=1.0 / D_MODEL, bias=com("eps")).then_inc(S["ffn_std"], 1)
                for n in range(16):
                    need("q_mm", l * 16 + n + 1)
                    f(QT[:, n, :], bank[n % 2][:, 0:T], ACT.Copy).then_inc(S["q_evac"], 1)
                for n in range(12):
                    tc, m = n // 4, P if n < 8 else DEC
                    need("sc_mm", l * 12 + n + 1)
                    f(SC[tc][0:m, (n % 4) * 4:(n % 4) * 4 + 4].rearrange("p a b -> p (a b)"),
                      bank[4 + n % 2][0:m, :], ACT.Copy).then_inc(S["sc_evac"], 1)
                need("sc_evac", l * 12 + 12)
                act.dma_start(PKR[0:64], SC[2][0:DEC]).then_inc(S["packed_in"], 16)

                def down_hi(n, b, slot, turn, on):
                    act.wait_ge(dn_in[slot], (on + 1) * 16)
                    act.wait_ge(S["pre_mm"], turn + (l * NK + n + 1))
                    f(DHL[:, b, 0], ring[:, RAWD + slot].rearrange("p k e -> p (k e)"), ACT.Copy)\
                        .then_inc(S["dhi_done"], 1)

                def gelu(n, b, i, per, first):
                    act.wait_ge(S["pre_mm"], i * per + (l * NK + n + 3))
                    f(ACTS[:, bass.ds(i * per + (n - first), 1), :].rearrange("p a t -> p (a t)"), bank[b][:, 0:T],
                      ACT.Gelu).then_inc(S["gelu_done"], 1)

                def up_hi(g, b, turn, half_g, on):
                    act.wait_ge(up_in[b], (on + 1) * 16)
                    act.wait_ge(S["out_mm"], turn * KD + (l * 2 * NGRP + g + 1) * KD)
                    f(UHL[:, b, 0].rearrange("p a m -> p (a m)"),
                      ring[:, RAWU + 2 * b:RAWU + 2 * b + 2].rearrange("p s k m -> p (s k m)"), ACT.Copy)\
                        .then_inc(S["uhi_done"], 1)
                    f(AHL[:, b, 0], ACTS[:, bass.ds(turn * GRP + half_g * GRP, GRP), :], ACT.Copy)\
                        .then_inc(S["ahi_done"], 1)

                n4 = l * (NK // 4)
                down_hi(0, 0, 0, 0, n4)
                with act.Fori(0, HALF // 4 - 1) as i:
                    for b in range(4):
                        down_hi(b + 1, (b + 1) % 2, (b + 1) % 4, i * 4, i + (n4 + (b + 1) // 4))
                        gelu(b, b % 2, i, 4, 0)
                for n in range(HALF - 4, HALF):
                    if n + 1 < HALF:
                        down_hi(n + 1, (n + 1) % 2, (n + 1) % 4, 0, n4 + (n + 1) // 4)
                    gelu(n, n % 2, 0, 4, 0)
                for tc in range(3):
                    need("sm_in", l * 3 + tc + 1)
                    ga = EG[tc][2] if tc < 2 else SGA[0:64]
                    f(ga, ga, ACT.Exp).then_inc(S["sm_exp"], 1)
                need("gs_done", l + 1)
                for k, src in enumerate((SE1, SE2, SGA)):
                    act.dma_start(EG[2][k][0:DEC].rearrange("p a b -> p (a b)"), src[0:64]).then_inc(S["packed_in"], 16)
                for hf in range(2):
                    need("g_evac", 2 + (l * 2 + hf + 1) * NB)

                    def group(g, b, turn, i, more=True):
                        down0 = HALF + 2 * g
                        if hf == 0:
                            for c in range(2):
                                down_hi(down0 + c, c, (2 * b + c) % 4, turn * 2, i + (n4 + (down0 + c) // 4))
                        if more:
                            up_hi(hf * NGRP + g + 1, 1 - b, turn, g + 1, i + (l * NGRP + hf * (NGRP // 2) + (g + 1) // 2))
                        if hf == 0:
                            act.wait_ge(S["alo_done"], turn + (l * 2 * NGRP + g + 3))
                            for c in range(2):
                                gelu(down0 + c, c, i, 4, HALF)

                    up_hi(hf * NGRP, 0, 0, 0, l * NGRP + hf * (NGRP // 2))
                    with act.Fori(0, NGRP // 2 - 1) as i:
                        for b in range(2):
                            group(b, b, i * 2, i)
                    group(NGRP - 2, 0, 0, 0)
                    group(NGRP - 1, 1, 0, 0, False)
            need("mix_ss", DEPTH + 1)
            f(NRM[:], bank[0][:, 0:T], ACT.Sqrt, scale=1.0 / D_MODEL, bias=com("eps")).then_inc(S["mix_std"], 1)
            need("h_ready", DEPTH + 1)
            act.dma_start(d["o_y"], hT[:, :, 0:T]).then_inc(S["y_out"], 16)
            for n in ("shift_out", "bd_out", "sr_out", "hp_out", "h_out", "sgo_out"):
                need(n, 16 * DEPTH)
            need("y_out", 16)

        @block.vector
        def _(dve):
            steps = [0]

            def need(name, n):
                dve.wait_ge(S[name], n)

            def step(ins):
                steps[0] += 1
                ins.then_inc(S["dve_step"], 1)
                dve.wait_ge(S["dve_step"], steps[0])

            def done(ins, name, n):
                ins.then_inc(S[name], 1)
                dve.wait_ge(S[name], n)

            def tt(out, a, b, op):
                return dve.tensor_tensor(out, a, b, op)

            def ts(out, a, s1, op0, s2=None, op1=ALU.bypass):
                if s2 is None:
                    return dve.tensor_scalar(out, a, s1, None, op0)
                return dve.tensor_scalar(out, a, s1, s2, op0, op1)

            def stt(out, a, s, b, op0, op1):
                return dve.scalar_tensor_tensor(out=out, in0=a, scalar=s, in1=b, op0=op0, op1=op1)

            def tiled(v, n, w=T):
                return over(v, w)

            def norm(l, g, std_name, std_n, ready, ready_n, sq_name, sq_n):
                done(tt(NSQ, xT[:], xT[:], ALU.mult), sq_name, sq_n)
                need(std_name, std_n)
                step(dve.reciprocal(NRM[:], NRM[:]))
                for k in range(KD):
                    ins = stt(hT[:, k, 0:T], xT[:, k, :], g(k), NRM[:], ALU.mult, ALU.mult)
                done(ins, ready, ready_n)

            dve.sem_inc(S["br_evac"], 2)
            dve.sem_inc(S["mg_add"], 1)
            dve.sem_inc(S["out_evac"], 4)
            dve.sem_inc(S["alo_done"], 2)
            dve.sem_inc(S["g_evac"], 2)
            need("par_in", 64)
            step(tt(LBS[:, 4], com("lb0"), com("lb1"), ALU.max))
            tt(LBS[:, 0], com("lb0"), LBS[:, 4], ALU.subtract)
            done(tt(LBS[:, 1], com("lb1"), LBS[:, 4], ALU.subtract), "lb_in", 1)
            need("lb_exp", 1)
            step(tt(LBS[:, 4], LBS[:, 2], LBS[:, 3], ALU.add))
            step(dve.reciprocal(LBS[:, 4], LBS[:, 4]))
            step(tt(LBS[:, 2:4], LBS[:, 2:4], rows(LBS[:, 4], 2), ALU.mult))
            step(tt(LBS[:, 5], LBS[:, 2], LBS[:, 3], ALU.add))
            tt(LBS[:, 4], LBS[:, 2], LBS[:, 2], ALU.subtract)
            step(tt(LBS[:, 5], LBS[:, 5], LBS[:, 2], ALU.subtract))
            step(ts(LBS[:, 4:6], LBS[:, 4:6], 0.0, ALU.max, 1.0, ALU.min))
            step(dve.memset(V1[:], 0.0))

            for l in range(DEPTH):
                norm(l, lambda k: par(l, "mix_g", k, k + 1), "mix_std", l + 1, "h_ready", l + 1, "mix_sq", l + 1)
                need("smalls_in", 16 * NSMALL * (l + 1))
                dve.memset(ZR[:, :, 0], 0.0)
                dve.memset(XV[0:32, 0:1], 0.0)
                step(tt(WST, WST, rows(cm("triu"), NW), ALU.mult))
                need("xv_evac", l + 1)
                tt(XVS[0:32, 0:SEQ], XV[0:32, 0:SEQ], XV[0:32, 1:SEQ + 1], ALU.subtract)
                step(tt(XVS[0:32, SEQ:T], XV[0:32, T + 1:ZR_W], XV[0:32, SEQ + 1:T + 1], ALU.subtract))
                done(stt(XVS[0:32], XVS[0:32], par(l, "vmu")[0:32], XV[0:32, 1:T + 1], ALU.mult, ALU.add),
                     "zs_ready", 2 * l + 1)
                need("z_evac", 2 + l * 38 + RT)
                tt(D[:, :, 0:SEQ], ZR[:, :, 0:SEQ], ZR[:, :, 1:SEQ + 1], ALU.subtract)
                step(tt(D[:, :, SEQ:T], ZR[:, :, T + 1:ZR_W], ZR[:, :, SEQ + 1:T + 1], ALU.subtract))
                step(tt(D, D, over(par(l, "mu"), T), ALU.mult))
                done(tt(D, D, ZR[:, :, 1:T + 1], ALU.add), "zs_ready", 2 * l + 2)
                R, K, V = D[:, 0:4, :], D[:, 4:8, :], D[:, 8:12, :]
                need("lora_evac", l * 16 + 4)
                step(ts(SW, SW, -float(np.exp(-0.5)), ALU.mult))
                for j in range(NW):
                    ins = dve.tensor_tensor_scan(CU[:, j, :], cm("rscan"), SW[:, j, :], 0.0, ALU.mult, ALU.add)
                step(ins)
                done(tt(T2, CU, SW, ALU.subtract), "decay_in", l + 1)
                need("lora_evac", l * 16 + 12)
                step(ts(VG, VG, par(l, "on"), ALU.mult))
                step(ts(V1[:], V1[:], par(l, "on"), ALU.mult))
                for j in range(NW):
                    ins = stt(V1[:, j], V[:, j], par(l, "off"), V1[:, j], ALU.mult, ALU.add)
                step(ins)
                step(tt(KK, V1[:], V, ALU.subtract))
                step(tt(KK, KK, VG, ALU.mult))
                step(tt(V, V, KK, ALU.add))

                def chunked(x):
                    return x[:, :, 0:SEQ].rearrange("p j (n t) -> p j n t", t=RC)

                def slot(g):
                    return BKV[:, :, g, :].rearrange("p (j n) t -> p j n t", j=NW)

                dve.tensor_copy(slot(2), chunked(V))
                step(tt(KK, K, over(par(l, "kk"), T), ALU.mult))
                done(tt(T3, KK, KK, ALU.mult), "kk_sq", l + 1)
                need("kk_std", l + 1)
                step(ts(T3, T3, 1e-12, ALU.max))
                step(dve.reciprocal(T3, T3))
                step(tt(KK, KK, T3, ALU.mult))
                need("decay_out", 3 * l + 3)
                tt(AR[:, :, 1, :], R, EC, ALU.mult)
                step(ts(T3, KK, -1.0, ALU.mult))
                step(tt(KK, KK, AA, ALU.mult))
                step(tt(AR[:, :, 0, :], T3, T1, ALU.mult))
                tt(slot(0), chunked(KK), chunked(T2), ALU.mult)
                step(ts(AA, AA, -1.0, ALU.add))
                step(tt(AA, AA, over(par(l, "ka"), T), ALU.mult))
                for j in range(NW):
                    ins = stt(K[:, j], AA[:, j], 1.0, K[:, j], ALU.add, ALU.mult)
                step(ins)
                tt(slot(1), chunked(K), chunked(T2), ALU.mult)
                step(tt(T1, R, K, ALU.mult))
                tt(T1, T1, over(par(l, "rk"), T), ALU.mult).then_inc(S["prep_done"], 1)
                for g, src in enumerate((T3, KK, K, R, EC, V)):
                    ins = dve.tensor_copy(SQ[:, g], src[:, :, SEQ:T])
                step(ins)
                need("bon_mm", l + 1)
                for j in range(NW):
                    ins = tt(BO[:, j, :], bank[2 + j][:, 0:T], V[:, j, :], ALU.mult)
                done(ins, "bon_done", l + 1)
                for g in range(2 * NRC):
                    need("mat_mm", l * 8 + g + 1)
                    ins = tt(M[:, 4 * g:4 * g + 4, :], bank[g % 4][:, :].rearrange("p (a b) -> p a b", a=NW),
                             rows(cm("rw"), NW), ALU.mult)
                    ins.then_inc(S["mat_evac"], 1)
                need("mat_evac", l * 8 + 8)
                for half in range(2):
                    need("l_mm", l * 2 + half + 1)
                    Lv = L_[0:RC].rearrange("p (n q j) s -> p n q (j s)", n=2, q=2)
                    for pr in range(2):
                        ins = tt(Lv[:, :, pr].rearrange("p n (j s) -> p n j s", j=NW),
                                 bank[4 + pr][0:RC, :].rearrange("p (n j s) -> p n j s", n=2, j=NW),
                                 cm("low")[0:RC].rearrange("p (a b s) -> p a b s", a=1, b=1)
                                 .broadcast_to([RC, 2, NW, RC]), ALU.mult)
                    done(ins, "l_evac", l * 2 + half + 1)
                    XH = XT_[0:RC, 16 * half:16 * half + 16, :]
                    I16 = rows(ident[0:RC, 0:RC], 16)
                    step(tt(X_[0:RC], L_[0:RC], rows(cm("lev", 0, RC)[0:RC], 16), ALU.mult))
                    tt(X_[0:RC], X_[0:RC], I16, ALU.add)
                    step(tt(XH, M[0:RC, 16 * half:16 * half + 16, 0:RC], rows(cm("n0")[0:RC], 16), ALU.mult))
                    step(tt(XH, XH, I16, ALU.add))
                    for lev in range(1, LEV_R):
                        e = (l * 2 + half) * (LEV_R - 1) + lev
                        done(tt(ML[0:RC], L_[0:RC], rows(cm("lev", RC * lev, RC)[0:RC], 16), ALU.mult), "x_in2", e)
                        need("x_mm", e)
                        for b in range(2):
                            c = slice(8 * b, 8 * b + 8)
                            xh = XT_[0:RC, 16 * half + 8 * b:16 * half + 8 * b + 8, :]
                            tt(xh, xh, bank[2 + b][0:RC, :].rearrange("p (a b) -> p a b", a=8), ALU.add)
                            ins = tt(X_[0:RC, c], X_[0:RC, c], bank[6 + b][0:RC, :].rearrange("p (a b) -> p a b", a=8),
                                     ALU.add)
                        step(ins)
                ins = dve.memset(BD, 0.0)
                done(ins, "s_evac", l * (NRC + 1) + 1)
                dve.memset(TT_, 0.0).then_inc(S["x_done"], 1)
                for n in range(NRC):
                    e = l * NRC + n + 1
                    need("y_mm", e)
                    step(dve.tensor_copy(YSC[0:RC], bank[4][0:RC, :]))
                    done(tt(YSC[0:RC], YSC[0:RC], bank[5][0:RC, :], ALU.add), "y_evac", e)
                    need("s_mm", e)
                    step(tt(TT_.rearrange("p (a b) -> p a b", a=NW), bank[7][:, :].rearrange("p (a b) -> p a b", a=NW),
                            rows(bones, NW), ALU.mult))
                    step(tt(BD, BD, TT_.rearrange("p (a b) -> p a b", a=NW), ALU.add))
                    done(tt(BD, BD, over(EC[:, :, (n + 1) * RC - 1], P), ALU.mult), "s_evac", e + l + 1)
                need("sr_in", 16 * (l + 1))
                need("rq_in", 96 * (l + 1))
                nkk, kka, k2, r, w, v = (RQ[0:64, g] for g in range(6))
                S64, T64 = SR[0:64], TR[0:64]
                step(tt(T64, S64, rows(nkk, RN), ALU.mult))
                step(dve.tensor_reduce(SA[0:64], T64, AX.X, ALU.add))
                step(tt(S64, S64, rows(w, RN), ALU.mult))
                step(tt(T64, over(SA[0:64], RN), rows(kka, RN), ALU.mult))
                step(tt(S64, S64, T64, ALU.add))
                step(tt(T64, over(v, RN), rows(k2, RN), ALU.mult))
                step(tt(S64, S64, T64, ALU.add))
                step(tt(T64, S64, rows(r, RN), ALU.mult))
                done(dve.tensor_reduce(OS[0:64], T64, AX.X, ALU.add), "sr_done", l + 1)
                need("gn_sq", l + 1)
                for j in range(NW):
                    ins = stt(YR[:, j], bank[2 + j][:, 0:T], -1.0 / RN, YR[:, j], ALU.mult, ALU.add)
                step(ins)
                done(tt(at(WORK + 1056, NW, T), YR, YR, ALU.mult), "gn_m", l + 1)
                need("gn_std", l + 1)
                step(dve.reciprocal(T3, T3))
                step(tt(YR, YR, T3, ALU.mult))
                step(tt(YR, YR, over(par(l, "lg"), T), ALU.mult))
                step(tt(YR, YR, over(par(l, "lb"), T), ALU.add))
                step(tt(YR, YR, BO, ALU.add))
                done(tt(YR, YR, GG, ALU.mult), "yr_done", 2 * l + 1)
                need("z_evac", 2 + (l + 1) * 38)
                need("sr_out", 16 * (l + 1))
                need("bd_out", 16 * (l + 1))
                done(dve.memset(HV["HX0"], 0.0), "hg_in", l + 1)
                need("hg_sig", 3 * (l + 1))
                FF, U1, U2, BC, EB, KH, QH = (HV[n] for n in ("FF", "U1", "U2", "BC", "EB", "KH", "QH"))
                tt(HG[:, 0:4, :], HG[:, 0:4, :], U1, ALU.mult)
                tt(HG[:, 12:16, :], HG[:, 12:16, :], U2, ALU.mult)
                lbl = LBS[:, 4 + l]
                step(ts(SC8[:, 0:4], lbl, -1.0, ALU.mult, 1.0, ALU.add))
                step(tt(FF, FF, over(SC8[:, 0:4], T), ALU.mult))
                step(tt(FF, FF, over(lbl, T), ALU.add))
                ts(HG[:, 4:8, :], FF, -1.0, ALU.mult, 1.0, ALU.add)
                step(ts(FF, FF, 1e-30, ALU.max))
                ts(U1, FF, 2.0 ** -60, ALU.max)
                done(ts(U2, FF, 2.0 ** 60, ALU.mult, 1.0, ALU.min), "f_ready", l + 1)
                need("f_ln", 2 * (l + 1))
                step(tt(U1, BC, KH, ALU.add))
                for j in range(NW):
                    ins = dve.tensor_tensor_scan(BC[:, j, :], cm("hscan"), U1[:, j, :], 0.0, ALU.mult, ALU.add)
                done(ins, "b_ready", l + 1)
                need("eb_done", l + 1)
                tt(QH, HG[:, 0:4, :], EB, ALU.mult).then_inc(S["lev_x"], 1)
                for c in range(NHC):
                    cc = slice(c * HC, (c + 1) * HC)
                    ins = tt(KH[:, :, cc], over(BC[:, :, (c + 1) * HC - 1], HC), BC[:, :, cc], ALU.subtract)
                ins.then_inc(S["kh_in"], 1)

                def cut(ap, b):
                    return ap.rearrange("p a (n b) -> p a n b", b=b)

                def att(lev):
                    for c in range(NHC):
                        e = l * 2 * (LEV_H + 1) + 2 * lev + c + 1
                        need("att_mm", e)
                        src = bank[c][:, :].rearrange("p (a b) -> p a b", a=NW)
                        if lev == 0:
                            done(tt(AT_[:, c], src, rows(cm("hg", P * LEV_H, P), NW), ALU.mult), "att_evac", e)
                        else:
                            step(tt(T5, src, rows(cm("hg", P * (lev - 1), P), NW), ALU.mult))
                            done(tt(AT_[:, c], AT_[:, c], T5, ALU.add), "att_evac", e)

                for lev in range(1, LEV_H + 1):
                    hx = HV[f"HX{lev % 2}"]
                    b = 1 << (lev - 1)
                    for j in range(NW):
                        bc = BC[:, j, 0:SEQ].rearrange("p (n b) -> p n b", b=2 * b)
                        hh = hx[:, j, 0:SEQ].rearrange("p (n b) -> p n b", b=2 * b)
                        ref = bc[:, :, b - 1:b].broadcast_to([P, SEQ // (2 * b), b])
                        tt(hh[:, :, 0:b], ref, bc[:, :, 0:b], ALU.subtract)
                        ins = tt(hh[:, :, b:2 * b], bc[:, :, b:2 * b], ref, ALU.subtract)
                    ins.then_inc(S["lev_in"], 1)
                    att(lev - 1)
                    need("lev_exp", l * LEV_H + lev)
                    for j in range(NW):
                        hh = hx[:, j, 0:SEQ].rearrange("p (n b) -> p n b", b=2 * b)
                        kk_ = HG[:, 4 + j, 0:SEQ].rearrange("p (n b) -> p n b", b=2 * b)
                        qq = HG[:, j, 0:SEQ].rearrange("p (n b) -> p n b", b=2 * b)
                        tt(hh[:, :, 0:b], hh[:, :, 0:b], kk_[:, :, 0:b], ALU.mult)
                        ins = tt(hh[:, :, b:2 * b], hh[:, :, b:2 * b], qq[:, :, b:2 * b], ALU.mult)
                    ins.then_inc(S["lev_x"], 1)
                att(LEV_H)
                need("kh_exp", l + 1)
                done(tt(KH[:, :, 0:SEQ], KH[:, :, 0:SEQ], HG[:, 4:8, 0:SEQ], ALU.mult), "kh_done", l + 1)
                done(dve.memset(SH, 0.0), "hs_evac", 3 * l + 1)
                for c in range(NHC):
                    need("hs_mm", 2 * l + c + 1)
                    step(tt(SH, SH, over(EB[:, :, (c + 1) * HC - 1], P), ALU.mult))
                    done(tt(SH, SH, bank[3][:, :].rearrange("p (a b) -> p a b", a=NW), ALU.add), "hs_evac", 3 * l + c + 2)
                need("shs_in", 16 * (l + 1))
                for b in range(DEC):
                    need("vb_mm", l * DEC + b + 1)
                    tt(SHS[:, b], SHS[:, b], over(EB[:, :, SEQ + b], P), ALU.mult)
                    step(tt(T5, bank[4 + b % 2][:, :].rearrange("p (a b) -> p a b", a=NW),
                            over(HG[:, 4:8, SEQ + b], P), ALU.mult))
                    done(tt(SHS[:, b], SHS[:, b], T5, ALU.add), "vb_evac", l * DEC + b + 1)
                need("ho_evac", 2 * (l + 1))
                need("hso_evac", l + 1)
                done(tt(U1, YH, YH, ALU.mult), "hn_sq", l + 1)
                need("hn_std", l + 1)
                step(dve.reciprocal(U2, U2))
                step(tt(YH, YH, U2, ALU.mult))
                step(tt(YH, YH, over(par(l, "hg"), T), ALU.mult))
                done(tt(YH, YH, HG[:, 12:16, :], ALU.mult), "yr_done", 2 * l + 2)
                need("sg_mm", l + 1)
                for j in range(NW):
                    ins = stt(VC[:, j], bank[0][:, 0:T], -1.0 / W, SG[:, NW + j], ALU.mult, ALU.add)
                step(ins)
                done(tt(VQ, VC, VC, ALU.mult), "sg_mu", l + 1)
                need("sg_std", l + 1)
                step(dve.reciprocal(NRM[:], NRM[:]))
                step(tt(VC, VC, rows(NRM[:], NW), ALU.mult))
                step(tt(VC, VC, over(par(l, "sg"), T), ALU.mult))
                done(tt(VC, VC, over(par(l, "sb"), T), ALU.add), "sg_vn", l + 1)
                need("mx_mm", l + 1)
                for c in range(NHC):
                    cc = slice(c * HC, (c + 1) * HC)
                    tt(YS[:, :, cc], bank[4 + c][:, :].rearrange("p (a b) -> p a b", a=NW), SG[:, 0:4, cc], ALU.mult)
                step(dve.tensor_copy(SC8, bank[6][:, 0:8]))
                step(tt(YS[:, :, SEQ:T], VC[:, :, SEQ:T], over(SC8[:, 0:4], DEC), ALU.mult))
                step(tt(YS[:, :, SEQ:T], YS[:, :, SEQ:T], over(SC8[:, 4:8], DEC), ALU.add))
                done(tt(YS[:, :, SEQ:T], YS[:, :, SEQ:T], SG[:, 0:4, SEQ:T], ALU.mult), "mx_evac", l + 1)
                with dve.Fori(0, 4) as i:
                    for q in range(6):
                        dve.wait_ge(S["gate_evac"], i * 6 + (l * 24 + q + 3))
                        dve.wait_ge(S["br_mm"], i * 6 + (l * 24 + q + 1))
                        mg = MG[:, bass.ds(i * 2 + q // 3, 1), :].rearrange("p a t -> p (a t)")
                        src = bank[2 + q % 2][:, 0:T]
                        if q % 3 == 0:
                            tt(mg, src, GS[:, q % 2, :], ALU.mult).then_inc(S["br_evac"], 1)
                        else:
                            dve.wait_ge(S["mg_add"], i * 4 + (l * 16 + q - 1 - q // 3 + 1))
                            tt(PR, src, GS[:, q % 2, :], ALU.mult).then_inc(S["br_evac"], 1)
                            dve.wait_ge(S["br_evac"], i * 6 + (l * 24 + q + 3))
                            tt(mg, mg, PR, ALU.add).then_inc(S["mg_add"], 1)
                need("br_evac", 2 + 24 * (l + 1))
                need("mg_add", 1 + 16 * (l + 1))
                done(dve.memset(PR, 0.0), "mg_done", l + 1)
                for m in range(KD):
                    need("wo_mm", l * 8 + m + 1)
                    ins = tt(xT[:, m, :], xT[:, m, :], bank[m][:, 0:T], ALU.add)
                    ins.then_inc(S["wo_evac"], 1)
                need("wo_evac", 8 * (l + 1))
                for n in ("shift_out", "sgo_out", "hp_out", "h_out"):
                    need(n, 16 * (l + 1))
                norm(l, lambda k: par(l, "ffn_g", k, k + 1), "ffn_std", l + 1, "h2_ready", l + 1, "ffn_sq", l + 1)
                step(dve.tensor_copy(HHL[:, 0], hT[:, :, 0:T]))
                done(tt(HHL[:, 1], hT[:, :, 0:T], HHL[:, 0].bitcast(F32), ALU.subtract), "hlo_done", l + 1)
                for tc in range(3):
                    m, nh = (P, PH) if tc < 2 else (64, 1)
                    if tc < 2:
                        need("sc_evac", l * 12 + 4 * tc + 4)
                        e1, e2, ga = (EG[tc][k] for k in range(3))
                    else:
                        need("packed_in", 64 * l + 16)
                        e1, e2, ga = (v[0:64].rearrange("p (a b) -> p a b", a=1) for v in (SE1, SE2, SGA))
                    sv, si, cv, ci = SV[0:m, 0:nh], SI[0:m, 0:nh], CV[0:m, 0:nh], CI[0:m, 0:nh]
                    for h in range(nh):
                        for p in range(2):
                            top16(dve, step, SC[tc][:, 2 * h + p] if tc < 2 else PKR[0:64, p],
                                  sv[:, h, p], si[:, h, p].bitcast(U32))
                    step(dve.tensor_copy(si, si.bitcast(U32)))
                    for h in range(nh):
                        step(tt(COMB[0:m, h], over(sv[:, h, 0], TOPK), rows(sv[:, h, 1], TOPK), ALU.add))
                        top16(dve, step, COMB[0:m, h].rearrange("p a b -> p (a b)"), cv[:, h], ci[:, h].bitcast(U32))
                    ts(e1.bitcast(U32), ci.bitcast(U32), 4, ALU.logical_shift_right)
                    step(ts(e2.bitcast(U32), ci.bitcast(U32), 15, ALU.bitwise_and))
                    dve.tensor_copy(e1, e1.bitcast(U32))
                    step(dve.tensor_copy(e2, e2.bitcast(U32)))
                    oh = COMB[0:m, 0:nh].rearrange("p a b c -> p (a b) c")
                    for p, e in enumerate((e1, e2)):
                        ef = e.rearrange("p a b -> p (a b)")
                        step(tt(oh, over(ef, TOPK), rows(cp("iota16")[0:m], nh * TOPK), ALU.is_equal))
                        for h in range(nh):
                            hr = slice(h * TOPK, (h + 1) * TOPK)
                            ins = tt(oh[:, hr], oh[:, hr], rows(si[:, h, p], TOPK), ALU.mult)
                        step(ins)
                        step(dve.tensor_reduce(ef, oh, AX.X, ALU.add))
                    done(tt(ga, cv, cv[:, :, 0:1].broadcast_to([m, nh, TOPK]), ALU.subtract), "sm_in", l * 3 + tc + 1)
                need("sm_exp", l * 3 + 3)
                for tc in (2, 0, 1):
                    m, nh = (P, PH) if tc < 2 else (64, 1)
                    ga = EG[tc][2] if tc < 2 else SGA[0:64].rearrange("p (a b) -> p a b", a=1)
                    step(dve.tensor_reduce(SM[0:m, 0, 0:nh], ga, AX.X, ALU.add))
                    step(dve.reciprocal(SM[0:m, 1, 0:nh], SM[0:m, 0, 0:nh]))
                    ins = tt(ga, ga, over(SM[0:m, 1, 0:nh], TOPK), ALU.mult)
                    if tc == 2:
                        done(ins, "gs_done", l + 1)
                    elif tc == 0:
                        step(ins)
                    else:
                        done(ins, "e_ready", l + 1)
                need("et_mm", l + 1)
                for tc in range(3):
                    m = P if tc < 2 else DEC
                    tcc = slice(tc * P, tc * P + m)
                    for k in range(2):
                        dve.tensor_copy(ET[:, k, tcc], bank[2 + tc][:, k * P:k * P + m])
                    step(dve.tensor_copy(GHL[:, 0, tcc], bank[2 + tc][:, 2 * P:2 * P + m]))
                    ins = tt(GHL[:, 1, tcc], bank[2 + tc][:, 2 * P:2 * P + m], GHL[:, 0, tcc].bitcast(F32), ALU.subtract)
                done(ins, "et_evac", l + 1)
                for hf in range(2):
                    need("gelu_done", 2 + l * NK + (hf + 1) * HALF)
                    iota = cp("iota")[:, hf * HALF:(hf + 1) * HALF]
                    nb = (l * 2 + hf) * NB

                    def one_hot(n, b, turn):
                        tok = bass.ds(turn * TB + n * TB, TB)
                        tt(OHE[:, b], over(ET[:, 1, tok], HALF), rows(iota, TB), ALU.is_equal).then_inc(S["oe_ready"], 1)
                        tt(OH1[:, b], over(ET[:, 0, tok], NK), rows(cp("iota"), TB), ALU.is_equal)\
                            .then_inc(S["oh1_ready"], 1)

                    def gated(n, b, turn):
                        dve.wait_ge(S["g_mm"], turn + (nb + n + 3))
                        a = ACTS[:, :, bass.ds(turn * TB + n * TB, TB)].rearrange("p e t -> p t e")
                        tt(a, a, bank[6 + b][:, :].rearrange("p (t e) -> p t e", t=TB), ALU.mult)\
                            .then_inc(S["g_evac"], 1)

                    for n in range(2):
                        one_hot(n, n, 0)
                    with dve.Fori(0, NB // 2 - 1) as i:
                        for b in range(2):
                            gated(b, b, i * 2)
                            one_hot(2 + b, b, i * 2)
                    gated(NB - 3, 0, 0)
                    one_hot(NB - 1, 0, 0)
                    gated(NB - 2, 1, 0)
                    gated(NB - 1, 0, 0)

                    def low(g, b, turn):
                        G = l * 2 * NGRP + hf * NGRP + g
                        dve.wait_ge(S["ahi_done"], turn + (G + 1))
                        tt(UHL[:, b, 1, 0], ring[:, RAWU + 2 * b].rearrange("p k m -> p (k m)"),
                           UHL[:, b, 0, 0].bitcast(F32), ALU.subtract)
                        tt(AHL[:, b, 1], ACTS[:, bass.ds(turn * GRP + g * GRP, GRP), :], AHL[:, b, 0].bitcast(F32),
                           ALU.subtract).then_inc(S["alo_done"], 1)

                    def gather(g, ks, turn):
                        for k in ks:
                            n = (l * 2 * NGRP + hf * NGRP + g) * KD + k
                            dve.wait_ge(S["out_mm"], turn * KD + (n + 1 + 2 * KD))
                            tt(xT[:, k, :], xT[:, k, :], bank[2 + k % 4][:, 0:T], ALU.add).then_inc(S["out_evac"], 1)

                    need("g_evac", 2 + nb + NB)
                    low(0, 0, 0)
                    with dve.Fori(0, NGRP // 2 - 1) as i:
                        for b in range(2):
                            gather(b, range(0, 4), i * 2)
                            low(b + 1, 1 - b, i * 2)
                            gather(b, range(4, 8), i * 2)
                    gather(NGRP - 2, range(0, 4), 0)
                    low(NGRP - 1, 1, 0)
                    gather(NGRP - 2, range(4, 8), 0)
                    gather(NGRP - 1, range(KD), 0)
                need("out_evac", 4 + (l + 1) * 2 * NGRP * KD)
                dve.sem_inc(S["arena_free"], 1)
            norm(0, lambda k: com("fin_g", k, k + 1), "mix_std", DEPTH + 1, "h_ready", DEPTH + 1, "mix_sq", DEPTH + 1)

        @block.gpsimd
        def _(pool):
            pool.sem_inc(S["dlo_done"], 4)
            pool.sem_inc(S["ulo_done"], 2)

            for l in range(DEPTH):
                def down_lo(n, b, slot, turn):
                    pool.wait_ge(S["dhi_done"], turn + (l * NK + n + 1))
                    pool.tensor_tensor(DHL[:, b, 1], ring[:, RAWD + slot].rearrange("p k e -> p (k e)"),
                                       DHL[:, b, 0].bitcast(F32), ALU.subtract).then_inc(S["dlo_done"], 1)

                def up_lo(g, b, turn):
                    pool.wait_ge(S["uhi_done"], turn + (l * 2 * NGRP + g + 1))
                    pool.tensor_tensor(UHL[:, b, 1, 1], ring[:, RAWU + 2 * b + 1].rearrange("p k m -> p (k m)"),
                                       UHL[:, b, 0, 1].bitcast(F32), ALU.subtract).then_inc(S["ulo_done"], 1)

                with pool.Fori(0, HALF // 4) as i:
                    for b in range(4):
                        down_lo(b, b % 2, b, i * 4)
                pool.wait_ge(S["et_evac"], l + 1)
                for hf in range(2):
                    if hf:
                        pool.wait_ge(S["out_mm"], 2 * KD + (l * 2 + 1) * NGRP * KD)
                    nb = (l * 2 + hf) * NB

                    def one_hot(n, b, turn):
                        pool.wait_ge(S["g_mm"], turn + (nb + n + 1))
                        pool.wait_ge(S["oe_ready"], turn + (nb + n + 1))
                        for q in range(2):
                            gate = over(GHL[:, q, bass.ds(turn * TB + n * TB, TB)].bitcast(F32), HALF)
                            ins = pool.tensor_tensor(OH2[:, b, q].rearrange("p (t e) -> p t e", t=TB),
                                                     OHE[:, b].bitcast(F32), gate, ALU.mult)
                        ins.then_inc(S["oh_ready"], 1)

                    with pool.Fori(0, NB // 2) as i:
                        for b in range(2):
                            one_hot(b, b, i * 2)
                    one_hot(NB - 1, 0, 0)

                    def group(g, b, turn, more=True):
                        if hf == 0:
                            for c in range(2):
                                down_lo(HALF + 2 * g + c, c, (2 * b + c) % 4, turn * 2)
                        if more:
                            up_lo(hf * NGRP + g + 1, 1 - b, turn)

                    up_lo(hf * NGRP, 0, 0)
                    with pool.Fori(0, NGRP // 2 - 1) as i:
                        for b in range(2):
                            group(b, b, i * 2)
                    group(NGRP - 2, 0, 0)
                    group(NGRP - 1, 1, 0, False)


def top16(dve, step, scores, values, index):
    step(dve.max(values[:, 0:8], scores))
    dve.max_index(index[:, 0:8], values[:, 0:8], scores)
    step(dve.match_replace(scores, values[:, 0:8], scores, -3.0e38))
    step(dve.max(values[:, 8:16], scores))
    step(dve.max_index(index[:, 8:16], values[:, 8:16], scores))


INS = ["x", "cp", "cm", "par", "com", "w2a2", "g2", "vw1", "vw2", "wst", "sb", "sh", "wm", "down", "up", "rs", "hs"]
OUTS = {"o_y": (P, KD, T), "o_shift": (DEPTH, P, KD, DEC + 1), "o_rp": (DEPTH, P, NW, P),
        "o_rs": (DEPTH, DEC * RH, RN, RN), "o_hp": (DEPTH, P, NW, P), "o_hs": (DEPTH, P, DEC, NW, P),
        "o_sg": (DEPTH, P, NW, DEC)}


def lay_out(a):
    def col(v):
        return v.reshape(-1, P).T

    def wtile(w, k):
        return w.reshape(k, P, -1, P).transpose(2, 1, 0, 3)

    f = np.float32
    z32 = np.zeros((96,), f)
    out = {"x": np.concatenate([a["x_prompt"][0], a["x_sample"][:, 0]], 0).T.reshape(KD, P, T).transpose(1, 0, 2)}
    out["cp"], out["cm"] = masks()
    par = []
    for l in range(DEPTH):
        vmu = a["vres_mu"][l - 1] if l else np.zeros(32, f)
        v0 = a["vres_v0"][l - 1] if l else np.zeros(W, f)
        cols = {"mix_g": a["norm_mix_g"][l], "ffn_g": a["norm_ffn_g"][l], "mu": a["shift_mu"][l],
                "w0": a["rwkv_w0"][l], "a0": a["rwkv_a0"][l], "kk": a["rwkv_kk"][l], "ka": a["rwkv_ka"][l],
                "rk": a["rwkv_rk"][l].reshape(-1), "lg": a["rwkv_lnx_g"][l], "lb": a["rwkv_lnx_b"][l],
                "vmu": np.concatenate([vmu, z32]), "v0": v0, "hg": a["hgrn_norm_g"][l], "sg": a["sgu_ln_g"][l],
                "sb": a["sgu_ln_b"][l], "on": np.full(P, float(l > 0), f), "off": np.full(P, float(l == 0), f)}
        par.append(np.concatenate([col(cols[n]) for n, _ in PARS], 1))
    out["par"] = np.stack(par, 1)
    out["com"] = np.concatenate([col(a["hgrn_lb"][0]), col(a["hgrn_lb"][1]), col(a["norm_final_g"]),
                                 np.full((P, 1), EPS, f), np.full((P, 1), LNX_EPS, f)], 1)
    out["w2a2"] = np.concatenate([a["rwkv_w2"], a["rwkv_a2"]], 1)
    out["g2"] = a["rwkv_g2"]
    z = np.zeros((1, D_MODEL, 32), f)
    out["vw1"] = np.concatenate([z, a["vres_w1"]], 0).reshape(DEPTH, KD, P, 32).transpose(0, 2, 1, 3)
    out["vw2"] = np.concatenate([np.zeros((1, 32, W), f), a["vres_w2"]], 0)
    out["wst"] = a["sgu_ws"].transpose(0, 3, 1, 2)
    out["sb"] = a["sgu_b"].reshape(DEPTH, 1, NW, P)
    out["sh"] = a["state_shift"].transpose(0, 2, 1).reshape(DEPTH, KD, P, DEC).transpose(0, 2, 1, 3)
    wm = []
    for l in range(DEPTH):
        win = wtile(a["w_in"][l], KD).reshape(-1, P, D_MODEL)
        gates = win[38:].reshape(3, KD, P, D_MODEL)
        br = np.stack([wtile(a[n][l], NW) for n in ("w_branch_rwkv", "w_branch_hgrn", "w_branch_sgu")])
        rows_ = [win[:38]]
        for mp in range(4):
            rows_.append(gates[:, 2 * mp:2 * mp + 2].transpose(1, 0, 2, 3).reshape(6, P, D_MODEL))
            b = br[:, 2 * mp:2 * mp + 2].transpose(1, 0, 2, 3, 4).reshape(3, 2, P, W)
            rows_.append(b.transpose(0, 2, 1, 3).reshape(3, P, D_MODEL))
        rows_.append(wtile(a["w_out"][l], KD).reshape(-1, P, D_MODEL))
        keys = a["peer_keys"][l].reshape(2 * PH, NK, P).transpose(2, 0, 1).reshape(P, 2, D_MODEL)
        rows_.append(wtile(a["peer_wq"][l], KD).reshape(-1, P, D_MODEL))
        rows_.append(keys.transpose(1, 0, 2))
        wm.append(np.concatenate(rows_, 0))
    out["wm"] = np.stack(wm)
    out["down"] = a["peer_down"].reshape(DEPTH, P, NK, KD, P).transpose(0, 2, 4, 3, 1).reshape(DEPTH, NK, P, D_MODEL)
    out["up"] = a["peer_up"].reshape(DEPTH, P, NK, D_MODEL)
    out["rs"] = a["state_rwkv"].reshape(DEPTH, DEC * RH, RN, RN)
    out["hs"] = a["state_hgrn"].transpose(0, 3, 1, 2, 4)
    return {n: np.ascontiguousarray(v) for n, v in out.items()}


def kernel(**inputs):
    import concourse.bacc as bacc
    from concourse.bass_utils import run_bass_kernel_spmd

    arrays = lay_out({n: np.asarray(v) for n, v in inputs.items()})
    nc = bacc.Bacc("TRN2", target_bir_lowering=False, num_devices=1)
    d = {n: nc.dram_tensor(n, arrays[n].shape, F32, kind="ExternalInput").ap() for n in INS}
    for n, shape in OUTS.items():
        d[n] = nc.dram_tensor(n, shape, F32, kind="ExternalOutput").ap()
    build(nc, d)
    r = run_bass_kernel_spmd(nc, [{n: arrays[n] for n in INS}], core_ids=[0]).results[0]
    y = r["o_y"].transpose(2, 1, 0).reshape(T, D_MODEL)
    sh = r["o_shift"].transpose(0, 3, 2, 1).reshape(DEPTH, DEC + 1, D_MODEL)
    rp = r["o_rp"].reshape(DEPTH, 2, RN, NW, 2, RN)
    rp = np.stack([rp[:, 0, :, :, 0], rp[:, 1, :, :, 1]], 3)
    rp = rp.transpose(0, 2, 3, 4, 1).reshape(DEPTH, 1, RH, RN, RN)
    return (y[None, :SEQ], y[SEQ:, None], sh[:, 0:1], sh[:, 1:], rp,
            r["o_rs"].reshape(DEPTH, DEC, RH, RN, RN),
            r["o_hp"].transpose(0, 2, 1, 3).reshape(DEPTH, 1, NW, P, P),
            r["o_hs"].transpose(0, 2, 3, 1, 4),
            r["o_sg"].transpose(0, 3, 2, 1).reshape(DEPTH, DEC, 1, W))
```

```python
from contextlib import ExitStack

import numpy as np

import concourse.bass as bass
from concourse import mybir

F32 = mybir.dt.float32
U32 = mybir.dt.uint32
BF16 = mybir.dt.bfloat16
ALU = mybir.AluOpType
ACT = mybir.ActivationFunctionType
AX = mybir.AxisListType

P = 128
D_MODEL = 1024
KD = D_MODEL // P
SEQ, DEC, DEPTH = 256, 8, 2
T = SEQ + DEC
TS = T + DEC
W = 512
NW = W // P
RH, RN = 8, 64
RC = 64
NRC = SEQ // RC
HC = 128
NHC = SEQ // HC
LEV_R, LEV_H = 6, 7
PH, TOPK, NK = 8, 16, 128
ZR_W = TS + 1
RT, HT_, ST = 14, 16, 8
EPS, LNX_EPS = 1e-6, 64e-5
RINGP = 5
HALF = NK // 2
GRP = 2
NGRP = HALF // GRP
TB = 8
NB = T // TB
GB = 4

PARS = [("mix_g", 8), ("ffn_g", 8), ("mu", RT), ("w0", 4), ("a0", 4), ("kk", 4), ("ka", 4), ("rk", 4),
        ("lg", 4), ("lb", 4), ("vmu", 1), ("v0", 4), ("hg", 4), ("sg", 4), ("sb", 4), ("on", 1), ("off", 1)]
PAR_AT, PAR_N = {}, 0
for _n, _c in PARS:
    PAR_AT[_n] = (PAR_N, _c)
    PAR_N += _c
COM_AT = {"lb0": (0, 4), "lb1": (4, 4), "fin_g": (8, 8), "eps": (16, 1), "leps": (17, 1)}
COM_N = 18

CP_AT = {"ident": (0, 128), "ones": (128, 128), "bones": (256, 128), "iota": (384, 128), "iota16": (512, 16)}
CP_N = 528
CM_AT = {"rw": (0, 128), "n0": (128, 64), "lev": (192, 64 * LEV_R), "low": (576, 64), "hg": (640, 128 * 8),
         "triu": (1664, 128), "rscan": (1792, T), "hscan": (1792 + T, T)}
CM_N = 1792 + 2 * T


def masks():
    i = np.arange(P)
    cp = np.zeros((P, CP_N), np.float32)
    cp[:, 0:128] = np.eye(P)
    cp[:, 128:256] = 1
    cp[:, 256:384] = (i[:, None] // RN == i[None] // RN)
    cp[:, 384:512] = i[None]
    cp[:, 512:528] = i[None, :16]
    cm = np.zeros((P, CM_N), np.float32)
    s, t = i[:, None] % RC, i[None, :RC]
    cm[:, 0:64], cm[:, 64:128] = s < t, s <= t
    r, c = i[:RC, None], i[None, :RC]
    for lev in range(LEV_R):
        b = 2 << lev
        m = (r // b == c // b) & (r % b >= b // 2) & (c % b < b // 2)
        cm[:RC, 192 + 64 * lev:256 + 64 * lev] = m
        if lev == 0:
            cm[:RC, 128:192] = m.T
    cm[:RC, 576:640] = c < r
    s, t = i[:, None], i[None]
    for lev in range(LEV_H):
        b = 2 << lev
        cm[:, 640 + 128 * lev:768 + 128 * lev] = (s // b == t // b) & (s % b < b // 2) & (t % b >= b // 2)
    cm[:, 640 + 128 * LEV_H:768 + 128 * LEV_H] = s == t
    cm[:, 1664:1792] = s <= t
    t = np.arange(T)
    cm[:, 1792:1792 + T] = ((t % RC != 0) & (t < SEQ))[None]
    cm[:, 1792 + T:] = ((t % HC != 0) & (t < SEQ))[None]
    return cp, cm


def build(nc, d):
    ctx = ExitStack()
    with ctx:
        def sb(name, *shape, dt=F32):
            return ctx.enter_context(nc.sbuf_tensor(name, list(shape), dt))

        xT = sb("xT", P, KD, T)
        hT = sb("hT", P, KD, TS)
        ring = sb("ring", P, 2 * RINGP, KD, P)
        CP = sb("CP", P, CP_N)
        PAR = sb("PAR", P, DEPTH, PAR_N)
        COM = sb("COM", P, COM_N)
        LBS = sb("LBS", P, 6, NW)
        V1 = sb("V1", P, NW, T)
        NRM = sb("NRM", P, T)
        ARENA = 36240
        mixer_memory = ExitStack()
        arena = mixer_memory.enter_context(nc.sbuf_tensor("arena", [P, ARENA], F32))
        bank = [ctx.enter_context(nc.psum_tensor(f"bank{i}", [P, 512], F32)) for i in range(8)]

        def at(off, *dims):
            n = 1
            for x in dims:
                n *= x
            assert off + n <= ARENA, (off, n)
            v = arena[:, off:off + n]
            if len(dims) == 2:
                v = v.rearrange("p (a b) -> p a b", a=dims[0])
            if len(dims) == 3:
                v = v.rearrange("p (a b c) -> p a b c", a=dims[0], b=dims[1])
            return v

        CM = at(0, CM_N)
        o = CM_N
        W2A2 = at(o, W)
        G2 = at(o + 512, W)
        VW1 = at(o + 1024, KD, 32)
        VW2 = at(o + 1280, W)
        WST = at(o + 1792, NW, P)
        SBR = at(o + 2304, NW, P)
        o += 2816
        ZR = at(o, RT, ZR_W)
        XV = at(o + RT * ZR_W, ZR_W)
        RZ = o
        o += 4096
        HG = at(o, HT_, T)
        o += HT_ * T
        SG = at(o, ST, T)
        o += ST * T
        YR, YH, YS = (at(o + n * NW * T, NW, T) for n in range(3))
        o += 3 * NW * T
        WORK = o
        AR = at(o, NW, 2, T)
        BKV = at(o + 2112, NW * NRC, 3, RC)
        EC = at(o + 5280, NW, T)
        GG = at(o + 6336, NW, T)
        BO = at(o + 7392, NW, T)
        M = at(o + 8448, 4 * RH, P)
        LEFT = o + 12544
        D = at(LEFT, RT, T)
        XVS, LW, SGX = (at(LEFT + RT * T + n * T, T) for n in range(3))
        SW, AA, VG = (at(o + 8448 + n * NW * T, NW, T) for n in range(3))
        CU, T1, T2 = (at(RZ + n * NW * T, NW, T) for n in range(3))
        KK, T3 = YH, YS
        XT_ = at(RZ, 4 * RH, RC)
        YSC = at(RZ + 2048, W)
        BD = at(RZ + 2560, NW, P)
        TT_ = at(RZ + 3072, W)
        SQ = at(RZ + 3584, 6, NW, DEC)
        X_, P1, ML, L_ = (at(LEFT + n * 1024, 2 * RH, RC) for n in range(4))
        BKT = at(LEFT, NRC, W)
        UV = at(LEFT + 2048, NRC, W)
        SR = at(o + 8448, RN, RN)
        TR = at(LEFT, RN, RN)
        RQ = at(o, 6, RN)
        SA = at(o + 384, RN)
        OS = at(o + 448, RN)
        OT = at(o + 512, W)
        TQ = at(o + 2112, 6, W)
        names = ["EB", "QH", "KH", "BC", "FF", "U1", "U2", "HX0", "HX1"]
        HV = {n: at(o + i * NW * T, NW, T) for i, n in enumerate(names)}
        q = o + len(names) * NW * T
        AT_, VT, KT = (at(q + n * 1024, NHC, NW, P) for n in range(3))
        q += 3072
        SH, T5, VS = (at(q + n * 512, NW, P) for n in range(3))
        SHA, SHB = at(WORK + 14112, 5, NW, P), at(RZ + 2560, DEC - 5, NW, P)
        GEA, GEB, GEC = at(RZ, 9, T), at(WORK + 16672, 3, T), at(CM_N, 6, T)

        def shs(b):
            return SHA[:, b] if b < 5 else SHB[:, b - 5]

        def early_gate(e):
            return GEA[:, e, :] if e < 9 else GEB[:, e - 9, :] if e < 12 else GEC[:, e - 12, :]
        VC, VQ = at(o, NW, T), at(o + 1056, NW, T)
        VT2 = at(o + 2112, NHC, NW, P)
        SC8 = at(o + 3136, 8)
        MG = at(o + 4096, KD, T)
        GS = at(o + 4096 + KD * T, 2, T)
        PR = at(o + 4096 + KD * T + 2 * T, T)
        NSQ = at(WORK, KD, T)

        mixer_memory.close()
        FR = mybir.dt.float32r
        ACTS = sb("ACTS", P, HALF, T)
        ET = sb("ET", P, 2, T, dt=BF16)
        GP = sb("GP", P, 3, T, dt=BF16)
        HHL = sb("HHL", P, 2, KD, T, dt=FR)
        DHL = sb("DHL", P, 2, 2, D_MODEL, dt=FR)
        topk_memory = ExitStack()
        TKN = 10304
        tk = topk_memory.enter_context(nc.sbuf_tensor("topk", [P, TKN], F32))
        topk_memory.close()
        gate_memory = ExitStack()
        OH1 = gate_memory.enter_context(nc.sbuf_tensor("OH1", [P, GB, NK, TB], BF16))
        OHE = gate_memory.enter_context(nc.sbuf_tensor("OHE", [P, GB, HALF, TB], BF16))
        OH2 = gate_memory.enter_context(nc.sbuf_tensor("OH2", [P, GB, 3, HALF, TB], BF16))
        IOTA = gate_memory.enter_context(nc.sbuf_tensor("IOTA", [P, NK, TB], BF16))
        gate_memory.close()
        UHL = sb("UHL", P, 2, 2, GRP, D_MODEL, dt=FR)
        AHL = sb("AHL", P, 2, 2, GRP, T, dt=FR)
        at_ = [0]

        def tka(*dims):
            n = int(np.prod(dims))
            v = tk[:, at_[0]:at_[0] + n]
            at_[0] += n
            assert at_[0] <= TKN
            if len(dims) == 2:
                v = v.rearrange("p (a b) -> p a b", a=dims[0])
            if len(dims) == 3:
                v = v.rearrange("p (a b c) -> p a b c", a=dims[0], b=dims[1])
            return v

        QT = tka(2 * PH, T)
        SC = [tka(2 * PH, P)] + [ring[:, 2 * n:2 * n + 2].rearrange("p s k m -> p (s k) m") for n in range(2)]
        SV, SI = tka(PH, 2, TOPK), tka(PH, 2, TOPK)
        COMB = tka(PH, TOPK, TOPK)
        CV, CI = tka(PH, TOPK), tka(PH, TOPK)
        EG = [[tka(PH, TOPK) for n in range(3)] for tc in range(3)]
        SM = tka(2, PH)
        qt = QT.rearrange("p a t -> p (a t)")
        PKR = qt[:, 0:2 * NK].rearrange("p (a b) -> p a b", a=2)
        SE1, SE2, SGA = (qt[:, 2 * NK + n * TOPK:2 * NK + (n + 1) * TOPK] for n in range(3))
        KEYS = ring[:, 4:6].rearrange("p s k m -> p (s k) m")
        RES = qt[:, 2 * NK + 3 * TOPK:2 * NK + 3 * TOPK + T]
        RAWD, RAWU = 6, 0

        names = """par_in smalls_in lb_in lb_exp mix_sq mix_ss mix_std h_ready shift_out z_mm z_evac xv_mm
            xv_evac zs_ready lora_in lora_mm lora_evac decay_in decay_out kk_sq kk_ss kk_std prep_done bon_done
            bon_mm mat_mm mat_evac l_mm l_evac p_mm p_evac x_in2 x_mm x_done tok_mm tok_evac y_mm y_evac u_mm
            u_evac o_evac s_mm s_evac sq_mm sq_evac rq_in sr_in sr_done sr_out so_out so_in ot_mm gn_m gn_sq gn_v
            gn_std yr_done hg_in hg_sig f_ready f_ln b_ready eb_done lev_in lev_exp lev_x att_mm att_evac kh_in
            kh_exp kh_done ht_mm ht_evac ho_evac hs_mm hs_evac shs_in vs_mm vs_evac vb_mm vb_evac hso_mm hso_evac
            hn_sq hn_mm hn_std h_out sg_mm sg_mu sg_vm sg_std sg_vn sgt_mm sgt_evac mx_mm mx_evac sgo_out
            gate_mm gate_evac br_mm br_evac wo_mm wo_evac ffn_sq ffn_ss ffn_std h2_ready q_mm q_evac
            sc_mm sc_evac sm_in sm_exp e_ready et_mm et_evac oh1_ready oe_ready oh_ready g_mm g_evac
            dhi_done dlo_done uhi_done ulo_done ahi_done alo_done hlo_done packed_in gs_done pre_mm gelu_done
            out_mm out_evac y_out bd_out at_add arena_free dve_step mg_add mg_done""".split()
        S = {n: ctx.enter_context(nc.semaphore(n)) for n in dict.fromkeys(names)}
        ring_in = [ctx.enter_context(nc.semaphore(f"ring_in{i}")) for i in range(RINGP)]
        ring_free = [ctx.enter_context(nc.semaphore(f"ring_free{i}")) for i in range(RINGP)]
        dn_in = [ctx.enter_context(nc.semaphore(f"dn_in{i}")) for i in range(4)]
        up_in = [ctx.enter_context(nc.semaphore(f"up_in{i}")) for i in range(2)]
        NSMALL = 8
        USES = [11, 11, 10, 9, 9]

        def par(l, n, a=0, b=None):
            c, k = PAR_AT[n]
            return PAR[:, l, c + a:c + (k if b is None else b)]

        def com(n, a=0, b=None):
            c, k = COM_AT[n]
            return COM[:, c + a:c + (k if b is None else b)]

        def cp(n):
            c, k = CP_AT[n]
            return CP[:, c:c + k]

        def cm(n, a=0, k=None):
            c, w = CM_AT[n]
            return CM[:, c + a:c + a + (w if k is None else k)]

        ident, ones, bones = cp("ident"), cp("ones"), cp("bones")

        def over(ap, n):
            return ap.rearrange("p (a b) -> p a b", b=1).broadcast_to([ap.shape[0], ap.shape[1], n])

        def rows(ap, n):
            return ap.rearrange("p (a b) -> p a b", a=1).broadcast_to([ap.shape[0], n, ap.shape[1]])

        block = ctx.enter_context(nc.Block())

        @block.sync
        def _(sp):
            sp.dma_start(xT[:], d["x"]).then_inc(S["par_in"], 16)
            for dst, src in ((CP[:], d["cp"]), (PAR[:], d["par"]), (COM[:], d["com"])):
                sp.dma_start(dst, src).then_inc(S["par_in"], 16)
            use = [0] * RINGP

            def pair(slot, src, l, n=2, i=0):
                sp.wait_ge(ring_free[slot], i + (l * USES[slot] + use[slot] + 1))
                sp.dma_start(ring[:, 2 * slot:2 * slot + n].rearrange("p s k m -> p s (k m)"), src)\
                    .then_inc(ring_in[slot], 16)

            for l in range(DEPTH):
                if l:
                    sp.wait_ge(S["arena_free"], l)
                for dst, src in ((CM, d["cm"]), (W2A2, d["w2a2"][l]), (G2, d["g2"][l]), (VW1, d["vw1"][l]),
                                 (VW2[0:32], d["vw2"][l]), (WST, d["wst"][l]), (SBR[0:1], d["sb"][l]),
                                 (hT[:, :, T:TS], d["sh"][l])):
                    sp.dma_start(dst, src).then_inc(S["smalls_in"], 16)
                use = [0] * RINGP
                wm = d["wm"][l]

                def tiles(first, n):
                    return wm[first:first + n].rearrange("s p m -> p s m")

                def rtiles(base, i, step, off, n):
                    return wm[bass.ds(i * step + (base + off), n)].rearrange("s p m -> p s m")

                with sp.Fori(0, 3) as i:
                    for s in range(RINGP):
                        pair(s, rtiles(0, i, 10, 2 * s, 2), l, i=i)
                use = [3] * RINGP
                for s in range(4):
                    pair(s, tiles(30 + 2 * s, 2), l)
                    use[s] += 1
                for n in range(18):
                    s = (19 + n) % RINGP
                    pair(s, tiles(38 + 2 * n, 2), l)
                    use[s] += 1
                for n in range(13):
                    s = n % RINGP
                    pair(s, tiles(74 + 2 * n, 2), l)
                    use[s] += 1
                assert use == USES, use
                def down(n, slot, turn):
                    sp.wait_ge(S["dlo_done"], turn + (l * NK + n + 1))
                    sp.dma_start(ring[:, RAWD + slot].rearrange("p k e -> p (k e)"),
                                 d["down"][l][bass.ds(turn + n, 1)].rearrange("a p m -> p (a m)"))\
                        .then_inc(dn_in[slot], 16)

                def up(g, slot, turn):
                    sp.wait_ge(S["ulo_done"], turn + (l * 2 * NGRP + g + 1))
                    sp.wait_ge(S["alo_done"], turn + (l * 2 * NGRP + g + 1))
                    sp.dma_start(ring[:, RAWU + 2 * slot:RAWU + 2 * slot + 2].rearrange("p s k m -> p s (k m)"),
                                 d["up"][l][:, bass.ds(turn * GRP + g * GRP, GRP)]).then_inc(up_in[slot], 16)

                sp.wait_ge(S["sc_mm"], 12 * (l + 1))
                with sp.Fori(0, HALF // 4) as i:
                    for b in range(4):
                        down(b, b, i * 4)
                sp.wait_ge(S["packed_in"], (l + 1) * 64)
                with sp.Fori(0, NGRP // 2) as i:
                    for b in range(2):
                        up(b, b, i * 2)
                        down(HALF + 2 * b, 2 * b, i * 4)
                        down(HALF + 2 * b + 1, 2 * b + 1, i * 4)
                with sp.Fori(0, NGRP // 2) as i:
                    for b in range(2):
                        up(NGRP + b, b, i * 2)
            sp.wait_ge(S["y_out"], 16)

        @block.tensor
        def _(pe):
            def mm(out, lhsT, rhs, start=True, stop=True):
                return pe.matmul(out, lhsT, rhs, start=start, stop=stop)

            def need(name, n):
                pe.wait_ge(S[name], n)

            for s in range(RINGP):
                pe.sem_inc(ring_free[s], 1)
            pe.sem_inc(S["pre_mm"], 2)
            pe.sem_inc(S["out_mm"], 2 * KD)
            pe.sem_inc(S["g_mm"], GB)
            need("par_in", 64)
            use = [0] * RINGP

            def arrive(slot, l, i=0):
                pe.wait_ge(ring_in[slot], (i + (l * USES[slot] + use[slot] + 1)) * 16)

            def proj(out, slot_tile, src, n, k=KD, half=0):
                for kk in range(k):
                    ins = mm(out, ring[:, slot_tile, half * k + kk, :], src[:, kk, 0:n], kk == 0, kk == k - 1)
                return ins

            def spread(sq, outs, weights=ones):
                for i, b in enumerate(outs):
                    ins = mm(b[:, 0:T], weights, sq[:, i, :])
                return ins

            for l in range(DEPTH):
                use = [0] * RINGP
                need("mix_sq", l + 1)
                for k in range(KD):
                    ins = mm(bank[0][:, 0:T], ones, NSQ[:, k, :], k == 0, k == KD - 1)
                ins.then_inc(S["mix_ss"], 1)
                need("h_ready", l + 1)
                need("smalls_in", 16 * NSMALL * (l + 1))
                for k in range(KD):
                    ins = mm(bank[2][0:32, 0:TS], VW1[:, k, :], hT[:, k, :], k == 0, k == KD - 1)
                ins.then_inc(S["xv_mm"], 1)
                def z_tiles(first, end, at=0):
                    for c in range(first, end):
                        slot = c // 2 % RINGP
                        if c % 2 == 0:
                            arrive(slot, l)
                        need("z_evac", l * 38 + c + 1)
                        proj(bank[at + c % 2][:, 0:TS], 2 * slot + c % 2, hT, TS).then_inc(S["z_mm"], 1)
                        if c % 2:
                            pe.drain().then_inc(ring_free[slot], 1)
                            use[slot] += 1

                z_tiles(0, 20)
                need("lora_in", 3 * (l + 1))
                need("zs_ready", 2 * (l + 1))
                lora = [(W2A2[0:64], LW[0:64]), (W2A2[64:128], LW[64:128]), (VW2[0:32], XVS[0:32]), (G2, SGX)]
                for n in range(16):
                    if n >= 4:
                        need("lora_evac", l * 16 + n - 3)
                    w, x = lora[n // 4]
                    mm(bank[2 + n % 4][:, 0:T], w[:, (n % 4) * P:(n % 4 + 1) * P], x).then_inc(S["lora_mm"], 1)
                z_tiles(20, 22)
                need("lora_evac", l * 16 + 16)
                need("kk_sq", l + 1)
                spread(T3, bank[2:6], bones).then_inc(S["kk_ss"], 1)
                z_tiles(22, 24)
                need("prep_done", l + 1)
                need("kk_std", l + 1)
                spread(SW, bank[2:6], bones).then_inc(S["bon_mm"], 1)
                z_tiles(24, 25)
                need("bon_done", l + 1)
                need("z_evac", 2 + l * 38 + 25)
                for g in range(2 * NRC):
                    n, pr = g // 2, g % 2
                    if g >= 4:
                        need("mat_evac", l * 8 + g - 3)
                    hp = slice(64 * pr, 64 * pr + 64)
                    for j in range(NW):
                        ins = mm(bank[g % 4][:, j * P:(j + 1) * P].rearrange("p (a t) -> p a t", a=2),
                                 BKV[hp, j * NRC + n, 0:2, :].rearrange("p a t -> p (a t)"),
                                 AR[hp, j, :, n * RC:(n + 1) * RC])
                    ins.then_inc(S["mat_mm"], 1)
                for half in range(2):
                    if half:
                        need("z_evac", 2 + l * 38 + 31)
                    for pr in range(2):
                        hp = slice(64 * pr, 64 * pr + 64)
                        if half:
                            need("l_evac", l * 2 + half)
                        for nn in range(2):
                            n = 2 * half + nn
                            for j in range(NW):
                                c = (nn * NW + j) * RC
                                ins = mm(bank[4 + pr][0:RC, c:c + RC], AR[hp, j, 0, n * RC:(n + 1) * RC],
                                         BKV[hp, j * NRC + n, 0, :])
                    ins.then_inc(S["l_mm"], 1)
                    need("l_evac", l * 2 + half + 1)
                    z_tiles((25, 31)[half], (27, 33)[half], 4)
                    for lev in range(1, LEV_R):
                        e = (l * 2 + half) * (LEV_R - 1) + lev
                        need("x_in2", e)
                        for m in range(2 * RH):
                            ins = mm(bank[m // 8][0:RC, (m % 8) * RC:(m % 8 + 1) * RC], ML[0:RC, m, :],
                                     XT_[0:RC, 16 * half + m, :])
                        ins.then_inc(S["p_mm"], 1)
                        need("p_evac", e)
                        for m in range(2 * RH):
                            c = slice((m % 8) * RC, (m % 8 + 1) * RC)
                            mm(bank[2 + m // 8][0:RC, c], X_[0:RC, m, :], P1[0:RC, m, :])
                        for m in range(2 * RH):
                            c = slice((m % 8) * RC, (m % 8 + 1) * RC)
                            ins = mm(bank[6 + m // 8][0:RC, c], P1[0:RC, m, :], X_[0:RC, m, :])
                        ins.then_inc(S["x_mm"], 1)
                        if half or lev < 5:
                            c = (26, 32)[half] + lev
                            z_tiles(c, c + 1, 4)
                need("x_done", l + 1)
                need("z_evac", 2 + (l + 1) * 38)
                for n in range(NRC):
                    for v in range(2):
                        g = 2 * n + v
                        if g >= 4:
                            need("tok_evac", l * 8 + g - 3)
                        for j in range(NW):
                            ins = pe.transpose(bank[g % 4][:, j * P:(j + 1) * P],
                                               BKV[:, j * NRC + n, v:v + 2, :].rearrange("p a t -> p (a t)"), ident)
                        ins.then_inc(S["tok_mm"], 1)
                need("tok_evac", l * 8 + 8)
                for n in range(NRC):
                    e = l * NRC + n + 1
                    c = slice(n * RC, (n + 1) * RC)
                    need("s_evac", e + l)
                    for j in range(NW):
                        mm(bank[4][0:RC, j * P:(j + 1) * P], AR[:, j, 0, c], BD[:, j, :])
                    for h in range(RH):
                        idx = n * RH + (h % 2) * NW + h // 2
                        hc = slice(h * RN, (h + 1) * RN)
                        ins = mm(bank[5][0:RC, hc], M[64:128, idx, 0:64], UV[64:128, n, hc])
                    ins.then_inc(S["y_mm"], 1)
                    need("y_evac", e)
                    for h in range(RH):
                        idx = n * RH + (h % 2) * NW + h // 2
                        hc = slice(h * RN, (h + 1) * RN)
                        ins = mm(bank[6][0:RC, hc], XT_[0:RC, idx, :], YSC[0:RC, hc])
                    ins.then_inc(S["u_mm"], 1)
                    need("u_evac", e)
                    if n:
                        need("o_evac", e - 1)
                    for j in range(NW):
                        mm(bank[7][:, j * P:(j + 1) * P], BKT[:, n, j * P:(j + 1) * P], UV[:, n, j * P:(j + 1) * P])
                    for j in range(NW):
                        oc = slice(j * RC, (j + 1) * RC)
                        mm(bank[0][:, oc], BD[:, j, :], AR[:, j, 1, c], True, False)
                        for hh in range(2):
                            idx = n * RH + hh * NW + j
                            h = 2 * j + hh
                            ins = mm(bank[0][64 * hh:64 * hh + 64, oc], UV[:, n, h * RN:(h + 1) * RN],
                                     M[:, idx, 64:128], False, True)
                    ins.then_inc(S["s_mm"], 1)
                need("o_evac", (l + 1) * NRC)
                for g in range(6):
                    if g >= 2:
                        need("sq_evac", l * 6 + g - 1)
                    for j in range(NW):
                        ins = pe.transpose(bank[g % 2][0:DEC, j * P:(j + 1) * P], SQ[:, g, j, :], ident)
                    ins.then_inc(S["sq_mm"], 1)
                def gate_tile(n, slot, out):
                    if n % 2 == 0:
                        arrive(slot, l)
                    need("gate_evac", l * 24 + n + 1)
                    proj(out[:, 0:T], 2 * slot + n % 2, hT, T).then_inc(S["gate_mm"], 1)
                    if n % 2:
                        pe.drain().then_inc(ring_free[slot], 1)
                        use[slot] += 1

                for n in range(12):
                    gate_tile(n, (19 + n // 2) % RINGP, bank[2 + n % 2])
                need("so_in", 16 * (l + 1))
                need("sq_evac", l * 6 + 6)
                for j in range(NW):
                    ins = pe.transpose(bank[0][:, j * DEC:(j + 1) * DEC], OT[0:DEC, j * P:(j + 1) * P], ident[0:DEC, 0:DEC])
                ins.then_inc(S["ot_mm"], 1)
                need("so_out", l + 1)
                need("gate_evac", l * 24 + 14)
                spread(YR, bank[2:6], bones).then_inc(S["gn_sq"], 1)
                need("gn_m", l + 1)
                spread(at(WORK + 1056, NW, T), bank[2:6], bones).then_inc(S["gn_v"], 1)
                for n in range(12, 18):
                    gate_tile(n, (19 + n // 2) % RINGP, bank[n % 2])

                need("gate_evac", l * 24 + 20)
                for lev in range(LEV_H + 1):
                    need("lev_x", l * (LEV_H + 1) + lev + 1)
                    for c in range(NHC):
                        if lev:
                            need("att_evac", l * 2 * (LEV_H + 1) + 2 * lev + c - 1)
                        cc = slice(c * HC, (c + 1) * HC)
                        for h in range(NW):
                            if lev == 0:
                                a, b = HG[:, 4 + h, cc], HG[:, h, cc]
                            else:
                                a = b = HV[f"HX{lev % 2}"][:, h, cc]
                            ins = mm(bank[c][:, h * P:(h + 1) * P], a, b)
                        ins.then_inc(S["att_mm"], 1)
                need("att_evac", (l + 1) * 2 * (LEV_H + 1))
                need("kh_done", l + 1)
                for g in range(2 * NHC):
                    c = g // 2
                    cc = slice(c * HC, (c + 1) * HC)
                    for h in range(NW):
                        src = HG[:, 8 + h, cc] if g % 2 == 0 else HV["KH"][:, h, cc]
                        ins = pe.transpose(bank[2 + g][:, h * P:(h + 1) * P], src, ident)
                    ins.then_inc(S["ht_mm"], 1)
                for h in range(NW):
                    ins = pe.transpose(bank[6][0:DEC, h * P:(h + 1) * P], HG[:, 8 + h, SEQ:T], ident)
                ins.then_inc(S["vs_mm"], 1)
                need("ht_evac", (l + 1) * 4)
                need("at_add", 2 * LEV_H * (l + 1))
                for c in range(NHC):
                    cc = slice(c * HC, (c + 1) * HC)
                    need("hs_evac", l * 3 + c + 1)
                    for h in range(NW):
                        hc = slice(h * P, (h + 1) * P)
                        mm(bank[2][:, hc], SH[:, h, :], HV["QH"][:, h, cc], True, False)
                        mm(bank[2][:, hc], VT[:, c, h, :], AT_[:, c, h, :], False, True)
                    for h in range(NW):
                        ins = mm(bank[3][:, h * P:(h + 1) * P], KT[:, c, h, :], VT[:, c, h, :])
                    ins.then_inc(S["hs_mm"], 1)
                    need("ho_evac", l * 2 + c + 1)
                need("vs_evac", l + 1)
                for b in range(DEC):
                    if b >= 2:
                        need("vb_evac", l * DEC + b - 1)
                    mm(bank[4 + b % 2][:, 0:W], ident[0:DEC, b:b + 1].broadcast_to([DEC, P]),
                       VS[0:DEC].rearrange("p a b -> p (a b)")).then_inc(S["vb_mm"], 1)
                need("vb_evac", (l + 1) * DEC)
                for b in range(DEC):
                    for h in range(NW):
                        ins = mm(bank[6][:, h * DEC + b:h * DEC + b + 1], shs(b)[:, h, :], HG[:, h, SEQ + b:SEQ + b + 1])
                ins.then_inc(S["hso_mm"], 1)
                for h in range(NW):
                    ins = mm(bank[0][:, 0:T], ones, SG[:, NW + h, :], h == 0, h == NW - 1)
                ins.then_inc(S["sg_mm"], 1)
                need("hn_sq", l + 1)
                spread(HV["U1"], bank[2:6]).then_inc(S["hn_mm"], 1)

                need("sg_mu", l + 1)
                for h in range(NW):
                    ins = mm(bank[1][:, 0:T], ones, VQ[:, h, :], h == 0, h == NW - 1)
                ins.then_inc(S["sg_vm"], 1)
                need("sg_vn", l + 1)
                for c in range(NHC):
                    for h in range(NW):
                        ins = pe.transpose(bank[2 + c][:, h * P:(h + 1) * P], VC[:, h, c * HC:(c + 1) * HC], ident)
                    ins.then_inc(S["sgt_mm"], 1)
                need("sgt_evac", 2 * (l + 1))
                for c in range(NHC):
                    for h in range(NW):
                        hc = slice(h * P, (h + 1) * P)
                        mm(bank[4 + c][:, hc], VT2[:, c, h, :], WST[:, h, :], True, False)
                        mm(bank[4 + c][:, hc], ones[0:1, :], SBR[0:1, h, :], False, True)
                mm(bank[6][:, 0:NW], ones[0:1, :], WST[0:1, :, 0])
                mm(bank[6][:, NW:2 * NW], ones[0:1, :], SBR[0:1, :, 0]).then_inc(S["mx_mm"], 1)

                need("mx_evac", l + 1)
                need("yr_done", 2 * (l + 1))
                for n in range(24):
                    q, b = n % 6, n // 2
                    slot = (28 + b // 2) % RINGP if b < 10 else 4
                    if n >= 18:
                        gate_tile(n, (3, 0, 1)[q // 2], bank[n % 2])
                    if n % 4 == 0:
                        arrive(slot, l)
                    need("br_evac", l * 24 + n + 1)
                    proj(bank[2 + n % 2][:, 0:T], 2 * slot + b % 2, (YR, YH, YS)[n % 3], T, NW, n % 2)\
                        .then_inc(S["br_mm"], 1)
                    if n % 4 == 3:
                        pe.drain().then_inc(ring_free[slot], 1)
                        use[slot] += 1
                need("br_evac", (l + 1) * 24 + 2)
                need("gate_evac", (l + 1) * 24 + 2)
                need("mg_done", l + 1)
                for m in range(KD):
                    s = m // 2
                    if m % 2 == 0:
                        arrive(s, l)
                    proj(bank[m][:, 0:T], m, MG, T).then_inc(S["wo_mm"], 1)
                    if m % 2:
                        pe.drain().then_inc(ring_free[s], 1)
                        use[s] += 1
                need("ffn_sq", l + 1)
                for k in range(KD):
                    ins = mm(bank[0][:, 0:T], ones, NSQ[:, k, :], k == 0, k == KD - 1)
                ins.then_inc(S["ffn_ss"], 1)
                need("h2_ready", l + 1)
                for n in range(2 * PH):
                    s = (4 + n // 2) % RINGP
                    if n % 2 == 0:
                        arrive(s, l)
                    if n >= 2:
                        need("q_evac", l * 16 + n - 1)
                    proj(bank[n % 2][:, 0:T], 2 * s + n % 2, hT, T).then_inc(S["q_mm"], 1)
                    if n % 2:
                        pe.drain().then_inc(ring_free[s], 1)
                        use[s] += 1
                need("q_evac", l * 16 + 16)
                arrive(2, l)
                use[2] += 1
                assert use == USES, use
                for g in range(12):
                    tc, hp0 = g // 4, 4 * (g % 4)
                    m = P if tc < 2 else DEC
                    if g >= 2:
                        need("sc_evac", l * 12 + g - 1)
                    for k in range(4):
                        ins = mm(bank[4 + g % 2][0:m, k * P:(k + 1) * P], QT[:, hp0 + k, tc * P:tc * P + m],
                                 KEYS[:, hp0 + k, :])
                    ins.then_inc(S["sc_mm"], 1)

                def down(n, b, turn):
                    pe.wait_ge(S["gelu_done"], turn + (l * NK + n + 1))
                    pe.wait_ge(S["dhi_done"], turn + (l * NK + n + 1))
                    for k in range(KD):
                        for q in range(2):
                            mm(bank[b][:, 0:T], DHL[:, b, 0, k * P:(k + 1) * P], HHL[:, q, k, :], k + q == 0, False)
                    pe.wait_ge(S["dlo_done"], turn + (l * NK + n + 5))
                    for k in range(KD):
                        ins = mm(bank[b][:, 0:T], DHL[:, b, 1, k * P:(k + 1) * P], HHL[:, 0, k, :], False, k == KD - 1)
                    ins.then_inc(S["pre_mm"], 1)

                def up(g, b, turn):
                    pe.wait_ge(S["alo_done"], turn + (l * 2 * NGRP + g + 3))
                    pe.wait_ge(S["ulo_done"], turn + (l * 2 * NGRP + g + 3))
                    for k in range(KD):
                        kc = slice(k * P, (k + 1) * P)
                        pe.wait_ge(S["out_evac"], turn * KD + ((l * 2 * NGRP + g) * KD + k + 1))
                        for j in range(GRP):
                            for q, r in ((0, 0), (0, 1), (1, 0)):
                                ins = mm(bank[2 + k % 4][:, 0:T], UHL[:, b, q, j, kc], AHL[:, b, r, j, :],
                                         j + q + r == 0, j == GRP - 1 and q == 1)
                        ins.then_inc(S["out_mm"], 1)

                def gates(n, b, turn):
                    pe.wait_ge(S["g_evac"], turn + (n + 1))
                    pe.wait_ge(S["oh1_ready"], turn + (n + 1))
                    pe.wait_ge(S["oh_ready"], turn + (n + 1))
                    for t in range(TB):
                        for q in range(3):
                            ins = mm(bank[4 + b][:, t * HALF:(t + 1) * HALF], OH1[:, b, :, t],
                                     OH2[:, b, q, :, t], q == 0, q == 2)
                    ins.then_inc(S["g_mm"], 1)

                need("hlo_done", l + 1)
                with pe.Fori(0, HALF // 2 - 2) as i:
                    for b in range(2):
                        down(b, b, i * 2)
                need("e_ready", l + 1)
                need("packed_in", 64 * (l + 1))
                for tc in range(3):
                    m = P if tc < 2 else DEC
                    for k in range(3):
                        ins = pe.transpose(bank[2 + tc][:, k * P:k * P + m], EG[tc][k][0:m].rearrange("p a b -> p (a b)"),
                                           ident[0:m, 0:m])
                ins.then_inc(S["et_mm"], 1)
                pe.sem_inc(ring_free[2], 1)
                for n in range(HALF - 4, HALF):
                    down(n, n % 2, 0)
                for hf in range(2):
                    base = (l * 2 + hf) * NB
                    with pe.Fori(0, NB // GB) as i:
                        for b in range(GB):
                            gates(base + b, b, i * GB)
                    gates(base + NB - 1, 0, 0)
                    if hf == 0:
                        with pe.Fori(0, NGRP // 2) as i:
                            for b in range(2):
                                up(b, b, i * 2)
                                down(HALF + 2 * b, 0, i * 4)
                                down(HALF + 2 * b + 1, 1, i * 4)
                    else:
                        with pe.Fori(0, NGRP // 2) as i:
                            for b in range(2):
                                up(NGRP + b, b, i * 2)
            need("mix_sq", DEPTH + 1)
            for k in range(KD):
                ins = mm(bank[0][:, 0:T], ones, NSQ[:, k, :], k == 0, k == KD - 1)
            ins.then_inc(S["mix_ss"], 1)

        @block.scalar
        def _(act):
            def need(name, n):
                act.wait_ge(S[name], n)

            def f(out, in_, fn, **kw):
                return act.activation(out, in_, fn, **kw)

            act.sem_inc(S["z_evac"], 2)
            act.sem_inc(S["gelu_done"], 2)
            act.sem_inc(S["gate_evac"], 2)
            need("par_in", 64)
            need("lb_in", 1)
            f(LBS[:, 2:4], LBS[:, 0:2], ACT.Exp).then_inc(S["lb_exp"], 1)
            for l in range(DEPTH):
                need("mix_ss", l + 1)
                f(NRM[:], bank[0][:, 0:T], ACT.Sqrt, scale=1.0 / D_MODEL, bias=com("eps")).then_inc(S["mix_std"], 1)
                need("h_ready", l + 1)
                need("smalls_in", 16 * NSMALL * (l + 1))
                act.dma_start(d["o_shift"][l], hT[:, :, SEQ - 1:T]).then_inc(S["shift_out"], 16)
                need("xv_mm", l + 1)
                f(XV[0:32, 1:ZR_W], bank[2][0:32, 0:TS], ACT.Copy).then_inc(S["xv_evac"], 1)
                def z_out(first, end, at=0):
                    for c in range(first, end):
                        need("z_mm", l * 38 + c + 1)
                        if c < RT:
                            f(ZR[:, c, 1:ZR_W], bank[at + c % 2][:, 0:TS], ACT.Copy).then_inc(S["z_evac"], 1)
                        elif c < RT + HT_:
                            f(HG[:, c - RT, :], bank[at + c % 2][:, 0:T], ACT.Copy).then_inc(S["z_evac"], 1)
                        else:
                            f(SG[:, c - RT - HT_, :], bank[at + c % 2][:, 0:T], ACT.Gelu).then_inc(S["z_evac"], 1)

                z_out(0, 19)
                need("zs_ready", 2 * l + 2)
                f(LW[0:64], D[0:64, 12, :], ACT.Tanh).then_inc(S["lora_in"], 1)
                f(LW[64:128], D[64:128, 12, :], ACT.Copy).then_inc(S["lora_in"], 1)
                f(SGX, D[:, 13, :], ACT.Sigmoid).then_inc(S["lora_in"], 1)
                z_out(19, 20)
                for n in range(16):
                    need("lora_mm", l * 16 + n + 1)
                    j = n % 4
                    src = bank[2 + j][:, 0:T]
                    if n < 12:
                        dst = (SW, AA, VG)[n // 4][:, j, :]
                        b = par(l, ("w0", "a0", "v0")[n // 4], j, j + 1)
                        f(dst, src, ACT.Sigmoid, bias=b).then_inc(S["lora_evac"], 1)
                    else:
                        f(GG[:, j, :], src, ACT.Copy).then_inc(S["lora_evac"], 1)
                need("decay_in", l + 1)
                f(EC, CU, ACT.Exp).then_inc(S["decay_out"], 1)
                f(T1, T2, ACT.Exp).then_inc(S["decay_out"], 1)
                need("decay_out", 3 * l + 2)
                f(T2, CU, ACT.Exp, scale=-1.0).then_inc(S["decay_out"], 1)
                z_out(20, 22)
                need("kk_ss", l + 1)
                need("decay_out", 3 * l + 3)
                for j in range(NW):
                    ins = f(T3[:, j, :], bank[2 + j][:, 0:T], ACT.Sqrt)
                ins.then_inc(S["kk_std"], 1)
                z_out(22, 25)
                for half in range(2):
                    z_out((25, 31)[half], (27, 33)[half], 4)
                    for lev in range(1, LEV_R):
                        e = (l * 2 + half) * (LEV_R - 1) + lev
                        need("p_mm", e)
                        for b in range(2):
                            ins = f(P1[0:RC, 8 * b:8 * b + 8].rearrange("p a b -> p (a b)"), bank[b][0:RC, :], ACT.Copy)
                        ins.then_inc(S["p_evac"], 1)
                        if half or lev < 5:
                            c = (26, 32)[half] + lev
                            z_out(c, c + 1, 4)
                for n in range(NRC):
                    for v in range(2):
                        need("tok_mm", l * 8 + 2 * n + v + 1)
                        if v == 0:
                            f(BKT[:, n], bank[2 * n % 4][:, :], ACT.Copy).then_inc(S["tok_evac"], 1)
                        else:
                            f(UV[64:128, n], bank[(2 * n + 1) % 4][64:128, :], ACT.Copy).then_inc(S["tok_evac"], 1)
                for n in range(NRC):
                    e = l * NRC + n + 1
                    need("u_mm", e)
                    f(UV[0:64, n], bank[6][0:64, :], ACT.Copy).then_inc(S["u_evac"], 1)
                    need("s_mm", e)
                    f(YR[:, :, n * RC:(n + 1) * RC], bank[0][:, 0:NW * RC].rearrange("p (a t) -> p a t", a=NW),
                      ACT.Copy).then_inc(S["o_evac"], 1)
                need("s_evac", (l + 1) * (NRC + 1))
                act.dma_start(d["o_rp"][l], BD).then_inc(S["bd_out"], 16)
                act.dma_start(SR[0:64], d["rs"][l]).then_inc(S["sr_in"], 16)
                for g in range(6):
                    need("sq_mm", l * 6 + g + 1)
                    f(TQ[0:DEC, g], bank[g % 2][0:DEC, :], ACT.Copy).then_inc(S["sq_evac"], 1)
                need("sq_evac", l * 6 + 6)
                for g in range(6):
                    act.dma_start(RQ[0:64, g], TQ[0:DEC, g]).then_inc(S["rq_in"], 16)
                for e in range(12):
                    need("gate_mm", l * 24 + e + 1)
                    f(early_gate(e), bank[2 + e % 2][:, 0:T], ACT.Sigmoid).then_inc(S["gate_evac"], 1)
                need("sr_done", l + 1)
                act.dma_start(OT[0:DEC], OS[0:64]).then_inc(S["so_in"], 16)
                act.dma_start(d["o_rs"][l], SR[0:64]).then_inc(S["sr_out"], 16)
                need("ot_mm", l + 1)
                f(YR[:, :, SEQ:T], bank[0][:, 0:NW * DEC].rearrange("p (a t) -> p a t", a=NW), ACT.Copy)\
                    .then_inc(S["so_out"], 1)
                need("rq_in", 96 * (l + 1))
                f(HV["U1"], HG[:, 0:4, :], ACT.Sigmoid).then_inc(S["hg_sig"], 1)
                f(HV["FF"], HG[:, 4:8, :], ACT.Sigmoid).then_inc(S["hg_sig"], 1)
                need("gn_v", l + 1)
                for j in range(NW):
                    ins = f(T3[:, j, :], bank[2 + j][:, 0:T], ACT.Sqrt, scale=1.0 / RN, bias=com("leps"))
                ins.then_inc(S["gn_std"], 1)
                f(HV["QH"], HG[:, 12:16, :], ACT.Sigmoid).then_inc(S["hg_sig"], 1)
                for e in range(12, 16):
                    need("gate_mm", l * 24 + e + 1)
                    f(early_gate(e), bank[e % 2][:, 0:T], ACT.Sigmoid).then_inc(S["gate_evac"], 1)
                need("hg_in", l + 1)
                act.dma_start(SHA, d["hs"][l][:, 0:5]).then_inc(S["shs_in"], 16)
                act.dma_start(SHB, d["hs"][l][:, 5:DEC]).then_inc(S["shs_in"], 16)
                need("f_ready", l + 1)
                f(HV["BC"], HV["U1"], ACT.Ln).then_inc(S["f_ln"], 1)
                f(HV["KH"], HV["U2"], ACT.Ln).then_inc(S["f_ln"], 1)
                for e in range(16, 18):
                    need("gate_mm", l * 24 + e + 1)
                    f(early_gate(e), bank[e % 2][:, 0:T], ACT.Sigmoid).then_inc(S["gate_evac"], 1)
                need("b_ready", l + 1)
                f(HV["EB"], HV["BC"], ACT.Exp).then_inc(S["eb_done"], 1)
                for lev in range(1, LEV_H + 1):
                    need("lev_in", l * LEV_H + lev)
                    hx = HV[f"HX{lev % 2}"]
                    f(hx[:, :, 0:SEQ], hx[:, :, 0:SEQ], ACT.Exp).then_inc(S["lev_exp"], 1)
                need("kh_in", l + 1)
                f(HV["KH"][:, :, 0:SEQ], HV["KH"][:, :, 0:SEQ], ACT.Exp).then_inc(S["kh_exp"], 1)
                for g in range(4):
                    need("ht_mm", l * 4 + g + 1)
                    f((VT, KT)[g % 2][:, g // 2].rearrange("p a b -> p (a b)"), bank[2 + g][:, :], ACT.Copy)\
                        .then_inc(S["ht_evac"], 1)
                need("vs_mm", l + 1)
                need("at_add", 2 * LEV_H * (l + 1))
                f(VS[0:DEC].rearrange("p a b -> p (a b)"), bank[6][0:DEC, :], ACT.Copy).then_inc(S["vs_evac"], 1)
                for c in range(NHC):
                    need("hs_mm", l * 2 + c + 1)
                    f(YH[:, :, c * HC:(c + 1) * HC], bank[2][:, :].rearrange("p (a t) -> p a t", a=NW),
                      ACT.Copy).then_inc(S["ho_evac"], 1)
                need("hs_evac", l * 3 + 3)
                act.dma_start(d["o_hp"][l], SH).then_inc(S["h_out"], 16)
                need("hso_mm", l + 1)
                f(YH[:, :, SEQ:T], bank[6][:, 0:NW * DEC].rearrange("p (a t) -> p a t", a=NW), ACT.Copy)\
                    .then_inc(S["hso_evac"], 1)
                act.dma_start(d["o_hs"][l][:, 0:5], SHA).then_inc(S["h_out"], 16)
                act.dma_start(d["o_hs"][l][:, 5:DEC], SHB).then_inc(S["h_out"], 16)
                need("hn_mm", l + 1)
                for j in range(NW):
                    ins = f(HV["U2"][:, j, :], bank[2 + j][:, 0:T], ACT.Sqrt, scale=1.0 / P, bias=com("eps"))
                ins.then_inc(S["hn_std"], 1)
                need("sg_vm", l + 1)
                f(NRM[:], bank[1][:, 0:T], ACT.Sqrt, scale=1.0 / W, bias=com("eps")).then_inc(S["sg_std"], 1)
                need("sg_vn", l + 1)
                act.dma_start(d["o_sg"][l], VC[:, :, SEQ:T]).then_inc(S["sgo_out"], 16)
                for c in range(NHC):
                    need("sgt_mm", l * 2 + c + 1)
                    f(VT2[:, c].rearrange("p a b -> p (a b)"), bank[2 + c][:, :], ACT.Copy).then_inc(S["sgt_evac"], 1)
                for n in range(18, 24):
                    need("gate_mm", l * 24 + n + 1)
                    need("br_evac", l * 24 + n + 1)
                    f(GS[:, n % 2, :], bank[n % 2][:, 0:T], ACT.Sigmoid).then_inc(S["gate_evac"], 1)
                need("ffn_ss", l + 1)
                f(NRM[:], bank[0][:, 0:T], ACT.Sqrt, scale=1.0 / D_MODEL, bias=com("eps")).then_inc(S["ffn_std"], 1)
                for n in range(16):
                    need("q_mm", l * 16 + n + 1)
                    f(QT[:, n, :], bank[n % 2][:, 0:T], ACT.Copy).then_inc(S["q_evac"], 1)
                for n in range(12):
                    tc, m = n // 4, P if n < 8 else DEC
                    need("sc_mm", l * 12 + n + 1)
                    f(SC[tc][0:m, (n % 4) * 4:(n % 4) * 4 + 4].rearrange("p a b -> p (a b)"),
                      bank[4 + n % 2][0:m, :], ACT.Copy).then_inc(S["sc_evac"], 1)
                need("sc_evac", l * 12 + 12)
                act.dma_start(PKR[0:64], SC[2][0:DEC]).then_inc(S["packed_in"], 16)

                def down_hi(n, b, slot, turn, on):
                    act.wait_ge(dn_in[slot], (on + 1) * 16)
                    act.wait_ge(S["pre_mm"], turn + (l * NK + n + 1))
                    f(DHL[:, b, 0], ring[:, RAWD + slot].rearrange("p k e -> p (k e)"), ACT.Copy)\
                        .then_inc(S["dhi_done"], 1)

                def gelu(n, b, i, per, first):
                    act.wait_ge(S["pre_mm"], i * per + (l * NK + n + 3))
                    f(ACTS[:, bass.ds(i * per + (n - first), 1), :].rearrange("p a t -> p (a t)"), bank[b][:, 0:T],
                      ACT.Gelu).then_inc(S["gelu_done"], 1)

                def up_hi(g, b, turn, half_g, on):
                    act.wait_ge(up_in[b], (on + 1) * 16)
                    act.wait_ge(S["out_mm"], turn * KD + (l * 2 * NGRP + g + 1) * KD)
                    f(UHL[:, b, 0].rearrange("p a m -> p (a m)"),
                      ring[:, RAWU + 2 * b:RAWU + 2 * b + 2].rearrange("p s k m -> p (s k m)"), ACT.Copy)\
                        .then_inc(S["uhi_done"], 1)
                    f(AHL[:, b, 0], ACTS[:, bass.ds(turn * GRP + half_g * GRP, GRP), :], ACT.Copy)\
                        .then_inc(S["ahi_done"], 1)

                n4 = l * (NK // 4)
                for n in range(2):
                    down_hi(n, n, n, 0, n4)
                with act.Fori(0, HALF // 8 - 1) as i:
                    for b in range(8):
                        gelu(b, b % 2, i, 8, 0)
                        down_hi(b + 2, b % 2, (b + 2) % 4, i * 8, i * 2 + (n4 + (b + 2) // 4))
                for n in range(HALF - 8, HALF):
                    if n == HALF - 8:
                        for tc in range(3):
                            need("sm_in", l * 3 + tc + 1)
                            ga = EG[tc][2] if tc < 2 else SGA[0:64]
                            f(ga, ga, ACT.Exp).then_inc(S["sm_exp"], 1)
                    if n == HALF - 6:
                        need("gs_done", l + 1)
                        for k, src in enumerate((SE1, SE2, SGA)):
                            act.dma_start(EG[2][k][0:DEC].rearrange("p a b -> p (a b)"), src[0:64])\
                                .then_inc(S["packed_in"], 16)
                    gelu(n, n % 2, 0, 8, 0)
                    if n + 2 < HALF:
                        down_hi(n + 2, n % 2, (n + 2) % 4, 0, n4 + (n + 2) // 4)
                for hf in range(2):
                    need("g_evac", GB + (l * 2 + hf + 1) * NB)

                    def group(g, b, turn, i, more=True):
                        down0 = HALF + 2 * g
                        if hf == 0:
                            for c in range(2):
                                down_hi(down0 + c, c, (2 * b + c) % 4, turn * 2, i + (n4 + (down0 + c) // 4))
                        if more:
                            up_hi(hf * NGRP + g + 1, 1 - b, turn, g + 1, i + (l * NGRP + hf * (NGRP // 2) + (g + 1) // 2))
                        if hf == 0:
                            act.wait_ge(S["alo_done"], turn + (l * 2 * NGRP + g + 3))
                            for c in range(2):
                                gelu(down0 + c, c, i, 4, HALF)

                    up_hi(hf * NGRP, 0, 0, 0, l * NGRP + hf * (NGRP // 2))
                    with act.Fori(0, NGRP // 2 - 1) as i:
                        for b in range(2):
                            group(b, b, i * 2, i)
                    group(NGRP - 2, 0, 0, 0)
                    group(NGRP - 1, 1, 0, 0, False)
            need("mix_ss", DEPTH + 1)
            f(NRM[:], bank[0][:, 0:T], ACT.Sqrt, scale=1.0 / D_MODEL, bias=com("eps")).then_inc(S["mix_std"], 1)
            need("h_ready", DEPTH + 1)
            act.dma_start(d["o_y"], hT[:, :, 0:T]).then_inc(S["y_out"], 16)
            for n in ("shift_out", "bd_out", "sr_out", "sgo_out"):
                need(n, 16 * DEPTH)
            need("h_out", 48 * DEPTH)
            need("y_out", 16)

        @block.vector
        def _(dve):
            steps = [0]

            def need(name, n):
                dve.wait_ge(S[name], n)

            def step(ins):
                steps[0] += 1
                ins.then_inc(S["dve_step"], 1)
                dve.wait_ge(S["dve_step"], steps[0])

            def done(ins, name, n):
                ins.then_inc(S[name], 1)
                dve.wait_ge(S[name], n)

            def tt(out, a, b, op):
                return dve.tensor_tensor(out, a, b, op)

            def ts(out, a, s1, op0, s2=None, op1=ALU.bypass):
                if s2 is None:
                    return dve.tensor_scalar(out, a, s1, None, op0)
                return dve.tensor_scalar(out, a, s1, s2, op0, op1)

            def stt(out, a, s, b, op0, op1):
                return dve.scalar_tensor_tensor(out=out, in0=a, scalar=s, in1=b, op0=op0, op1=op1)

            def tiled(v, n, w=T):
                return over(v, w)

            def norm(l, g, std_name, std_n, ready, ready_n, sq_name, sq_n):
                done(tt(NSQ, xT[:], xT[:], ALU.mult), sq_name, sq_n)
                need(std_name, std_n)
                step(dve.reciprocal(NRM[:], NRM[:]))
                for k in range(KD):
                    ins = stt(hT[:, k, 0:T], xT[:, k, :], g(k), NRM[:], ALU.mult, ALU.mult)
                done(ins, ready, ready_n)

            dve.sem_inc(S["br_evac"], 2)
            dve.sem_inc(S["mg_add"], 1)
            dve.sem_inc(S["out_evac"], 4)
            dve.sem_inc(S["alo_done"], 2)
            dve.sem_inc(S["g_evac"], GB)
            need("par_in", 64)
            step(tt(LBS[:, 4], com("lb0"), com("lb1"), ALU.max))
            tt(LBS[:, 0], com("lb0"), LBS[:, 4], ALU.subtract)
            done(tt(LBS[:, 1], com("lb1"), LBS[:, 4], ALU.subtract), "lb_in", 1)
            need("lb_exp", 1)
            step(tt(LBS[:, 4], LBS[:, 2], LBS[:, 3], ALU.add))
            step(dve.reciprocal(LBS[:, 4], LBS[:, 4]))
            step(tt(LBS[:, 2:4], LBS[:, 2:4], rows(LBS[:, 4], 2), ALU.mult))
            step(tt(LBS[:, 5], LBS[:, 2], LBS[:, 3], ALU.add))
            tt(LBS[:, 4], LBS[:, 2], LBS[:, 2], ALU.subtract)
            step(tt(LBS[:, 5], LBS[:, 5], LBS[:, 2], ALU.subtract))
            step(ts(LBS[:, 4:6], LBS[:, 4:6], 0.0, ALU.max, 1.0, ALU.min))
            step(dve.memset(V1[:], 0.0))

            for l in range(DEPTH):
                norm(l, lambda k: par(l, "mix_g", k, k + 1), "mix_std", l + 1, "h_ready", l + 1, "mix_sq", l + 1)
                need("smalls_in", 16 * NSMALL * (l + 1))
                dve.memset(ZR[:, :, 0], 0.0)
                dve.memset(XV[0:32, 0:1], 0.0)
                step(tt(WST, WST, rows(cm("triu"), NW), ALU.mult))
                need("xv_evac", l + 1)
                tt(XVS[0:32, 0:SEQ], XV[0:32, 0:SEQ], XV[0:32, 1:SEQ + 1], ALU.subtract)
                step(tt(XVS[0:32, SEQ:T], XV[0:32, T + 1:ZR_W], XV[0:32, SEQ + 1:T + 1], ALU.subtract))
                done(stt(XVS[0:32], XVS[0:32], par(l, "vmu")[0:32], XV[0:32, 1:T + 1], ALU.mult, ALU.add),
                     "zs_ready", 2 * l + 1)
                need("z_evac", 2 + l * 38 + RT)
                tt(D[:, :, 0:SEQ], ZR[:, :, 0:SEQ], ZR[:, :, 1:SEQ + 1], ALU.subtract)
                step(tt(D[:, :, SEQ:T], ZR[:, :, T + 1:ZR_W], ZR[:, :, SEQ + 1:T + 1], ALU.subtract))
                step(tt(D, D, over(par(l, "mu"), T), ALU.mult))
                done(tt(D, D, ZR[:, :, 1:T + 1], ALU.add), "zs_ready", 2 * l + 2)
                R, K, V = D[:, 0:4, :], D[:, 4:8, :], D[:, 8:12, :]
                need("lora_evac", l * 16 + 4)
                step(ts(SW, SW, -float(np.exp(-0.5)), ALU.mult))
                for j in range(NW):
                    ins = dve.tensor_tensor_scan(CU[:, j, :], cm("rscan"), SW[:, j, :], 0.0, ALU.mult, ALU.add)
                step(ins)
                done(tt(T2, CU, SW, ALU.subtract), "decay_in", l + 1)
                need("lora_evac", l * 16 + 12)
                step(ts(VG, VG, par(l, "on"), ALU.mult))
                step(ts(V1[:], V1[:], par(l, "on"), ALU.mult))
                for j in range(NW):
                    ins = stt(V1[:, j], V[:, j], par(l, "off"), V1[:, j], ALU.mult, ALU.add)
                step(ins)
                step(tt(KK, V1[:], V, ALU.subtract))
                step(tt(KK, KK, VG, ALU.mult))
                step(tt(V, V, KK, ALU.add))

                def chunked(x):
                    return x[:, :, 0:SEQ].rearrange("p j (n t) -> p j n t", t=RC)

                def slot(g):
                    return BKV[:, :, g, :].rearrange("p (j n) t -> p j n t", j=NW)

                dve.tensor_copy(slot(2), chunked(V))
                step(tt(KK, K, over(par(l, "kk"), T), ALU.mult))
                done(tt(T3, KK, KK, ALU.mult), "kk_sq", l + 1)
                step(ts(SW, AA, -1.0, ALU.add))
                step(tt(SW, SW, over(par(l, "ka"), T), ALU.mult))
                for j in range(NW):
                    ins = stt(K[:, j], SW[:, j], 1.0, K[:, j], ALU.add, ALU.mult)
                step(ins)
                step(tt(SW, R, K, ALU.mult))
                done(tt(SW, SW, over(par(l, "rk"), T), ALU.mult), "prep_done", l + 1)
                need("kk_std", l + 1)
                step(ts(T3, T3, 1e-12, ALU.max))
                step(dve.reciprocal(T3, T3))
                step(tt(KK, KK, T3, ALU.mult))
                need("decay_out", 3 * l + 3)
                tt(AR[:, :, 1, :], R, EC, ALU.mult)
                step(ts(T3, KK, -1.0, ALU.mult))
                step(tt(KK, KK, AA, ALU.mult))
                step(tt(AR[:, :, 0, :], T3, T1, ALU.mult))
                tt(slot(0), chunked(KK), chunked(T2), ALU.mult)
                step(tt(slot(1), chunked(K), chunked(T2), ALU.mult))
                for g, src in enumerate((T3, KK, K, R, EC, V)):
                    ins = dve.tensor_copy(SQ[:, g], src[:, :, SEQ:T])
                step(ins)
                need("bon_mm", l + 1)
                for j in range(NW):
                    ins = tt(BO[:, j, :], bank[2 + j][:, 0:T], V[:, j, :], ALU.mult)
                done(ins, "bon_done", l + 1)
                for g in range(2 * NRC):
                    need("mat_mm", l * 8 + g + 1)
                    ins = tt(M[:, 4 * g:4 * g + 4, :], bank[g % 4][:, :].rearrange("p (a b) -> p a b", a=NW),
                             rows(cm("rw"), NW), ALU.mult)
                    ins.then_inc(S["mat_evac"], 1)
                need("mat_evac", l * 8 + 8)
                for half in range(2):
                    need("l_mm", l * 2 + half + 1)
                    Lv = L_[0:RC].rearrange("p (n q j) s -> p n q (j s)", n=2, q=2)
                    for pr in range(2):
                        ins = tt(Lv[:, :, pr].rearrange("p n (j s) -> p n j s", j=NW),
                                 bank[4 + pr][0:RC, :].rearrange("p (n j s) -> p n j s", n=2, j=NW),
                                 cm("low")[0:RC].rearrange("p (a b s) -> p a b s", a=1, b=1)
                                 .broadcast_to([RC, 2, NW, RC]), ALU.mult)
                    done(ins, "l_evac", l * 2 + half + 1)
                    XH = XT_[0:RC, 16 * half:16 * half + 16, :]
                    I16 = rows(ident[0:RC, 0:RC], 16)
                    step(tt(X_[0:RC], L_[0:RC], rows(cm("lev", 0, RC)[0:RC], 16), ALU.mult))
                    tt(X_[0:RC], X_[0:RC], I16, ALU.add)
                    step(tt(XH, M[0:RC, 16 * half:16 * half + 16, 0:RC], rows(cm("n0")[0:RC], 16), ALU.mult))
                    step(tt(XH, XH, I16, ALU.add))
                    for lev in range(1, LEV_R):
                        e = (l * 2 + half) * (LEV_R - 1) + lev
                        done(tt(ML[0:RC], L_[0:RC], rows(cm("lev", RC * lev, RC)[0:RC], 16), ALU.mult), "x_in2", e)
                        need("x_mm", e)
                        for b in range(2):
                            c = slice(8 * b, 8 * b + 8)
                            xh = XT_[0:RC, 16 * half + 8 * b:16 * half + 8 * b + 8, :]
                            tt(xh, xh, bank[2 + b][0:RC, :].rearrange("p (a b) -> p a b", a=8), ALU.add)
                            ins = tt(X_[0:RC, c], X_[0:RC, c], bank[6 + b][0:RC, :].rearrange("p (a b) -> p a b", a=8),
                                     ALU.add)
                        step(ins)
                ins = dve.memset(BD, 0.0)
                done(ins, "s_evac", l * (NRC + 1) + 1)
                dve.memset(TT_, 0.0).then_inc(S["x_done"], 1)
                for n in range(NRC):
                    e = l * NRC + n + 1
                    need("y_mm", e)
                    step(dve.tensor_copy(YSC[0:RC], bank[4][0:RC, :]))
                    done(tt(YSC[0:RC], YSC[0:RC], bank[5][0:RC, :], ALU.add), "y_evac", e)
                    need("s_mm", e)
                    step(tt(TT_.rearrange("p (a b) -> p a b", a=NW), bank[7][:, :].rearrange("p (a b) -> p a b", a=NW),
                            rows(bones, NW), ALU.mult))
                    step(tt(BD, BD, TT_.rearrange("p (a b) -> p a b", a=NW), ALU.add))
                    done(tt(BD, BD, over(EC[:, :, (n + 1) * RC - 1], P), ALU.mult), "s_evac", e + l + 1)
                need("sr_in", 16 * (l + 1))
                need("rq_in", 96 * (l + 1))
                nkk, kka, k2, r, w, v = (RQ[0:64, g] for g in range(6))
                S64, T64 = SR[0:64], TR[0:64]
                step(tt(T64, S64, rows(nkk, RN), ALU.mult))
                step(dve.tensor_reduce(SA[0:64], T64, AX.X, ALU.add))
                step(tt(S64, S64, rows(w, RN), ALU.mult))
                step(tt(T64, over(SA[0:64], RN), rows(kka, RN), ALU.mult))
                step(tt(S64, S64, T64, ALU.add))
                step(tt(T64, over(v, RN), rows(k2, RN), ALU.mult))
                step(tt(S64, S64, T64, ALU.add))
                step(tt(T64, S64, rows(r, RN), ALU.mult))
                done(dve.tensor_reduce(OS[0:64], T64, AX.X, ALU.add), "sr_done", l + 1)
                need("gn_sq", l + 1)
                for j in range(NW):
                    ins = stt(YR[:, j], bank[2 + j][:, 0:T], -1.0 / RN, YR[:, j], ALU.mult, ALU.add)
                step(ins)
                done(tt(at(WORK + 1056, NW, T), YR, YR, ALU.mult), "gn_m", l + 1)
                need("hg_sig", 3 * l + 2)
                FF, U1, U2, BC, EB, KH, QH = (HV[n] for n in ("FF", "U1", "U2", "BC", "EB", "KH", "QH"))
                tt(HG[:, 0:4, :], HG[:, 0:4, :], U1, ALU.mult)
                lbl = LBS[:, 4 + l]
                step(ts(SC8[:, 0:4], lbl, -1.0, ALU.mult, 1.0, ALU.add))
                step(tt(FF, FF, over(SC8[:, 0:4], T), ALU.mult))
                step(tt(FF, FF, over(lbl, T), ALU.add))
                ts(HG[:, 4:8, :], FF, -1.0, ALU.mult, 1.0, ALU.add)
                step(ts(FF, FF, 1e-30, ALU.max))
                need("gn_std", l + 1)
                step(dve.reciprocal(T3, T3))
                step(tt(YR, YR, T3, ALU.mult))
                step(tt(YR, YR, over(par(l, "lg"), T), ALU.mult))
                step(tt(YR, YR, over(par(l, "lb"), T), ALU.add))
                step(tt(YR, YR, BO, ALU.add))
                done(tt(YR, YR, GG, ALU.mult), "yr_done", 2 * l + 1)
                need("hg_sig", 3 * (l + 1))
                need("sr_out", 16 * (l + 1))
                need("bd_out", 16 * (l + 1))
                done(dve.memset(HV["HX0"], 0.0), "hg_in", l + 1)
                ts(U1, FF, 2.0 ** -60, ALU.max)
                done(ts(U2, FF, 2.0 ** 60, ALU.mult, 1.0, ALU.min), "f_ready", l + 1)
                tt(HG[:, 12:16, :], HG[:, 12:16, :], QH, ALU.mult)
                need("f_ln", 2 * (l + 1))
                step(tt(U1, BC, KH, ALU.add))
                for j in range(NW):
                    ins = dve.tensor_tensor_scan(BC[:, j, :], cm("hscan"), U1[:, j, :], 0.0, ALU.mult, ALU.add)
                done(ins, "b_ready", l + 1)
                need("eb_done", l + 1)
                tt(QH, HG[:, 0:4, :], EB, ALU.mult).then_inc(S["lev_x"], 1)
                for c in range(NHC):
                    cc = slice(c * HC, (c + 1) * HC)
                    ins = tt(KH[:, :, cc], over(BC[:, :, (c + 1) * HC - 1], HC), BC[:, :, cc], ALU.subtract)
                ins.then_inc(S["kh_in"], 1)

                def cut(ap, b):
                    return ap.rearrange("p a (n b) -> p a n b", b=b)

                def att(lev):
                    for c in range(NHC):
                        e = l * 2 * (LEV_H + 1) + 2 * lev + c + 1
                        need("att_mm", e)
                        src = bank[c][:, :].rearrange("p (a b) -> p a b", a=NW)
                        if lev == 0:
                            done(tt(AT_[:, c], src, rows(cm("hg", P * LEV_H, P), NW), ALU.mult), "att_evac", e)
                        else:
                            if lev > 1:
                                need("at_add", l * 2 * LEV_H + 2 * (lev - 2) + c + 1)
                            done(tt((T5, VS)[c], src, rows(cm("hg", P * (lev - 1), P), NW), ALU.mult), "att_evac", e)

                for lev in range(1, LEV_H + 1):
                    hx = HV[f"HX{lev % 2}"]
                    b = 1 << (lev - 1)
                    for j in range(NW):
                        bc = BC[:, j, 0:SEQ].rearrange("p (n b) -> p n b", b=2 * b)
                        hh = hx[:, j, 0:SEQ].rearrange("p (n b) -> p n b", b=2 * b)
                        ref = bc[:, :, b - 1:b].broadcast_to([P, SEQ // (2 * b), b])
                        tt(hh[:, :, 0:b], ref, bc[:, :, 0:b], ALU.subtract)
                        ins = tt(hh[:, :, b:2 * b], bc[:, :, b:2 * b], ref, ALU.subtract)
                    ins.then_inc(S["lev_in"], 1)
                    att(lev - 1)
                    need("lev_exp", l * LEV_H + lev)
                    for j in range(NW):
                        hh = hx[:, j, 0:SEQ].rearrange("p (n b) -> p n b", b=2 * b)
                        kk_ = HG[:, 4 + j, 0:SEQ].rearrange("p (n b) -> p n b", b=2 * b)
                        qq = HG[:, j, 0:SEQ].rearrange("p (n b) -> p n b", b=2 * b)
                        tt(hh[:, :, 0:b], hh[:, :, 0:b], kk_[:, :, 0:b], ALU.mult)
                        ins = tt(hh[:, :, b:2 * b], hh[:, :, b:2 * b], qq[:, :, b:2 * b], ALU.mult)
                    ins.then_inc(S["lev_x"], 1)
                att(LEV_H)
                need("kh_exp", l + 1)
                done(tt(KH[:, :, 0:SEQ], KH[:, :, 0:SEQ], HG[:, 4:8, 0:SEQ], ALU.mult), "kh_done", l + 1)
                done(dve.memset(SH, 0.0), "hs_evac", 3 * l + 1)
                for c in range(NHC):
                    need("hs_mm", 2 * l + c + 1)
                    step(tt(SH, SH, over(EB[:, :, (c + 1) * HC - 1], P), ALU.mult))
                    done(tt(SH, SH, bank[3][:, :].rearrange("p (a b) -> p a b", a=NW), ALU.add), "hs_evac", 3 * l + c + 2)
                need("shs_in", 32 * (l + 1))
                need("at_add", 2 * LEV_H * (l + 1))
                for b in range(DEC):
                    need("vb_mm", l * DEC + b + 1)
                    tt(shs(b), shs(b), over(EB[:, :, SEQ + b], P), ALU.mult)
                    step(tt(T5, bank[4 + b % 2][:, :].rearrange("p (a b) -> p a b", a=NW),
                            over(HG[:, 4:8, SEQ + b], P), ALU.mult))
                    done(tt(shs(b), shs(b), T5, ALU.add), "vb_evac", l * DEC + b + 1)
                need("ho_evac", 2 * (l + 1))
                need("hso_evac", l + 1)
                done(tt(U1, YH, YH, ALU.mult), "hn_sq", l + 1)
                need("sg_mm", l + 1)
                for j in range(NW):
                    ins = stt(VC[:, j], bank[0][:, 0:T], -1.0 / W, SG[:, NW + j], ALU.mult, ALU.add)
                step(ins)
                done(tt(VQ, VC, VC, ALU.mult), "sg_mu", l + 1)
                need("sg_std", l + 1)
                step(dve.reciprocal(NRM[:], NRM[:]))
                step(tt(VC, VC, rows(NRM[:], NW), ALU.mult))
                step(tt(VC, VC, over(par(l, "sg"), T), ALU.mult))
                done(tt(VC, VC, over(par(l, "sb"), T), ALU.add), "sg_vn", l + 1)
                need("hn_std", l + 1)
                step(dve.reciprocal(U2, U2))
                step(tt(YH, YH, U2, ALU.mult))
                step(tt(YH, YH, over(par(l, "hg"), T), ALU.mult))
                done(tt(YH, YH, HG[:, 12:16, :], ALU.mult), "yr_done", 2 * l + 2)
                need("mx_mm", l + 1)
                for c in range(NHC):
                    cc = slice(c * HC, (c + 1) * HC)
                    tt(YS[:, :, cc], bank[4 + c][:, :].rearrange("p (a b) -> p a b", a=NW), SG[:, 0:4, cc], ALU.mult)
                step(dve.tensor_copy(SC8, bank[6][:, 0:8]))
                step(tt(YS[:, :, SEQ:T], VC[:, :, SEQ:T], over(SC8[:, 0:4], DEC), ALU.mult))
                step(tt(YS[:, :, SEQ:T], YS[:, :, SEQ:T], over(SC8[:, 4:8], DEC), ALU.add))
                done(tt(YS[:, :, SEQ:T], YS[:, :, SEQ:T], SG[:, 0:4, SEQ:T], ALU.mult), "mx_evac", l + 1)
                for n in range(24):
                    if n == 0 or n >= 18:
                        need("gate_evac", l * 24 + max(n, 17) + 3)
                    need("br_mm", l * 24 + n + 1)
                    mg, src = MG[:, n // 3, :], bank[2 + n % 2][:, 0:T]
                    gate = early_gate(n) if n < 18 else GS[:, n % 2, :]
                    if n % 3 == 0:
                        tt(mg, src, gate, ALU.mult).then_inc(S["br_evac"], 1)
                    else:
                        need("mg_add", l * 16 + n - n // 3)
                        tt(PR, src, gate, ALU.mult).then_inc(S["br_evac"], 1)
                        need("br_evac", l * 24 + n + 3)
                        tt(mg, mg, PR, ALU.add).then_inc(S["mg_add"], 1)
                need("br_evac", 2 + 24 * (l + 1))
                need("mg_add", 1 + 16 * (l + 1))
                done(dve.memset(PR, 0.0), "mg_done", l + 1)
                for m in range(KD):
                    need("wo_mm", l * 8 + m + 1)
                    ins = tt(xT[:, m, :], xT[:, m, :], bank[m][:, 0:T], ALU.add)
                    ins.then_inc(S["wo_evac"], 1)
                need("wo_evac", 8 * (l + 1))
                need("h_out", 48 * (l + 1))
                for n in ("shift_out", "sgo_out"):
                    need(n, 16 * (l + 1))
                norm(l, lambda k: par(l, "ffn_g", k, k + 1), "ffn_std", l + 1, "h2_ready", l + 1, "ffn_sq", l + 1)
                step(dve.tensor_copy(HHL[:, 0], hT[:, :, 0:T]))
                done(tt(HHL[:, 1], hT[:, :, 0:T], HHL[:, 0].bitcast(F32), ALU.subtract), "hlo_done", l + 1)
                for tc in range(3):
                    m, nh = (P, PH) if tc < 2 else (64, 1)
                    if tc < 2:
                        need("sc_evac", l * 12 + 4 * tc + 4)
                        e1, e2, ga = (EG[tc][k] for k in range(3))
                    else:
                        need("packed_in", 64 * l + 16)
                        e1, e2, ga = (v[0:64].rearrange("p (a b) -> p a b", a=1) for v in (SE1, SE2, SGA))
                    sv, si, cv, ci = SV[0:m, 0:nh], SI[0:m, 0:nh], CV[0:m, 0:nh], CI[0:m, 0:nh]
                    for h in range(nh):
                        for p in range(2):
                            top16(dve, step, SC[tc][:, 2 * h + p] if tc < 2 else PKR[0:64, p],
                                  sv[:, h, p], si[:, h, p].bitcast(U32))
                    step(dve.tensor_copy(si, si.bitcast(U32)))
                    for h in range(nh):
                        step(tt(COMB[0:m, h], over(sv[:, h, 0], TOPK), rows(sv[:, h, 1], TOPK), ALU.add))
                        top16(dve, step, COMB[0:m, h].rearrange("p a b -> p (a b)"), cv[:, h], ci[:, h].bitcast(U32))
                    ts(e1.bitcast(U32), ci.bitcast(U32), 4, ALU.logical_shift_right)
                    step(ts(e2.bitcast(U32), ci.bitcast(U32), 15, ALU.bitwise_and))
                    dve.tensor_copy(e1, e1.bitcast(U32))
                    step(dve.tensor_copy(e2, e2.bitcast(U32)))
                    oh = COMB[0:m, 0:nh].rearrange("p a b c -> p (a b) c")
                    for p, e in enumerate((e1, e2)):
                        ef = e.rearrange("p a b -> p (a b)")
                        step(tt(oh, over(ef, TOPK), rows(cp("iota16")[0:m], nh * TOPK), ALU.is_equal))
                        for h in range(nh):
                            hr = slice(h * TOPK, (h + 1) * TOPK)
                            ins = tt(oh[:, hr], oh[:, hr], rows(si[:, h, p], TOPK), ALU.mult)
                        step(ins)
                        step(dve.tensor_reduce(ef, oh, AX.X, ALU.add))
                    done(tt(ga, cv, cv[:, :, 0:1].broadcast_to([m, nh, TOPK]), ALU.subtract), "sm_in", l * 3 + tc + 1)
                need("sm_exp", l * 3 + 3)
                for tc in (2, 0, 1):
                    m, nh = (P, PH) if tc < 2 else (64, 1)
                    ga = EG[tc][2] if tc < 2 else SGA[0:64].rearrange("p (a b) -> p a b", a=1)
                    step(dve.tensor_reduce(SM[0:m, 0, 0:nh], ga, AX.X, ALU.add))
                    step(dve.reciprocal(SM[0:m, 1, 0:nh], SM[0:m, 0, 0:nh]))
                    ins = tt(ga, ga, over(SM[0:m, 1, 0:nh], TOPK), ALU.mult)
                    if tc == 2:
                        done(ins, "gs_done", l + 1)
                    elif tc == 0:
                        step(ins)
                    else:
                        done(ins, "e_ready", l + 1)
                need("et_mm", l + 1)
                for tc in range(3):
                    m = P if tc < 2 else DEC
                    tcc = slice(tc * P, tc * P + m)
                    for k in range(2):
                        dve.tensor_copy(ET[:, k, tcc], bank[2 + tc][:, k * P:k * P + m])
                    gate = bank[2 + tc][:, 2 * P:2 * P + m]
                    step(dve.tensor_copy(GP[:, 0, tcc], gate))
                    step(tt(RES[:, tcc], gate, GP[:, 0, tcc], ALU.subtract))
                    step(dve.tensor_copy(GP[:, 1, tcc], RES[:, tcc]))
                    step(tt(RES[:, tcc], RES[:, tcc], GP[:, 1, tcc], ALU.subtract))
                    ins = dve.tensor_copy(GP[:, 2, tcc], RES[:, tcc])
                done(ins, "et_evac", l + 1)
                for hf in range(2):
                    step(dve.tensor_copy(IOTA[:], over(cp("iota"), TB)))
                    nb = (l * 2 + hf) * NB

                    def one_hot(n, b, turn):
                        tok = bass.ds(turn * TB + n * TB, TB)
                        tt(OHE[:, b], rows(ET[:, 1, tok], HALF), IOTA[:, hf * HALF:(hf + 1) * HALF], ALU.is_equal)\
                            .then_inc(S["oe_ready"], 1)
                        tt(OH1[:, b], rows(ET[:, 0, tok], NK), IOTA[:], ALU.is_equal)
                        dve.wait_ge(S["oe_ready"], turn + (nb + n + 1))
                        tt(OH2[:, b, 0], OHE[:, b], rows(GP[:, 0, tok], HALF), ALU.mult).then_inc(S["oh1_ready"], 1)

                    def gated(n, b, turn):
                        dve.wait_ge(S["g_mm"], turn + (nb + n + 1 + GB))
                        a = ACTS[:, :, bass.ds(turn * TB + n * TB, TB)].rearrange("p e t -> p t e")
                        tt(a, a, bank[4 + b][:, :].rearrange("p (t e) -> p t e", t=TB), ALU.mult)\
                            .then_inc(S["g_evac"], 1)

                    for n in range(GB):
                        one_hot(n, n, 0)
                    need("gelu_done", 2 + l * NK + (hf + 1) * HALF)
                    with dve.Fori(0, NB // GB - 1) as i:
                        for b in range(GB):
                            gated(b, b, i * GB)
                            one_hot(GB + b, b, i * GB)
                    for n in range(NB - 1 - GB, NB):
                        gated(n, n % GB, 0)
                        if n + GB < NB:
                            one_hot(n + GB, n % GB, 0)

                    def low(g, b, turn):
                        G = l * 2 * NGRP + hf * NGRP + g
                        dve.wait_ge(S["ahi_done"], turn + (G + 1))
                        tt(UHL[:, b, 1, 0], ring[:, RAWU + 2 * b].rearrange("p k m -> p (k m)"),
                           UHL[:, b, 0, 0].bitcast(F32), ALU.subtract)
                        tt(AHL[:, b, 1], ACTS[:, bass.ds(turn * GRP + g * GRP, GRP), :], AHL[:, b, 0].bitcast(F32),
                           ALU.subtract).then_inc(S["alo_done"], 1)

                    def gather(g, ks, turn):
                        for k in ks:
                            n = (l * 2 * NGRP + hf * NGRP + g) * KD + k
                            dve.wait_ge(S["out_mm"], turn * KD + (n + 1 + 2 * KD))
                            tt(xT[:, k, :], xT[:, k, :], bank[2 + k % 4][:, 0:T], ALU.add).then_inc(S["out_evac"], 1)

                    need("g_evac", GB + nb + NB)
                    low(0, 0, 0)
                    with dve.Fori(0, NGRP // 2 - 1) as i:
                        for b in range(2):
                            gather(b, range(0, 4), i * 2)
                            low(b + 1, 1 - b, i * 2)
                            gather(b, range(4, 8), i * 2)
                    gather(NGRP - 2, range(0, 4), 0)
                    low(NGRP - 1, 1, 0)
                    gather(NGRP - 2, range(4, 8), 0)
                    gather(NGRP - 1, range(KD), 0)
                need("out_evac", 4 + (l + 1) * 2 * NGRP * KD)
                dve.sem_inc(S["arena_free"], 1)
            norm(0, lambda k: com("fin_g", k, k + 1), "mix_std", DEPTH + 1, "h_ready", DEPTH + 1, "mix_sq", DEPTH + 1)

        @block.gpsimd
        def _(pool):
            pool.sem_inc(S["dlo_done"], 4)
            pool.sem_inc(S["ulo_done"], 2)

            for l in range(DEPTH):
                for lev in range(1, LEV_H + 1):
                    for c in range(NHC):
                        pool.wait_ge(S["att_evac"], l * 2 * (LEV_H + 1) + 2 * lev + c + 1)
                        if lev > 1:
                            pool.wait_ge(S["at_add"], l * 2 * LEV_H + 2 * (lev - 2) + c + 1)
                        pool.tensor_tensor(AT_[:, c], AT_[:, c], (T5, VS)[c], ALU.add).then_inc(S["at_add"], 1)

                def down_lo(n, b, slot, turn):
                    pool.wait_ge(S["dhi_done"], turn + (l * NK + n + 1))
                    pool.tensor_tensor(DHL[:, b, 1], ring[:, RAWD + slot].rearrange("p k e -> p (k e)"),
                                       DHL[:, b, 0].bitcast(F32), ALU.subtract).then_inc(S["dlo_done"], 1)

                def up_lo(g, b, turn):
                    pool.wait_ge(S["uhi_done"], turn + (l * 2 * NGRP + g + 1))
                    pool.tensor_tensor(UHL[:, b, 1, 1], ring[:, RAWU + 2 * b + 1].rearrange("p k m -> p (k m)"),
                                       UHL[:, b, 0, 1].bitcast(F32), ALU.subtract).then_inc(S["ulo_done"], 1)

                with pool.Fori(0, HALF // 4) as i:
                    for b in range(4):
                        down_lo(b, b % 2, b, i * 4)
                pool.wait_ge(S["et_evac"], l + 1)
                for hf in range(2):
                    if hf:
                        pool.wait_ge(S["out_mm"], 2 * KD + (l * 2 + 1) * NGRP * KD)
                    nb = (l * 2 + hf) * NB

                    def one_hot(n, b, turn):
                        pool.wait_ge(S["g_mm"], turn + (nb + n + 1))
                        pool.wait_ge(S["oe_ready"], turn + (nb + n + 1))
                        for q in range(1, 3):
                            gate = rows(GP[:, q, bass.ds(turn * TB + n * TB, TB)], HALF)
                            ins = pool.tensor_tensor(OH2[:, b, q], OHE[:, b], gate, ALU.mult)
                        ins.then_inc(S["oh_ready"], 1)

                    with pool.Fori(0, NB // GB) as i:
                        for b in range(GB):
                            one_hot(b, b, i * GB)
                    one_hot(NB - 1, 0, 0)

                    def group(g, b, turn, more=True):
                        if hf == 0:
                            for c in range(2):
                                down_lo(HALF + 2 * g + c, c, (2 * b + c) % 4, turn * 2)
                        if more:
                            up_lo(hf * NGRP + g + 1, 1 - b, turn)

                    up_lo(hf * NGRP, 0, 0)
                    with pool.Fori(0, NGRP // 2 - 1) as i:
                        for b in range(2):
                            group(b, b, i * 2)
                    group(NGRP - 2, 0, 0)
                    group(NGRP - 1, 1, 0, False)


def top16(dve, step, scores, values, index):
    step(dve.max(values[:, 0:8], scores))
    dve.max_index(index[:, 0:8], values[:, 0:8], scores)
    step(dve.match_replace(scores, values[:, 0:8], scores, -3.0e38))
    step(dve.max(values[:, 8:16], scores))
    step(dve.max_index(index[:, 8:16], values[:, 8:16], scores))


INS = ["x", "cp", "cm", "par", "com", "w2a2", "g2", "vw1", "vw2", "wst", "sb", "sh", "wm", "down", "up", "rs", "hs"]
OUTS = {"o_y": (P, KD, T), "o_shift": (DEPTH, P, KD, DEC + 1), "o_rp": (DEPTH, P, NW, P),
        "o_rs": (DEPTH, DEC * RH, RN, RN), "o_hp": (DEPTH, P, NW, P), "o_hs": (DEPTH, P, DEC, NW, P),
        "o_sg": (DEPTH, P, NW, DEC)}


def lay_out(a):
    def col(v):
        return v.reshape(-1, P).T

    def wtile(w, k):
        return w.reshape(k, P, -1, P).transpose(2, 1, 0, 3)

    f = np.float32
    z32 = np.zeros((96,), f)
    out = {"x": np.concatenate([a["x_prompt"][0], a["x_sample"][:, 0]], 0).T.reshape(KD, P, T).transpose(1, 0, 2)}
    out["cp"], out["cm"] = masks()
    par = []
    for l in range(DEPTH):
        vmu = a["vres_mu"][l - 1] if l else np.zeros(32, f)
        v0 = a["vres_v0"][l - 1] if l else np.zeros(W, f)
        cols = {"mix_g": a["norm_mix_g"][l], "ffn_g": a["norm_ffn_g"][l], "mu": a["shift_mu"][l],
                "w0": a["rwkv_w0"][l], "a0": a["rwkv_a0"][l], "kk": a["rwkv_kk"][l], "ka": a["rwkv_ka"][l],
                "rk": a["rwkv_rk"][l].reshape(-1), "lg": a["rwkv_lnx_g"][l], "lb": a["rwkv_lnx_b"][l],
                "vmu": np.concatenate([vmu, z32]), "v0": v0, "hg": a["hgrn_norm_g"][l], "sg": a["sgu_ln_g"][l],
                "sb": a["sgu_ln_b"][l], "on": np.full(P, float(l > 0), f), "off": np.full(P, float(l == 0), f)}
        par.append(np.concatenate([col(cols[n]) for n, _ in PARS], 1))
    out["par"] = np.stack(par, 1)
    out["com"] = np.concatenate([col(a["hgrn_lb"][0]), col(a["hgrn_lb"][1]), col(a["norm_final_g"]),
                                 np.full((P, 1), EPS, f), np.full((P, 1), LNX_EPS, f)], 1)
    out["w2a2"] = np.concatenate([a["rwkv_w2"], a["rwkv_a2"]], 1)
    out["g2"] = a["rwkv_g2"]
    z = np.zeros((1, D_MODEL, 32), f)
    out["vw1"] = np.concatenate([z, a["vres_w1"]], 0).reshape(DEPTH, KD, P, 32).transpose(0, 2, 1, 3)
    out["vw2"] = np.concatenate([np.zeros((1, 32, W), f), a["vres_w2"]], 0)
    out["wst"] = a["sgu_ws"].transpose(0, 3, 1, 2)
    out["sb"] = a["sgu_b"].reshape(DEPTH, 1, NW, P)
    out["sh"] = a["state_shift"].transpose(0, 2, 1).reshape(DEPTH, KD, P, DEC).transpose(0, 2, 1, 3)
    wm = []
    for l in range(DEPTH):
        win = wtile(a["w_in"][l], KD).reshape(-1, P, D_MODEL)
        gates = win[38:].reshape(3, KD, P, D_MODEL)
        br = np.stack([wtile(a[n][l], NW) for n in ("w_branch_rwkv", "w_branch_hgrn", "w_branch_sgu")])
        rows_ = [win[:38]]
        gate, branch = [], []
        for mp in range(4):
            gate.append(gates[:, 2 * mp:2 * mp + 2].transpose(1, 0, 2, 3).reshape(6, P, D_MODEL))
            b = br[:, 2 * mp:2 * mp + 2].transpose(1, 0, 2, 3, 4).reshape(3, 2, P, W)
            branch.append(b.transpose(0, 2, 1, 3).reshape(3, P, D_MODEL))
        rows_ += gate[:3] + branch[:3] + [branch[3][:1], gate[3][:2], branch[3][1:], gate[3][2:]]
        rows_.append(wtile(a["w_out"][l], KD).reshape(-1, P, D_MODEL))
        keys = a["peer_keys"][l].reshape(2 * PH, NK, P).transpose(2, 0, 1).reshape(P, 2, D_MODEL)
        rows_.append(wtile(a["peer_wq"][l], KD).reshape(-1, P, D_MODEL))
        rows_.append(keys.transpose(1, 0, 2))
        wm.append(np.concatenate(rows_, 0))
    out["wm"] = np.stack(wm)
    out["down"] = a["peer_down"].reshape(DEPTH, P, NK, KD, P).transpose(0, 2, 4, 3, 1).reshape(DEPTH, NK, P, D_MODEL)
    out["up"] = a["peer_up"].reshape(DEPTH, P, NK, D_MODEL)
    out["rs"] = a["state_rwkv"].reshape(DEPTH, DEC * RH, RN, RN)
    out["hs"] = a["state_hgrn"].transpose(0, 3, 1, 2, 4)
    return {n: np.ascontiguousarray(v) for n, v in out.items()}


def kernel(**inputs):
    import concourse.bacc as bacc
    from concourse.bass_utils import run_bass_kernel_spmd

    arrays = lay_out({n: np.asarray(v) for n, v in inputs.items()})
    nc = bacc.Bacc("TRN2", target_bir_lowering=False, num_devices=1)
    d = {n: nc.dram_tensor(n, arrays[n].shape, F32, kind="ExternalInput").ap() for n in INS}
    for n, shape in OUTS.items():
        d[n] = nc.dram_tensor(n, shape, F32, kind="ExternalOutput").ap()
    build(nc, d)
    r = run_bass_kernel_spmd(nc, [{n: arrays[n] for n in INS}], core_ids=[0]).results[0]
    y = r["o_y"].transpose(2, 1, 0).reshape(T, D_MODEL)
    sh = r["o_shift"].transpose(0, 3, 2, 1).reshape(DEPTH, DEC + 1, D_MODEL)
    rp = r["o_rp"].reshape(DEPTH, 2, RN, NW, 2, RN)
    rp = np.stack([rp[:, 0, :, :, 0], rp[:, 1, :, :, 1]], 3)
    rp = rp.transpose(0, 2, 3, 4, 1).reshape(DEPTH, 1, RH, RN, RN)
    return (y[None, :SEQ], y[SEQ:, None], sh[:, 0:1], sh[:, 1:], rp,
            r["o_rs"].reshape(DEPTH, DEC, RH, RN, RN),
            r["o_hp"].transpose(0, 2, 1, 3).reshape(DEPTH, 1, NW, P, P),
            r["o_hs"].transpose(0, 2, 3, 1, 4),
            r["o_sg"].transpose(0, 3, 2, 1).reshape(DEPTH, DEC, 1, W))
```
